# Optimizing a Trainium2 kernel written in Bass

```python
import math
import jax
import jax.numpy as jnp
from jax import lax
import numpy as np

D_MODEL = 1024
BATCH = 1
SEQ = 256
DEPTH = 2

GRID_W = 64
CTX_LEN = 256
N_MIXERS = 3
N_MOD = 9
FFN_DIM = 2816
EPS = 1e-6

HYENA_ORDER = 2
HYENA_SHORT_K = 3
HYENA_EMB = 33
HYENA_BANDS = (HYENA_EMB - 1) // 2
HYENA_FILTER_HIDDEN = 64
HYENA_FAST_DECAY = 0.3
HYENA_SLOW_DECAY = 1.5
HYENA_DECAY_TARGET = 1e-2

SSM_INNER = 2 * D_MODEL
SSM_HEAD_DIM = 64
SSM_HEADS = SSM_INNER // SSM_HEAD_DIM
SSM_GROUPS = 8
HEADS_PER_GROUP = SSM_HEADS // SSM_GROUPS
SSM_STATE = 128
SSM_CONV_K = 3
SSM_CHUNK = 128
SSM_BC_DIM = SSM_GROUPS * SSM_STATE
SSM_CONV_DIM = SSM_INNER + 2 * SSM_BC_DIM
SSM_IN_DIM = SSM_INNER + SSM_CONV_DIM + 2 * SSM_HEADS

MLA_HEADS = 16
MLA_NOPE = 64
MLA_ROPE = 32
MLA_V = 64
MLA_Q_RANK = 768
MLA_KV_RANK = 256
MLA_QK = MLA_NOPE + MLA_ROPE
MLA_SCALE = MLA_QK ** -0.5
MLA_DOWN = MLA_Q_RANK + MLA_KV_RANK + MLA_ROPE
ROPE_AXIS = MLA_ROPE // 2
ROPE_BASE = 10000.0
Q_BLOCK = 128

N_HYENA = (DEPTH + N_MIXERS - 1) // N_MIXERS
N_MAMBA = (DEPTH + N_MIXERS - 2) // N_MIXERS
N_MLA = DEPTH // N_MIXERS

kernel_name = 'hybrid_hyena_ssd_mla_macaron_prefix'

def rms_norm(x, eps=EPS):
    xf = x.astype(jnp.float32)
    return (xf * lax.rsqrt(jnp.mean(xf * xf, axis=-1, keepdims=True) + eps)).astype(x.dtype)

def adaln(x, mod, k):
    return rms_norm(x) * (1 + mod[:, :, k + 1]) + mod[:, :, k]

def swiglu(h, w_in, w_out):
    g, u = jnp.split(h @ w_in, 2, axis=-1)
    return (jax.nn.silu(g) * u) @ w_out

def dwconv_centered(x, w, b):
    k = w.shape[0]
    y = lax.conv_general_dilated(x, w.astype(x.dtype)[:, None, :], window_strides=(1,),
                                 padding=[(k // 2, k // 2)],
                                 dimension_numbers=('NWC', 'WIO', 'NWC'),
                                 feature_group_count=x.shape[-1])
    return y + b

def hyena_filters(L, w1, b1, freq, w2, b2, w3):
    f32 = jnp.float32
    pos = jnp.arange(L, dtype=f32)
    t = jnp.linspace(0.0, 1.0, L, dtype=f32)
    bands = jnp.linspace(1e-4, HYENA_BANDS - 1, HYENA_BANDS, dtype=f32)
    ang = (2.0 * math.pi / L) * pos[:, None] * bands[None, :]
    z = jnp.concatenate([t[:, None], jnp.cos(ang), -jnp.sin(ang)], axis=-1)
    fr = freq.astype(f32)
    hid = jnp.sin(fr * (z @ w1.astype(f32) + b1.astype(f32)))
    hid = jnp.sin(fr * (hid @ w2.astype(f32) + b2.astype(f32)))
    h = (hid @ w3.astype(f32)).reshape(L, HYENA_ORDER, 2, D_MODEL)
    max_decay = math.log(HYENA_DECAY_TARGET) / HYENA_FAST_DECAY
    min_decay = math.log(HYENA_DECAY_TARGET) / HYENA_SLOW_DECAY
    deltas = jnp.abs(jnp.linspace(min_decay, max_decay, D_MODEL, dtype=f32))
    return h * jnp.exp(-t[:, None] * deltas[None, :])[:, None, None, :]

def two_sided(h_fwd, h_bwd):
    return jnp.concatenate([h_fwd, jnp.zeros_like(h_fwd[:1]), jnp.flip(h_bwd[1:], axis=0)], axis=0)

def long_conv(u, k):
    n = 2 * u.shape[1]
    uf = jnp.fft.rfft(u.astype(jnp.float32), n=n, axis=1)
    kf = jnp.fft.rfft(k, n=n, axis=0)
    return jnp.fft.irfft(uf * kf[None], n=n, axis=1)[:, :u.shape[1]].astype(u.dtype)

def hyena_mixer(a, in_w, in_b, conv_w, conv_b, w1, b1, freq, w2, b2, w3, bias, out_w, out_b):
    L = a.shape[1]
    u = dwconv_centered(a @ in_w + in_b, conv_w, conv_b)
    x1, x2, v = jnp.split(u, 3, axis=-1)
    filt = hyena_filters(L, w1, b1, freq, w2, b2, w3)
    z = x1 * (long_conv(v, two_sided(filt[:, 0, 0], filt[:, 0, 1])) + v * bias[0])
    y = x2 * (long_conv(z, two_sided(filt[:, 1, 0], filt[:, 1, 1])) + z * bias[1])
    return y @ out_w + out_b

def segsum(a):
    T = a.shape[-1]
    cs = jnp.cumsum(a, axis=-1)
    diff = cs[..., :, None] - cs[..., None, :]
    return jnp.where(jnp.tril(jnp.ones((T, T), dtype=bool)), diff, -jnp.inf)

def ssd_chunked(xdt, da, bm, cm, init):
    b, L, G, R, P = xdt.shape
    N = bm.shape[-1]
    nc = L // SSM_CHUNK
    x = xdt.reshape(b, nc, SSM_CHUNK, G, R, P)
    bc = bm.reshape(b, nc, SSM_CHUNK, G, N)
    cc = cm.reshape(b, nc, SSM_CHUNK, G, N)
    a = da.reshape(b, nc, SSM_CHUNK, G, R).transpose(0, 3, 4, 1, 2)
    a_cs = jnp.cumsum(a, axis=-1)
    decay_in = jnp.exp(segsum(a))
    cb = jnp.einsum('bclgn,bcsgn->bgcls', cc, bc)
    y_diag = jnp.einsum('bgcls,bgrcls,bcsgrp->bclgrp', cb, decay_in, x)
    decay_to_end = jnp.exp(a_cs[..., -1:] - a_cs)
    chunk_states = jnp.einsum('bclgn,bgrcl,bclgrp->bcgrpn', bc, decay_to_end, x)
    states = jnp.concatenate([init[:, None].astype(chunk_states.dtype), chunk_states], axis=1)
    chunk_tot = jnp.pad(a_cs[..., -1], [(0, 0), (0, 0), (0, 0), (1, 0)])
    decay_chunk = jnp.exp(segsum(chunk_tot))
    states = jnp.einsum('bgrzc,bcgrpn->bzgrpn', decay_chunk, states)
    prev_states, final = states[:, :-1], states[:, -1]
    y_off = jnp.einsum('bclgn,bcgrpn,bgrcl->bclgrp', cc, prev_states, jnp.exp(a_cs))
    return (y_diag + y_off).reshape(b, L, G, R, P), final

def mamba2_mixer(a, ac, in_w, conv_w, conv_b, dt_bias, a_log, d_skip, norm_w, out_w, want_ctx):
    f32 = jnp.float32
    A = -jnp.exp(a_log.astype(f32))

    def project(h):
        b, L, _ = h.shape
        zxbcdt = h @ in_w
        z = zxbcdt[..., :SSM_INNER]
        xbc = jax.nn.silu(dwconv_centered(zxbcdt[..., SSM_INNER:SSM_INNER + SSM_CONV_DIM], conv_w, conv_b))
        xs = xbc[..., :SSM_INNER].reshape(b, L, SSM_GROUPS, HEADS_PER_GROUP, SSM_HEAD_DIM)
        bm = xbc[..., SSM_INNER:SSM_INNER + SSM_BC_DIM].reshape(b, L, SSM_GROUPS, SSM_STATE)
        cm = xbc[..., SSM_INNER + SSM_BC_DIM:].reshape(b, L, SSM_GROUPS, SSM_STATE)
        dt = zxbcdt[..., SSM_INNER + SSM_CONV_DIM:].astype(f32).reshape(b, L, 2, SSM_HEADS)
        dt = jax.nn.softplus(dt + dt_bias.astype(f32))
        return z, xs, bm, cm, dt

    def scan(xs, bm, cm, dt, d, init):
        dt_d = dt[:, :, d].reshape(dt.shape[0], dt.shape[1], SSM_GROUPS, HEADS_PER_GROUP)
        return ssd_chunked(xs * dt_d[..., None], dt_d * A[d].reshape(SSM_GROUPS, HEADS_PER_GROUP), bm, cm, init)

    def finish(y, xs, z):
        b, L = z.shape[:2]
        y = (y + d_skip.astype(f32).reshape(SSM_GROUPS, HEADS_PER_GROUP, 1) * xs).reshape(b, L, SSM_INNER)
        y = y * jax.nn.silu(z.astype(f32))
        yg = y.reshape(b, L, SSM_GROUPS, SSM_INNER // SSM_GROUPS)
        yg = yg * lax.rsqrt(jnp.mean(yg * yg, axis=-1, keepdims=True) + EPS)
        return (yg.reshape(b, L, SSM_INNER) * norm_w).astype(z.dtype) @ out_w

    flip = lambda t: jnp.flip(t, axis=1)
    zc, xc, bcx, ccx, dtc = project(ac)
    zl, xl, bl, cl, dtl = project(a)
    zero = jnp.zeros((a.shape[0], SSM_GROUPS, HEADS_PER_GROUP, SSM_HEAD_DIM, SSM_STATE), f32)
    yc_f, s_f = scan(xc, bcx, ccx, dtc, 0, zero)
    yc_b, s_b = scan(flip(xc), flip(bcx), flip(ccx), flip(dtc), 1, zero)
    yl_f, _ = scan(xl, bl, cl, dtl, 0, s_f)
    yl_b, _ = scan(flip(xl), flip(bl), flip(cl), flip(dtl), 1, s_b)
    y = finish(yl_f + flip(yl_b), xl, zl)
    yc = finish(yc_f + flip(yc_b), xc, zc) if want_ctx else None
    return y, yc

def axial_rope(row, col):
    inv = 1.0 / (ROPE_BASE ** (jnp.arange(0, ROPE_AXIS, 2, dtype=jnp.float32) / ROPE_AXIS))
    ar = row.astype(jnp.float32)[:, None] * inv[None, :]
    ac = col.astype(jnp.float32)[:, None] * inv[None, :]
    ang = jnp.concatenate([ar, ar, ac, ac], axis=-1)
    return jnp.cos(ang), jnp.sin(ang)

def rope_2d(x, cos, sin):
    def rot(v):
        v1, v2 = jnp.split(v, 2, axis=-1)
        return jnp.concatenate([-v2, v1], axis=-1)
    xr, xc = jnp.split(x, 2, axis=-1)
    return x * cos + jnp.concatenate([rot(xr), rot(xc)], axis=-1) * sin

def mla_mixer(a, ac, w_down, q_norm, w_uq, kv_norm, w_ukv, w_o, cos, sin, want_ctx):
    def down(h):
        d = h @ w_down
        cq = rms_norm(d[..., :MLA_Q_RANK]) * q_norm
        ckv = rms_norm(d[..., MLA_Q_RANK:MLA_Q_RANK + MLA_KV_RANK]) * kv_norm
        return cq, ckv, d[..., MLA_Q_RANK + MLA_KV_RANK:]

    def up_q(cq):
        q = (cq @ w_uq).reshape(cq.shape[0], cq.shape[1], MLA_HEADS, MLA_QK)
        return q[..., :MLA_NOPE], q[..., MLA_NOPE:]

    def up_kv(ckv):
        kv = (ckv @ w_ukv).reshape(ckv.shape[0], ckv.shape[1], MLA_HEADS, MLA_NOPE + MLA_V)
        return kv[..., :MLA_NOPE], kv[..., MLA_NOPE:]

    cq_c, ckv_c, kc_pe = down(ac)
    kc_nope, vc = up_kv(ckv_c)
    n_ctx = kc_nope.shape[1]
    cq_l, ckv_l, k_pe = down(a)
    k_nope, v = up_kv(ckv_l)
    k_rot = rope_2d(k_pe, cos, sin)
    q_nope, q_pe = up_q(cq_l)
    q_rot = rope_2d(q_pe, cos[:, None], sin[:, None])

    b, L = a.shape[:2]
    nb = L // Q_BLOCK
    to_blocks = lambda t: jnp.swapaxes(t.reshape(b, nb, Q_BLOCK, *t.shape[2:]), 0, 1)

    def attend(blk):
        qn, qr, qp = blk
        s_ctx = (jnp.einsum('bqhd,bkhd->bhqk', qn, kc_nope)
                 + jnp.einsum('bqhr,bkr->bhqk', qp, kc_pe))
        s_lat = (jnp.einsum('bqhd,bkhd->bhqk', qn, k_nope)
                 + jnp.einsum('bqhr,bkr->bhqk', qr, k_rot))
        p = jax.nn.softmax(jnp.concatenate([s_ctx, s_lat], axis=-1).astype(jnp.float32) * MLA_SCALE,
                           axis=-1).astype(v.dtype)
        return (jnp.einsum('bhqk,bkhd->bqhd', p[..., :n_ctx], vc)
                + jnp.einsum('bhqk,bkhd->bqhd', p[..., n_ctx:], v))

    o = lax.map(attend, (to_blocks(q_nope), to_blocks(q_rot), to_blocks(q_pe)))
    y = jnp.swapaxes(o, 0, 1).reshape(b, L, MLA_HEADS * MLA_V) @ w_o
    yc = None
    if want_ctx:
        qcn, qcp = up_q(cq_c)
        s = jnp.einsum('bqhd,bkhd->bhqk', qcn, kc_nope) + jnp.einsum('bqhr,bkr->bhqk', qcp, kc_pe)
        p = jax.nn.softmax(s.astype(jnp.float32) * MLA_SCALE, axis=-1).astype(vc.dtype)
        yc = jnp.einsum('bhqk,bkhd->bqhd', p, vc).reshape(b, n_ctx, MLA_HEADS * MLA_V) @ w_o
    return y, yc

def setup_inputs(seed: int = 0) -> dict:
    key = jax.random.key(seed)
    ks = jax.random.split(key, 40)
    f32 = jnp.float32

    def nrm(i, shape, scale):
        return jax.random.normal(ks[i], shape, f32) * scale

    def gain(i, shape):
        return 1.0 + nrm(i, shape, 0.02)

    dt0 = jnp.exp(jax.random.uniform(ks[24], (N_MAMBA, 2, SSM_HEADS), f32, math.log(1e-3), math.log(1e-1)))
    return {
        'x': nrm(0, (BATCH, SEQ, D_MODEL), 1.0),
        'c': nrm(1, (BATCH, D_MODEL), 1.0),
        'ctx': nrm(2, (BATCH, CTX_LEN, D_MODEL), 1.0),
        'c_ctx': nrm(3, (D_MODEL,), 1.0),
        'ada_w': nrm(4, (DEPTH, D_MODEL, N_MOD * D_MODEL), 0.5 * D_MODEL ** -0.5),
        'ada_b': nrm(5, (DEPTH, N_MOD * D_MODEL), 0.02),
        'ffn_in': nrm(6, (DEPTH, 2, D_MODEL, 2 * FFN_DIM), D_MODEL ** -0.5),
        'ffn_out': nrm(7, (DEPTH, 2, FFN_DIM, D_MODEL), FFN_DIM ** -0.5),
        'hy_in_w': nrm(8, (N_HYENA, D_MODEL, 3 * D_MODEL), D_MODEL ** -0.5),
        'hy_in_b': nrm(9, (N_HYENA, 3 * D_MODEL), 0.02),
        'hy_conv_w': nrm(10, (N_HYENA, HYENA_SHORT_K, 3 * D_MODEL), HYENA_SHORT_K ** -0.5),
        'hy_conv_b': nrm(11, (N_HYENA, 3 * D_MODEL), 0.02),
        'hy_pos_w1': nrm(12, (N_HYENA, HYENA_EMB, HYENA_FILTER_HIDDEN), HYENA_EMB ** -0.5),
        'hy_pos_b1': nrm(13, (N_HYENA, HYENA_FILTER_HIDDEN), 0.1),
        'hy_freq': 1.0 + nrm(14, (N_HYENA, HYENA_FILTER_HIDDEN), 0.1),
        'hy_pos_w2': nrm(15, (N_HYENA, HYENA_FILTER_HIDDEN, HYENA_FILTER_HIDDEN), HYENA_FILTER_HIDDEN ** -0.5),
        'hy_pos_b2': nrm(16, (N_HYENA, HYENA_FILTER_HIDDEN), 0.1),
        'hy_pos_w3': nrm(17, (N_HYENA, HYENA_FILTER_HIDDEN, HYENA_ORDER * 2 * D_MODEL), 0.05 * HYENA_FILTER_HIDDEN ** -0.5),
        'hy_bias': nrm(18, (N_HYENA, HYENA_ORDER, D_MODEL), 0.5),
        'hy_out_w': nrm(19, (N_HYENA, D_MODEL, D_MODEL), D_MODEL ** -0.5),
        'hy_out_b': nrm(20, (N_HYENA, D_MODEL), 0.02),
        'mb_in_w': nrm(21, (N_MAMBA, D_MODEL, SSM_IN_DIM), D_MODEL ** -0.5),
        'mb_conv_w': nrm(22, (N_MAMBA, SSM_CONV_K, SSM_CONV_DIM), SSM_CONV_K ** -0.5),
        'mb_conv_b': nrm(23, (N_MAMBA, SSM_CONV_DIM), 0.02),
        'mb_dt_bias': dt0 + jnp.log(-jnp.expm1(-dt0)),
        'mb_A_log': jnp.log(jax.random.uniform(ks[25], (N_MAMBA, 2, SSM_HEADS), f32, 1.0, 16.0)),
        'mb_D': 1.0 + nrm(26, (N_MAMBA, SSM_HEADS), 0.1),
        'mb_norm_w': gain(27, (N_MAMBA, SSM_INNER)),
        'mb_out_w': nrm(28, (N_MAMBA, SSM_INNER, D_MODEL), SSM_INNER ** -0.5),
        'mla_w_down': nrm(29, (N_MLA, D_MODEL, MLA_DOWN), D_MODEL ** -0.5),
        'mla_q_norm': gain(30, (N_MLA, MLA_Q_RANK)),
        'mla_w_uq': nrm(31, (N_MLA, MLA_Q_RANK, MLA_HEADS * MLA_QK), MLA_Q_RANK ** -0.5),
        'mla_kv_norm': gain(32, (N_MLA, MLA_KV_RANK)),
        'mla_w_ukv': nrm(33, (N_MLA, MLA_KV_RANK, MLA_HEADS * (MLA_NOPE + MLA_V)), MLA_KV_RANK ** -0.5),
        'mla_w_o': nrm(34, (N_MLA, MLA_HEADS * MLA_V, D_MODEL), (MLA_HEADS * MLA_V) ** -0.5),
        'final_norm_w': gain(35, (D_MODEL,)),
    }

def reference(x, c, ctx, c_ctx, ada_w, ada_b, ffn_in, ffn_out,
              hy_in_w, hy_in_b, hy_conv_w, hy_conv_b, hy_pos_w1, hy_pos_b1, hy_freq,
              hy_pos_w2, hy_pos_b2, hy_pos_w3, hy_bias, hy_out_w, hy_out_b,
              mb_in_w, mb_conv_w, mb_conv_b, mb_dt_bias, mb_A_log, mb_D, mb_norm_w, mb_out_w,
              mla_w_down, mla_q_norm, mla_w_uq, mla_kv_norm, mla_w_ukv, mla_w_o,
              final_norm_w):
    n_lat = x.shape[1]
    rows = n_lat // GRID_W
    row = jnp.repeat(jnp.arange(rows), GRID_W)
    col = jnp.tile(jnp.arange(GRID_W), rows)
    cos, sin = axial_rope(row, col)

    sc = jax.nn.silu(c)
    scc = jax.nn.silu(c_ctx)
    h, hc = x, ctx
    for i in range(DEPTH):
        kind, j, last = i % N_MIXERS, i // N_MIXERS, i == DEPTH - 1
        mod = (sc @ ada_w[i] + ada_b[i]).reshape(-1, 1, N_MOD, D_MODEL)
        modc = (scc @ ada_w[i] + ada_b[i]).reshape(1, 1, N_MOD, D_MODEL)
        ctx_needed = not (last and kind == 0)
        ctx_out = not last

        h = h + 0.5 * mod[:, :, 2] * swiglu(adaln(h, mod, 0), ffn_in[i, 0], ffn_out[i, 0])
        if ctx_needed:
            hc = hc + 0.5 * modc[:, :, 2] * swiglu(adaln(hc, modc, 0), ffn_in[i, 0], ffn_out[i, 0])

        a = adaln(h, mod, 3)
        ac = adaln(hc, modc, 3) if ctx_needed else None
        if kind == 0:
            hp = (hy_in_w[j], hy_in_b[j], hy_conv_w[j], hy_conv_b[j], hy_pos_w1[j], hy_pos_b1[j],
                  hy_freq[j], hy_pos_w2[j], hy_pos_b2[j], hy_pos_w3[j], hy_bias[j], hy_out_w[j], hy_out_b[j])
            y = hyena_mixer(a, *hp)
            yc = hyena_mixer(ac, *hp) if ctx_out else None
        elif kind == 1:
            y, yc = mamba2_mixer(a, ac, mb_in_w[j], mb_conv_w[j], mb_conv_b[j], mb_dt_bias[j],
                                 mb_A_log[j], mb_D[j], mb_norm_w[j], mb_out_w[j], ctx_out)
        else:
            y, yc = mla_mixer(a, ac, mla_w_down[j], mla_q_norm[j], mla_w_uq[j], mla_kv_norm[j],
                              mla_w_ukv[j], mla_w_o[j], cos, sin, ctx_out)
        h = h + mod[:, :, 5] * y.astype(h.dtype)

        h = h + 0.5 * mod[:, :, 8] * swiglu(adaln(h, mod, 6), ffn_in[i, 1], ffn_out[i, 1])
        if ctx_out:
            hc = hc + modc[:, :, 5] * yc.astype(hc.dtype)
            hc = hc + 0.5 * modc[:, :, 8] * swiglu(adaln(hc, modc, 6), ffn_in[i, 1], ffn_out[i, 1])

    return rms_norm(h) * final_norm_w


_drawn_inputs = setup_inputs


def setup_inputs(seed=0):
    import zlib

    import numpy as np

    out = dict(_drawn_inputs(seed))
    spreads = {}
    factors = {'ctx': 3.783,
     'c_ctx': 3.738,
     'hy_in_b': 8.0,
     'hy_conv_b': 8.0,
     'hy_pos_b1': 5.183,
     'hy_freq': 8.0,
     'hy_pos_b2': 3.665,
     'hy_out_b': 8.0,
     'mb_conv_b': 6.787,
     'mb_D': 4.651,
     'mb_norm_w': 8.0,
     'final_norm_w': 2.933}
    for name, (base, spread) in spreads.items():
        noise = np.random.default_rng([zlib.crc32(name.encode()), seed]).standard_normal(out[name].shape)
        drawn = base * np.exp(spread * noise) if base else spread * noise
        out[name] = jnp.asarray(drawn.astype(out[name].dtype))
    for name, factor in factors.items():
        out[name] = (out[name] * factor).astype(out[name].dtype)
    return out
```

```python
from contextlib import ExitStack, contextmanager

import concourse.bass as bass
from concourse import mybir

F32 = mybir.dt.float32
F32R = mybir.dt.float32r
ALU = mybir.AluOpType
ACT = mybir.ActivationFunctionType

P = 128
D = 1024
DT = D // P
L = 256
NT = 2 * L
FFN = 2816
FT = FFN // P
INNER = 2048
IT = INNER // P
GROUPS = 8
HPG = 4
HEADS = GROUPS * HPG
HD = 64
CONVT = 32
MB_IN = 6208
EPS = 1e-6
CW = 2048
MODT = 9 * DT
ADA_CHUNKS = 36
FIRST_ADA = 14

V_ADA = 0
V_HY_IN_B = 144
V_HY_CW = 168
V_HY_CB = 240
V_HY_BIAS = 264
V_HY_OUT_B = 280
V_MB_CW = 288
V_MB_CB = 384
V_MB_NORM = 416
V_FINAL = 432
V_C = 440
V_CCTX = 448
V_ALL = 456
VEC_ROWS = (("ada_b", 144), ("hy_in_b", 24), ("hy_conv_w", 72), ("hy_conv_b", 24), ("hy_bias", 16),
            ("hy_out_b", 8), ("mb_conv_w", 96), ("mb_conv_b", 32), ("mb_norm_w", 16), ("final_norm_w", 8),
            ("c", 8), ("c_ctx", 8))


def vec_pieces():
    base, out = 0, []
    for name, count in VEC_ROWS:
        done = 0
        while done < count:
            k = min(count - done, P - (base + done) % P)
            out.append((name, done, k, base + done))
            done += k
        base += count
    return out


VEC_DMAS = len(vec_pieces())

TWO_PI = (6.28125, 0.0019350051879882812, 3.019916050561733e-07)
ROUND = 12582912.0
PI_DOWN = 3.1415925


class Chain:

    def __init__(self, eng, sem):
        self.eng, self.sem, self.base, self.n = eng, sem, 0, 0

    def mark(self, ins):
        ins.then_inc(self.sem, 1)
        self.n += 1

    def sync(self):
        self.eng.wait_ge(self.sem, self.base + self.n)

    def __call__(self, ins):
        self.mark(ins)
        self.sync()


@contextmanager
def rolled(eng, count, chain=None, per=0):
    start = chain.base + chain.n if chain else 0
    with eng.Fori(0, count) as i:
        if chain:
            chain.base, chain.n = i * per + start, 0
        yield i
        if chain:
            assert chain.n == per, (chain.n, per)
    if chain:
        chain.base, chain.n = start + count * per, 0


def steps(eng, count, body, chain=None, per=0):
    if count > 1:
        with rolled(eng, count - 1, chain, per) as i:
            body(i, False)
    body(count - 1, True)


class Place:

    def __init__(self, plan, w=0, a=0, q=0, h=0, gate=0, conv=0, zf=0, norm=0):
        self.w, self.a, self.raw, self.q, self.h = plan["w"], plan["a"], plan["raw"], plan["q"], plan["h"]
        self.gate, self.conv, self.zf, self.norm = plan["gate"], plan["conv"], plan["zf"], plan["norm"]
        for name, add in (("w", w), ("a", a), ("raw", w + a), ("q", q), ("h", h), ("gate", gate),
                          ("conv", conv), ("zf", zf), ("norm", norm)):
            plan[name] += add


def core_groups(eng, group, tail, chain=None, per=0):
    group(0, 0, True, False)
    group(0, 1, False, True)
    with rolled(eng, GROUPS // 2 - 1, chain, per) as i:
        group(i + 1, 0, False, True)
        group(i + 1, 1, False, True)
    tail()


def build(nc, t, out, kscr, afscr):
    plan = dict(w=0, a=0, raw=0, q=0, h=0, gate=1, conv=3, zf=3, norm=0)
    P0 = Place(plan, w=2, a=FIRST_ADA, q=16, h=DT)
    ffn_in, ffn_out, norms = {}, {}, {}

    def plan_norm(key, k=DT):
        norms[key] = Place(plan, q=k, norm=1)

    def plan_ffn(key, a_in, a_out):
        plan_norm(key)
        ffn_in[key] = Place(plan, w=FT, a=a_in, q=FT, gate=FT)
        ffn_out[key] = Place(plan, w=2 * DT, a=a_out, h=DT)

    plan_ffn("00", 22, 16)
    plan_norm("hy")
    HYIN = Place(plan, w=12, zf=24)
    HYDFT = Place(plan, w=1, q=32)
    HYY = Place(plan, q=8)
    HYOUT = Place(plan, w=4, h=DT)
    plan_ffn("01", 20, 0)
    plan_ffn("10", 0, 0)
    plan_norm("mb")
    XB = Place(plan, w=12, conv=24)
    DTP = Place(plan, w=1)
    CP = Place(plan, w=4, conv=8)
    ZP = Place(plan, w=8, zf=16)
    MBN = Place(plan, q=8)
    MBOUT = Place(plan, w=8, h=DT)
    plan_ffn("11", 0, 0)
    plan_norm("fin", 0)

    with ExitStack() as ctx:
        top = [16512]

        def at(name, shape, dt, offset):
            return nc.alloc_sbuf_tensor_at(name, shape, dt, offset=offset)

        def room(nbytes):
            o = top[0]
            top[0] = o + (nbytes + 31) // 32 * 32
            assert top[0] <= 229344, top[0]
            return o

        def sb(name, cols, dt=F32):
            n = 4
            for c in cols:
                n *= c
            return at(name, [P, *cols], dt, room(n))

        def sem(name):
            return ctx.enter_context(nc.semaphore(name))

        KB = 1024
        hT = sb("hT", [DT, NT])
        o_xh = room(16 * KB)
        o_xl = room(16 * KB)
        assert o_xl == o_xh + 16 * KB
        xh = at("xh", [P, DT, NT], F32R, o_xh)
        xl = at("xl", [P, DT, NT], F32R, o_xl)
        xtok = at("xtok", [P, 2, 2, INNER], F32, o_xh)
        xstage = at("xstage", [P, 4, D], F32, o_xl)
        big = room(88 * KB)
        gh = at("gh", [P, FT, NT], F32R, big)
        gl = at("gl", [P, FT, NT], F32R, big + 44 * KB)
        ksb = at("ksb", [P, 2, 5, D], F32, big)
        hyu = at("hyu", [P, 24, NT], F32, big + 40 * KB)
        w3 = at("w3", [64, 4 * D], F32, big + 40 * KB)
        decay = at("decay", [P, 2, D], F32, big + 56 * KB)
        feh = at("feh", [P, 2, 2, 512], F32R, big + 64 * KB)
        fel = at("fel", [P, 2, 2, 512], F32R, big + 72 * KB)
        hsm = at("hsm", [64, 7, L], F32, big + 80 * KB)
        xb = at("xb", [P, 2, 24, L], F32, big)
        csb = at("csb", [P, 8, L], F32, big + 48 * KB)
        zsb = at("zsb", [P, IT, L], F32, big + 56 * KB)
        ssb = at("ssb", [P, 2, INNER], F32, big + 72 * KB)
        ynh = at("ynh", [P, IT, L], F32R, big + 24 * KB)
        ynl = at("ynl", [P, IT, L], F32R, big + 56 * KB)
        ost = at("ost", [P, 2, D], F32, big)
        raw = [sb(f"raw{i}", [CW]) for i in range(2)]
        o_w = room(32 * KB)
        wh = [at(f"wh{i}", [P, CW], F32R, o_w + i * 8 * KB) for i in range(2)]
        wl = [at(f"wl{i}", [P, CW], F32R, o_w + (2 + i) * 8 * KB) for i in range(2)]
        o = [o_w]

        def core(name, cols, parts=P):
            n = 4
            for c in cols:
                n *= c
            o[0] += n
            assert o[0] <= o_w + 32 * KB
            return at(name, [parts, *cols], F32, o[0] - n)

        ee = [core(f"ee{i}", [3 * L]) for i in range(2)]
        mm_ = [core(f"mm{i}", [3 * L]) for i in range(2)]
        afb = [core(f"afb{i}", [2, L]) for i in range(2)]
        csx = [core(f"csx{i}", [2, L]) for i in range(2)]
        dm = core("dm", [3 * L])
        cbx = core("cbx", [3 * L])
        mask = core("mask", [3 * L])
        bst = core("bst", [L])
        btok = at("btok", [P, 2, D], F32, o_w)
        dts = at("dts", [P, 8, L], F32, o_w + 12 * KB)
        tt = [sb(f"tt{i}", [NT]) for i in range(4)]
        pp = [sb(f"pp{i}", [NT]) for i in range(2)]
        acc = sb("acc", [NT])
        rs = sb("rs", [NT])
        vecs = sb("vecs", [V_ALL])
        mods = [sb(f"mods{i}", [MODT, 2]) for i in range(2)]
        sc = sb("sc", [DT, 2])
        small = sb("small", [129])
        ones = sb("ones", [P])
        eps = sb("eps", [1])
        par = sb("par", [4])
        dcol = sb("dcol", [IT])
        tk = sb("tk", [6, 64])
        ident = small[:, 0:P]
        mask0 = small[:, P:P + 1]

        bank = [ctx.enter_context(nc.psum_tensor(f"bank{i}", [P, 512], F32)) for i in range(8)]

        raw_in = [sem(f"raw_in{i}") for i in range(2)]
        w_hi = sem("w_hi")
        w_lo = sem("w_lo")
        w_used = sem("w_used")
        ada_used = sem("ada_used")
        ada_out = sem("ada_out")
        p_ready = sem("p_ready")
        p_hi = sem("p_hi")
        p_lo = sem("p_lo")
        h_done = sem("h_done")
        sq_done = sem("sq_done")
        acc_done = sem("acc_done")
        acc_zero = sem("acc_zero")
        nsum = sem("nsum")
        rms_done = sem("rms_done")
        gate_ready = sem("gate_ready")
        conv_free = sem("conv_free")
        z_free = sem("z_free")
        act_own = sem("act_own")
        dve_own = sem("dve_own")
        pool_own = sem("pool_own")
        s_vec = sem("s_vec")
        s_x = sem("s_x")
        s_cst = sem("s_cst")
        s_fil = sem("s_fil")
        s_par = sem("s_par")
        s_set = sem("s_set")
        vec_t = sem("vec_t")
        vec_out = sem("vec_out")
        sc_done = sem("sc_done")
        x_t = sem("x_t")
        hid_mm = sem("hid_mm")
        hid_arg = sem("hid_arg")
        hid_sin = sem("hid_sin")
        fil_mm = sem("fil_mm")
        fil_read = sem("fil_read")
        spec_mm = sem("spec_mm")
        spec_out = sem("spec_out")
        spec_st = sem("spec_st")
        spec_ld = sem("spec_ld")
        hy_ready = sem("hy_ready")
        vt_t = sem("vt_t")
        vt_hi = sem("vt_hi")
        vt_lo = sem("vt_lo")
        fwd_mm = sem("fwd_mm")
        fwd_read = sem("fwd_read")
        cm_mul = sem("cm_mul")
        cm_add = sem("cm_add")
        inv_mm = sem("inv_mm")
        inv_out = sem("inv_out")
        cv_in = sem("cv_in")
        cv_out = sem("cv_out")
        cv_silu = sem("cv_silu")
        dt_v = sem("dt_v")
        dt_e = sem("dt_e")
        af_st = sem("af_st")
        tk_t = sem("tk_t")
        tk_out = sem("tk_out")
        tr_mm = sem("tr_mm")
        tr_out = sem("tr_out")
        tb_mm = sem("tb_mm")
        tb_out = sem("tb_out")
        st_mm = sem("st_mm")
        st_out = sem("st_out")
        s_mask = sem("s_mask")
        afb_in = [sem(f"afb_in{i}") for i in range(2)]
        b_st = sem("b_st")
        cb_mm = sem("cb_mm")
        cb_out = sem("cb_out")
        d_done = sem("d_done")
        e_done = sem("e_done")
        ex_done = sem("ex_done")
        cs_done = sem("cs_done")
        m_done = sem("m_done")
        head_mm = sem("head_mm")
        y_out = sem("y_out")
        yt_t = sem("yt_t")
        y_done = sem("y_done")
        g_sq = sem("g_sq")
        g_sum = sem("g_sum")
        g_rms = sem("g_rms")
        g_read = sem("g_read")
        fin_p = sem("fin_p")
        fin_t = sem("fin_t")
        fin_o = sem("fin_o")
        s_out = sem("s_out")

        rows = lambda a: a.rearrange("(k p) n -> p k n", p=P)
        ada_v = [rows(t["ada_w"][i]) for i in range(2)]
        ffi_v = [[rows(t["ffn_in"][i, j]) for j in range(2)] for i in range(2)]
        ffo_v = [[rows(t["ffn_out"][i, j]) for j in range(2)] for i in range(2)]
        hyi_v = rows(t["hy_in_w"][0])
        hyo_v = rows(t["hy_out_w"][0])
        mbi_v = rows(t["mb_in_w"][0])
        mbo_v = rows(t["mb_out_w"][0])
        ds = bass.ds

        OUT_COLS = 11 * P

        block = ctx.enter_context(nc.Block())

        @block.sync
        def _(sp):
            def load(r, src, k, n):
                slot = r % 2
                dst = raw[slot][:, 0:k * n].rearrange("p (k n) -> p k n", n=n)
                sp.dma_start(dst, src).then_inc(raw_in[slot], 16)

            def begin(pl):
                if pl.w:
                    sp.wait_ge(w_lo, pl.w)
                if pl.a:
                    sp.wait_ge(ada_used, pl.a)

            def stream(pl, count, src, k, n, ada=None):
                begin(pl)

                def pair(i, last):
                    for u in range(2):
                        j = i * 2 + u
                        if ada is None:
                            sp.wait_ge(w_lo, pl.w - 1 + j)
                            load(pl.raw + u, src(i, u), k, n)
                        else:
                            sp.wait_ge(w_lo, pl.w + j)
                            load(pl.raw, src(i, u), k, n)
                            sp.wait_ge(ada_used, pl.a + j)
                            load(pl.raw + 1, ada(j), 8, 256)
                with sp.Fori(0, count // 2) as i:
                    pair(i, False)

            def wide(view, col0=0):
                return lambda i, u: view[:, :, ds(i * 512 + (col0 + u * 256), 256)]

            def ffn_in_src(view):
                return lambda i, u: view[:, :, ds(i * 256 + u * FFN, 256)]

            def ffn_out_stream(pl, view, ada):
                begin(pl)
                with sp.Fori(0, DT) as m:
                    for half in range(2):
                        j = m * 2 + half
                        if ada is None:
                            sp.wait_ge(w_lo, pl.w - 1 + j)
                            load(pl.raw + half, view[:, half * 11:half * 11 + 11, ds(m * P, P)], 11, P)
                        else:
                            sp.wait_ge(w_lo, pl.w + j)
                            load(pl.raw, view[:, half * 11:half * 11 + 11, ds(m * P, P)], 11, P)
                            sp.wait_ge(ada_used, pl.a + j)
                            load(pl.raw + 1, ada(j), 8, 256)

            def ada_src(layer, first):
                return lambda j: ada_v[layer][:, :, ds(j * 256 + first * 256, 256)]

            sp.dma_start(small[:], t["c_small"]).then_inc(s_cst, 16)
            load(0, t["c_dft1"].rearrange("p (k n) -> p k n", n=256), 8, 256)
            load(1, t["c_dft2"].rearrange("p (k n) -> p k n", n=256), 1, 256)
            sp.dma_start(xstage[:, 0:2, :], t["x"][0].rearrange("(a p) d -> p a d", p=P)).then_inc(s_x, 16)
            sp.dma_start(xstage[:, 2:4, :], t["ctx"][0].rearrange("(a p) d -> p a d", p=P)).then_inc(s_x, 16)
            for i in range(FIRST_ADA):
                if i < 2:
                    sp.wait_ge(w_lo, i + 1)
                else:
                    sp.wait_ge(ada_used, i - 1)
                c = i if i < 12 else 22 + i
                load(2 + i, ada_v[0][:, :, c * 256:c * 256 + 256], 8, 256)

            stream(ffn_in["00"], FT, ffn_in_src(ffi_v[0][0]), 8, 256, ada_src(0, 12))
            ffn_out_stream(ffn_out["00"], ffo_v[0][0], ada_src(1, 0))

            stream(HYIN, 12, wide(hyi_v), 8, 256)
            begin(HYDFT)
            load(HYDFT.raw, t["c_dft1"].rearrange("p (k n) -> p k n", n=256), 8, 256)
            begin(HYOUT)
            for j in range(4):
                if j >= 2:
                    sp.wait_ge(w_lo, HYOUT.w - 1 + j)
                load(HYOUT.raw + j, hyo_v[:, :, j * 256:j * 256 + 256], 8, 256)

            pl = ffn_in["01"]
            stream(pl, 20, ffn_in_src(ffi_v[0][1]), 8, 256, ada_src(1, 16))
            sp.wait_ge(w_lo, pl.w + 20)
            load(pl.raw + 40, ffi_v[0][1][:, :, 10 * 256:11 * 256], 8, 256)
            sp.wait_ge(ada_used, pl.a + 20)
            load(pl.raw + 41, ffi_v[0][1][:, :, FFN + 10 * 256:FFN + 11 * 256], 8, 256)
            ffn_out_stream(ffn_out["01"], ffo_v[0][1], None)

            stream(ffn_in["10"], FT, ffn_in_src(ffi_v[1][0]), 8, 256)
            ffn_out_stream(ffn_out["10"], ffo_v[1][0], None)

            stream(XB, 12, wide(mbi_v, INNER), 8, 256)
            begin(DTP)
            load(DTP.raw, mbi_v[:, :, MB_IN - P:MB_IN], 8, P)
            stream(CP, 4, wide(mbi_v, INNER + 3072), 8, 256)
            stream(ZP, 8, wide(mbi_v, 0), 8, 256)

            sp.wait_ge(af_st, 32)
            sp.wait_ge(st_out, GROUPS)
            for hh in range(2):
                sp.dma_start(afb[hh][:], afscr[hh].partition_broadcast(P)).then_inc(afb_in[hh], 16)
            with sp.Fori(0, HEADS // 2 - 1) as i:
                for u in range(2):
                    sp.wait_ge(d_done, i * 2 + u + 1)
                    sp.wait_ge(ex_done, i * 2 + u + 1)
                    sp.dma_start(afb[u][:], afscr[i * 2 + u + 2].partition_broadcast(P)).then_inc(afb_in[u], 16)

            begin(MBOUT)
            with sp.Fori(0, DT // 2) as i:
                for u in range(2):
                    sp.wait_ge(w_lo, MBOUT.w - 1 + i * 2 + u)
                    load(MBOUT.raw + u, mbo_v[:, :, ds(i * 256 + u * P, P)], 16, P)

            stream(ffn_in["11"], FT, ffn_in_src(ffi_v[1][1]), 8, 256)
            ffn_out_stream(ffn_out["11"], ffo_v[1][1], None)

            sp.wait_ge(fin_o, DT)
            sp.dma_start(out[0].rearrange("(a p) d -> p a d", p=P), ost[:]).then_inc(s_out, 16)
            sp.wait_ge(s_out, 16)
            sp.wait_ge(spec_st, 16)
            sp.wait_ge(af_st, 32)

        @block.scalar
        def _(act):
            own = Chain(act, act_own)

            def split_hi(n, cols, r_slot, r_uses, w_free):
                act.wait_ge(raw_in[r_slot], r_uses * 16)
                if w_free is not None:
                    act.wait_ge(w_used, w_free)
                return act.activation(wh[n % 2][:, 0:cols], raw[r_slot][:, 0:cols], ACT.Copy).then_inc(w_hi, 1)

            def next_hi(pl, ada, i, u, per, cols=CW, ahead=1):
                j = i * per + (u + ahead)
                r = pl.raw + (2 * (u + ahead) if ada else u + ahead)
                rr = per * (2 if ada else 1) // 2
                split_hi(pl.w + u + ahead, cols, r % 2, i * rr + (r // 2 + 1), pl.w - 1 + j)

            def hi_tile(q, uses, dst, src=None):
                act.wait_ge(p_ready, uses)
                act.activation(dst, src if src is not None else pp[q % 2][:, :], ACT.Copy).then_inc(p_hi, 1)

            def norm(key, n=NT):
                pl = norms[key]
                act.wait_ge(nsum, pl.norm + 1)
                act.activation(rs[:, 0:n], bank[0][:, 0:n], ACT.Sqrt, bias=eps[:, 0:1],
                               scale=1.0 / D).then_inc(rms_done, 1)

            def norm_hi(key, n=NT):
                pl = norms[key]
                for k in range(DT):
                    hi_tile(pl.q + k, pl.q + k + 1, xh[:, k, 0:n], pp[(pl.q + k) % 2][:, 0:n])

            def ffn(key, ada_pairs, ada_out_on, after, n=NT):
                norm(key, n)
                norm_hi(key, n)
                pi, po = ffn_in[key], ffn_out[key]

                def pair(i, last):
                    if ada_pairs and last and ada_pairs < FT // 2:
                        r = pi.raw + 4 * ada_pairs
                        split_hi(pi.w + FT - 1, CW, (r + 1) % 2, (r + 1) // 2 + 1, pi.w - 1 + FT - 1)
                    else:
                        next_hi(pi, ada_pairs, i, 0, 2)
                    act.wait_ge(w_used, i * 2 + (pi.w + 1))
                    act.wait_ge(p_ready, i * 2 + pi.q)
                    for u in range(2):
                        act.activation(tt[u][:, 0:n], bank[u][:, 0:n], ACT.Silu).then_inc(gate_ready, 1)
                    if last:
                        split_hi(po.w, OUT_COLS, po.raw % 2, po.raw // 2 + 1, po.w - 1)
                    else:
                        next_hi(pi, ada_pairs, i, 1, 2)
                    for u in range(2):
                        hi_tile(pi.q + u, i * 2 + (pi.q + u + 1), gh[:, i * 2 + u, 0:n], pp[(pi.q + u) % 2][:, 0:n])

                steps(act, FT // 2, pair)
                act.wait_ge(p_ready, pi.q + FT)

                def mpair(i, last):
                    for um in range(2):
                        for half in range(2):
                            u = um * 2 + half
                            if last and u == 3:
                                if after is not None:
                                    split_hi(after.w, CW, after.raw % 2, after.raw // 2 + 1, after.w - 1)
                            else:
                                next_hi(po, ada_out_on, i, u, 4, OUT_COLS)
                        square(po, i, um, n)

                steps(act, DT // 2, mpair)

            def square(pl, i, um, n):
                act.wait_ge(h_done, i * 2 + (pl.h + um + 1))
                act.wait_ge(acc_done, i * 2 + (pl.h + um - 1))
                act.activation(tt[um][:, 0:n], hT[:, i * 2 + um, 0:n], ACT.Square).then_inc(sq_done, 1)

            stage = tt[0][:, :].rearrange("p (a c) -> p a c", c=P)
            for name, row, k, r in vec_pieces():
                v = t[name]
                if len(v.shape) > 1:
                    v = v.rearrange({2: "a b -> (a b)", 3: "a b c -> (a b c)"}[len(v.shape)])
                v = v.rearrange("(r c) -> r c", c=P)
                act.dma_start(stage[r % P:r % P + k, r // P, :], v[row:row + k, :]).then_inc(s_vec, 16)
            act.dma_start(hsm[0:33, 0, :], t["c_z"]).then_inc(s_fil, 16)
            act.dma_start(hsm[0:33, 1, 0:64], t["hy_pos_w1"][0]).then_inc(s_fil, 16)
            act.dma_start(hsm[:, 1, 64:128], t["hy_pos_w2"][0]).then_inc(s_fil, 16)
            for n, name in enumerate(("hy_pos_b1", "hy_freq", "hy_pos_b2")):
                act.dma_start(hsm[:, 1, 128 + n:129 + n], t[name][0].rearrange("(p o) -> p o", o=1)).then_inc(s_fil, 16)
            act.dma_start(w3[:], t["hy_pos_w3"][0]).then_inc(s_fil, 16)
            act.dma_start(decay[:], t["c_decay"].rearrange("p (a n) -> p a n", a=2)).then_inc(s_fil, 16)
            act.dma_start(par[64:128, 0:1], t["mb_dt_bias"][0].rearrange("d (h o) -> (d h) o", o=1)).then_inc(s_par, 16)
            act.dma_start(par[64:128, 1:2], t["mb_A_log"][0].rearrange("d (h o) -> (d h) o", o=1)).then_inc(s_par, 16)
            dv = t["mb_D"][0].rearrange("(m a) -> a m", a=2)
            with nc.allow_non_contiguous_dma(reason="32 scalars spread over partitions"):
                for a in range(2):
                    act.dma_start(dcol[64 * a:64 * a + 64, :], dv[a].partition_broadcast(64)).then_inc(s_par, 16)

            split_hi(0, CW, 0, 1, None)
            split_hi(1, 256, 1, 1, None)
            act.wait_ge(vec_out, 1)
            own.mark(act.activation(sc[:, :, 0], vecs[:, V_C:V_C + DT], ACT.Silu))
            act.activation(sc[:, :, 1], vecs[:, V_CCTX:V_CCTX + DT], ACT.Silu).then_inc(sc_done, 1)
            own.sync()
            act.activation(tt[3][:, 0:1], small[:, 0:1], ACT.Silu).then_inc(gate_ready, 1)
            act.activation(tt[3][:, 1:2], small[:, 0:1], ACT.Copy).then_inc(z_free, 3)
            act.activation(tt[3][:, 10:11], small[:, 0:1], ACT.Copy).then_inc(cv_silu, 2)
            for layer in range(2):
                act.wait_ge(hid_arg, layer + 1)
                act.activation(hsm[:, 3 + layer, :], hsm[:, 2, :], ACT.Sin).then_inc(hid_sin, 1)
            for m in range(DT):
                act.wait_ge(h_done, m + 1)
                if m >= 2:
                    act.wait_ge(acc_done, m - 1)
                act.activation(tt[m % 2][:], hT[:, m, :], ACT.Square).then_inc(sq_done, 1)
            for unit in range(4):
                o_, hh = unit // 2, unit % 2
                if unit:
                    act.wait_ge(spec_mm, 5 * unit)
                for n in range(4):
                    q = unit * 4 + n
                    hi_tile(q, q + 1, feh[:, n % 2, n // 2, :])
                for kt in range(5):
                    x = unit * 5 + kt
                    act.wait_ge(spec_mm, x + 1)
                    act.activation(ksb[:, o_, kt, hh * 512:hh * 512 + 512], bank[4 + x % 2][:], ACT.Identity,
                                   scale=mask0 if kt == 2 else 1.0).then_inc(spec_out, 1)
            act.wait_ge(spec_out, 20)
            act.dma_start(kscr, ksb[:].rearrange("p a b c -> p (a b c)")).then_inc(spec_st, 16)
            act.wait_ge(spec_st, 16)
            pl = ffn_in["00"]
            split_hi(pl.w, CW, pl.raw % 2, pl.raw // 2 + 1, pl.w - 1)

            ffn("00", 11, True, HYIN)
            norm("hy")
            norm_hi("hy")
            act.dma_start(ksb[:].rearrange("p a b c -> p (a b c)"), kscr).then_inc(spec_ld, 16)

            def hy_in_pair(i, last):
                for u in range(2):
                    if last and u == 1:
                        split_hi(HYDFT.w, CW, HYDFT.raw % 2, HYDFT.raw // 2 + 1, HYDFT.w - 1)
                    else:
                        next_hi(HYIN, False, i, u, 2)
                    act.wait_ge(w_used, i * 2 + (HYIN.w + u + 1))
                    for s in range(2):
                        m = i * 4 + (u * 2 + s)
                        act.wait_ge(hy_ready, m + 1)
                        act.activation(tt[s][:], bank[2 * u + s][:], ACT.Identity,
                                       bias=vecs[:, ds(m + V_HY_IN_B, 1)]).then_inc(z_free, 1)
            steps(act, 6, hy_in_pair)

            for conv in range(2):
                for b in range(8):
                    act.wait_ge(vt_t, conv * 8 + b + 1)
                    act.activation(xh[:, b, :], bank[4 + b % 2][:], ACT.Copy).then_inc(vt_hi, 1)
                for unit in range(4):
                    x = conv * 4 + unit
                    if x:
                        act.wait_ge(inv_mm, 2 * x)
                    for n in range(4):
                        q = HYDFT.q + x * 4 + n
                        hi_tile(q, q + 1, wh[1][:, n * 512:n * 512 + 512])
            for k in range(DT):
                hi_tile(HYY.q + k, HYY.q + k + 1, xh[:, k, :])
            for j in range(4):
                r = HYOUT.raw + j
                split_hi(HYOUT.w + j, CW, r % 2, r // 2 + 1, HYOUT.w if j == 0 else HYOUT.w + j - 1)
                if j:
                    for um in range(2):
                        square(HYOUT, j - 1, um, NT)
            for um in range(2):
                square(HYOUT, 3, um, NT)
            pl = ffn_in["01"]
            split_hi(pl.w, CW, pl.raw % 2, pl.raw // 2 + 1, pl.w - 1)
            ffn("01", 10, False, ffn_in["10"])

            ffn("10", 0, False, XB)
            norm("mb")
            norm_hi("mb")

            def conv_chunk(pl, i, u, count, split, dst, n):
                split()
                act.wait_ge(w_used, i * 2 + (pl.w + u + 1))
                first = pl.conv - 3
                for s in range(2):
                    m = i * 4 + (u * 2 + s)
                    act.wait_ge(cv_silu, m + (first + 1))
                    act.activation(tt[2 + s][:, 0:n], bank[2 * u + s][:, 0:n], ACT.Identity,
                                   bias=vecs[:, ds(m + (V_MB_CB + first), 1)],
                                   scale=vecs[:, ds(m + (V_MB_CW + CONVT + first), 1)]).then_inc(cv_in, 1)
                for s in range(2):
                    m = i * 4 + (u * 2 + s)
                    act.wait_ge(conv_free, m + (pl.conv + 1))
                    act.activation(dst(m), tt[2 + s][:, 0:n] if n == L else
                                   tt[2 + s][:].rearrange("p (a n) -> p a n", a=2), ACT.Silu).then_inc(cv_silu, 1)

            def xb_pair(i, last):
                for u in range(2):
                    split = lambda: (split_hi(DTP.w, 8 * P, DTP.raw % 2, DTP.raw // 2 + 1, DTP.w - 1)
                                     if last and u == 1 else next_hi(XB, False, i, u, 2))
                    conv_chunk(XB, i, u, 12, split, lambda m: xb[:, :, m, :], NT)
            steps(act, 6, xb_pair)

            split_hi(CP.w, CW, CP.raw % 2, CP.raw // 2 + 1, CP.w - 1)
            act.wait_ge(s_par, 64)
            act.wait_ge(dt_v, 1)
            act.activation(tt[1][64:128, :], tt[0][64:128, :], ACT.Exp, scale=-1.0).then_inc(dt_e, 1)
            act.activation(par[64:128, 2:3], par[64:128, 1:2], ACT.Exp).then_inc(dt_e, 1)

            def c_pair(i, last):
                for u in range(2):
                    split = lambda: (split_hi(ZP.w, CW, ZP.raw % 2, ZP.raw // 2 + 1, ZP.w - 1)
                                     if last and u == 1 else next_hi(CP, False, i, u, 2))
                    conv_chunk(CP, i, u, 4, split, lambda m: csb[:, m, :], L)
            steps(act, 2, c_pair)

            def z_pair(i, last):
                for u in range(2):
                    if not (last and u == 1):
                        next_hi(ZP, False, i, u, 2)
                    act.wait_ge(w_used, i * 2 + (ZP.w + u + 1))
                    for s in range(2):
                        act.activation(zsb[:, i * 4 + (u * 2 + s), :], bank[2 * u + s][:, 0:L],
                                       ACT.Silu).then_inc(z_free, 1)
            steps(act, 4, z_pair)

            act.wait_ge(dt_v, 2)
            act.activation(dts[64:128, 4, :], dts[64:128, 3, :], ACT.Exp).then_inc(dt_e, 1)
            act.wait_ge(dt_v, 3)
            for d in range(2):
                act.dma_start(afscr[:, d, :], dts[64 + 32 * d:96 + 32 * d, 5, :]).then_inc(af_st, 16)
            for b in range(4):
                act.wait_ge(tb_mm, b + 1)
                act.activation(btok[:, b // 2, (b % 2) * 512:(b % 2) * 512 + 512], bank[6 + b % 2][:],
                               ACT.Copy).then_inc(tb_out, 1)
            for g in range(GROUPS):
                act.wait_ge(st_mm, g + 1)
                act.activation(ssb[:, :, g * 256:g * 256 + 256], bank[4 + g % 2][:].rearrange("p (a n) -> p a n", a=2),
                               ACT.Copy).then_inc(st_out, 1)
            act.wait_ge(st_mm, GROUPS)
            act.dma_start(mask[:], t["c_mask"]).then_inc(s_mask, 16)

            def group(i, u, first, finish):
                g = i * 2 + u
                if not first:
                    act.wait_ge(cb_mm, g)
                act.activation(bst[:], xb[:, 0, g + IT, :], ACT.Copy).then_inc(b_st, 1)
                act.wait_ge(cb_mm, g + 1)
                if not first:
                    act.wait_ge(m_done, g * HPG)
                for a, lo, hi in ((0, 0, 256), (256, 384, 512), (384, 0, 128), (512, 256, 512)):
                    ins = act.activation(cbx[:, a:a + hi - lo], bank[6][:, lo:hi], ACT.Copy)
                ins.then_inc(cb_out, 1)
                for r in range(HPG):
                    if finish and r == 1:
                        copy_y(g, 1 - u)
                    b = r % 2
                    h1 = i * 8 + (u * HPG + r + 1)
                    use = i * 4 + (u * 2 + r // 2 + 1)
                    act.wait_ge(afb_in[b], use * 16)
                    if not (first and r < 2):
                        act.wait_ge(head_mm, h1 - 2)
                    act.activation(csx[b][:], afb[b][:], ACT.Exp).then_inc(ex_done, 1)
                    if not (first and r < 2):
                        act.wait_ge(m_done, h1 - 2)
                    act.wait_ge(d_done, h1)
                    act.activation(ee[b][:], dm[:], ACT.Exp).then_inc(e_done, 1)

            def copy_y(g, odd):
                act.wait_ge(head_mm, g * HPG)
                if not isinstance(g, int) or g > 1:
                    act.wait_ge(yt_t, g - 1)
                act.activation(tt[2][:], bank[4 + odd][:], ACT.Copy).then_inc(y_out, 1)

            core_groups(act, group, lambda: copy_y(GROUPS, 1))

            for g in range(GROUPS + 1):
                if g < GROUPS:
                    act.wait_ge(y_done, GROUPS)
                    if g >= 2:
                        act.wait_ge(g_sum, g - 1)
                    act.activation(tt[g % 2][:], zsb[:, 2 * g:2 * g + 2, :].rearrange("p a n -> p (a n)"),
                                   ACT.Square).then_inc(g_sq, 1)
                if g:
                    act.wait_ge(g_sum, g)
                    if g >= 2:
                        act.wait_ge(g_read, g - 1)
                    act.activation(rs[:, 0:L], bank[6 + (g - 1) % 2][:, 0:L], ACT.Sqrt, bias=eps[:, 0:1],
                                   scale=1.0 / 256).then_inc(g_rms, 1)
                    hi_tile(MBN.q + g - 1, MBN.q + g, ynh[:, 2 * g - 2:2 * g, :].rearrange("p a n -> p (a n)"))

            split_hi(MBOUT.w, CW, MBOUT.raw % 2, MBOUT.raw // 2 + 1, MBOUT.w)

            def mb_pair(i, last):
                for um in range(2):
                    if last and um == 1:
                        pl = ffn_in["11"]
                        split_hi(pl.w, CW, pl.raw % 2, pl.raw // 2 + 1, pl.w - 1)
                    else:
                        next_hi(MBOUT, False, i, um, 2)
                    square(MBOUT, i, um, L)
            steps(act, DT // 2, mb_pair)
            ffn("11", 0, False, None, L)
            norm("fin", L)
            for k in range(DT):
                act.wait_ge(fin_t, k + 1)
                act.activation(ost[:, :, k * P:k * P + P], bank[k % 4][:, 0:L].rearrange("p (a n) -> p a n", a=2),
                               ACT.Copy).then_inc(fin_o, 1)

        @block.vector
        def _(dve):
            own = Chain(dve, dve_own)

            def split_lo(n_slot, count, cols, r_slot):
                dve.wait_ge(w_hi, count)
                dve.tensor_tensor(wl[n_slot][:, 0:cols], raw[r_slot][:, 0:cols],
                                  wh[n_slot][:, 0:cols].bitcast(F32), ALU.subtract).then_inc(w_lo, 1)

            def next_lo(pl, ada, i, u, per, cols=CW):
                r = pl.raw + (2 * (u + 1) if ada else u + 1)
                split_lo((pl.w + u + 1) % 2, i * per + (pl.w + u + 2), cols, r % 2)

            def open_lo(pl, cols=CW):
                split_lo(pl.w % 2, pl.w + 1, cols, pl.raw % 2)

            def pp_free(q):
                if not isinstance(q, int) or q >= 2:
                    dve.wait_ge(p_lo, q - 1)

            def norm(key, layer, k0, n=NT):
                pl = norms[key]
                m = mods[layer]
                dve.wait_ge(rms_done, pl.norm + 1)
                own(dve.reciprocal(rs[:, 0:n], rs[:, 0:n]))
                for k in range(DT):
                    q = pl.q + k
                    p = pp[q % 2]
                    pp_free(q)
                    own(dve.tensor_tensor(p[:, 0:n], hT[:, k, 0:n], rs[:, 0:n], ALU.mult))
                    sh, s1 = DT * k0 + k, DT * (k0 + 1) + k
                    for w in range(n // L):
                        ins = dve.tensor_scalar(p[:, w * L:w * L + L], p[:, w * L:w * L + L], m[:, s1, w:w + 1],
                                                m[:, sh, w:w + 1], ALU.mult, ALU.add)
                    ins.then_inc(p_ready, 1)

            def residual(pl, layer, k5, i, um, n, chunk_done):
                dve.wait_ge(w_used, chunk_done)
                for w in range(n // L):
                    x = hT[:, i * 2 + um, w * L:w * L + L]
                    ins = dve.scalar_tensor_tensor(x, bank[4 + um][:, w * L:w * L + L],
                                                   mods[layer][:, i * 2 + (DT * k5 + um), w:w + 1], x,
                                                   ALU.mult, ALU.add)
                ins.then_inc(h_done, 1)

            def ffn(key, layer, k0, ada_pairs, ada_out_on, after, n=NT):
                norm(key, layer, k0, n)
                pi, po = ffn_in[key], ffn_out[key]

                def pair(i, last):
                    if ada_pairs and last and ada_pairs < FT // 2:
                        split_lo((pi.w + 1) % 2, pi.w + FT, CW, (pi.raw + 4 * ada_pairs + 1) % 2)
                    else:
                        next_lo(pi, ada_pairs, i, 0, 2)
                    if last:
                        open_lo(po, OUT_COLS)
                    else:
                        next_lo(pi, ada_pairs, i, 1, 2)
                    dve.wait_ge(w_used, i * 2 + (pi.w + 2))
                    for u in range(2):
                        dve.wait_ge(gate_ready, i * 2 + (pi.gate + u + 1))
                        pp_free(i * 2 + (pi.q + u))
                        dve.tensor_tensor(pp[(pi.q + u) % 2][:, 0:n], tt[u][:, 0:n], bank[2 + u][:, 0:n],
                                          ALU.mult).then_inc(p_ready, 1)
                steps(dve, FT // 2, pair)

                def mpair(i, last):
                    for um in range(2):
                        for half in range(2):
                            u = um * 2 + half
                            if last and u == 3:
                                if after is not None:
                                    open_lo(after)
                            else:
                                next_lo(po, ada_out_on, i, u, 4, OUT_COLS)
                        residual(po, layer, k0 + 2, i, um, n, i * 4 + (po.w + 2 * um + 2))
                steps(dve, DT // 2, mpair)

            def take_mods(layer, used, spans, plus, halve):
                dve.wait_ge(ada_used, used)
                m = mods[layer]
                for a, b in spans:
                    n = b - a
                    own.mark(dve.tensor_tensor(
                        m[:, a:b, :], bank[6 + layer][:, 2 * a:2 * b].rearrange("p (m c) -> p m c", c=2),
                        vecs[:, V_ADA + MODT * layer + a:V_ADA + MODT * layer + b].unsqueeze(2).to_broadcast([P, n, 2]),
                        ALU.add))
                own.sync()
                for idx in plus:
                    x = m[:, DT * idx:DT * idx + DT, :]
                    own.mark(dve.tensor_scalar(x, x, 1.0, None, ALU.add))
                for idx in halve:
                    x = m[:, DT * idx:DT * idx + DT, :]
                    own.mark(dve.tensor_scalar(x, x, 0.5, None, ALU.mult))
                dve.tensor_copy(tt[3][:, 4:5], tt[3][:, 3:4]).then_inc(ada_out, 1)
                own.sync()

            own.mark(dve.memset(tt[3][:, 2:8], 0.0))
            dve.memset(ones[:], 1.0).then_inc(s_set, 1)
            dve.memset(eps[:], EPS).then_inc(s_set, 1)
            dve.memset(tt[3][:, 8:9], 0.0).then_inc(conv_free, 3)
            dve.memset(tt[3][:, 9:10], 0.0).then_inc(hy_ready, 2)
            own.sync()
            split_lo(0, 1, CW, 0)
            split_lo(1, 2, 256, 1)
            dve.wait_ge(vec_t, 1)
            dve.tensor_copy(vecs[:], bank[7][:, 0:V_ALL]).then_inc(vec_out, 1)
            for m in range(DT):
                dve.wait_ge(x_t, m + 1)
                dve.tensor_copy(hT[:, m, :], bank[m % 4][:]).then_inc(h_done, 1)
            dve.wait_ge(s_fil, 16 * 8)
            for layer in range(2):
                arg, cyc, red = hsm[:, 5, :], hsm[:, 6, :], hsm[:, 2, :]
                dve.wait_ge(hid_mm, layer + 1)
                b = hsm[:, 1, 128 + 2 * layer:129 + 2 * layer]
                if layer:
                    dve.wait_ge(hid_sin, 1)
                own(dve.tensor_scalar(arg, bank[7][0:64, 0:L], b, hsm[:, 1, 129:130], ALU.add, ALU.mult))
                own(dve.tensor_scalar(cyc, arg, 0.15915494309189535, ROUND, ALU.mult, ALU.add))
                own(dve.tensor_scalar(cyc, cyc, ROUND, None, ALU.subtract))
                for part in TWO_PI:
                    own(dve.scalar_tensor_tensor(arg, cyc, -part, arg, ALU.mult, ALU.add))
                dve.tensor_scalar(red, arg, PI_DOWN, -PI_DOWN, ALU.min, ALU.max).then_inc(hid_arg, 1)
            for unit in range(4):
                o_, hh = unit // 2, unit % 2
                cols = slice(hh * 512, hh * 512 + 512)
                for n in range(2):
                    dve.wait_ge(fil_mm, unit * 2 + n + 1)
                    if unit or n:
                        dve.wait_ge(p_ready, unit * 4 + n * 2)
                    own.mark(dve.tensor_tensor(tt[2][:], bank[n][:], decay[:, n, cols], ALU.mult))
                    own.mark(dve.scalar_tensor_tensor(tt[3][:], bank[2 + n][:], mask0 if n == 0 else 1.0,
                                                      decay[:, n, cols], ALU.mult, ALU.mult))
                    own.sync()
                    for w in range(2):
                        q = unit * 4 + n * 2 + w
                        pp_free(q)
                        ins = dve.tensor_tensor(pp[q % 2][:], tt[2][:], tt[3][:], ALU.subtract if w else ALU.add)
                        ins.then_inc(p_ready, 1)
            take_mods(0, FIRST_ADA, [(0, 24), (68, 72)], (1,), (2,))
            open_lo(ffn_in["00"])

            ffn("00", 0, 0, 11, True, HYIN)
            take_mods(0, FIRST_ADA + 22, [(24, 68)], (4, 7), (8,))
            norm("hy", 0, 3)

            def hy_in_pair(i, last):
                for u in range(2):
                    if last and u == 1:
                        open_lo(HYDFT)
                    else:
                        next_lo(HYIN, False, i, u, 2)
                    for s in range(2):
                        m = i * 4 + (u * 2 + s)
                        src = tt[s][:].rearrange("p (a n) -> p a n", a=2)
                        dst = hyu[:, m, :].rearrange("p (a n) -> p a n", a=2)
                        tap = lambda w: vecs[:, ds(m + (V_HY_CW + 24 * w), 1)]
                        dve.wait_ge(z_free, m + (HYIN.zf + 1))
                        own(dve.tensor_scalar(hyu[:, m, :], tt[s][:], tap(1), vecs[:, ds(m + V_HY_CB, 1)],
                                              ALU.mult, ALU.add))
                        own(dve.scalar_tensor_tensor(dst[:, :, 1:L], src[:, :, 0:L - 1], tap(0), dst[:, :, 1:L],
                                                     ALU.mult, ALU.add))
                        dve.scalar_tensor_tensor(dst[:, :, 0:L - 1], src[:, :, 1:L], tap(2), dst[:, :, 0:L - 1],
                                                 ALU.mult, ALU.add).then_inc(hy_ready, 1)
            dve.wait_ge(w_used, HYIN.w)
            steps(dve, 6, hy_in_pair, own, 8)

            dve.wait_ge(spec_ld, 16)
            for conv in range(2):
                for b in range(8):
                    dve.wait_ge(vt_hi, conv * 8 + b + 1)
                    dve.tensor_tensor(xl[:, b, :], bank[4 + b % 2][:], xh[:, b, :].bitcast(F32),
                                      ALU.subtract).then_inc(vt_lo, 1)
                for unit in range(5):
                    x = conv * 4 + unit
                    if unit < 4:
                        cols = slice((unit % 2) * 512, (unit % 2) * 512 + 512)
                        for n in range(4):
                            ft = n % 2
                            a, b_ = (ft, 2 + ft) if n < 2 else (2 + ft, 4 if ft == 0 else ft)
                            dve.wait_ge(fwd_mm, x + 1)
                            c0 = x * 4 + n
                            if c0 >= 2:
                                dve.wait_ge(p_ready, HYDFT.q + c0 - 1)
                            w0, w1 = tt[2 * (n % 2)], tt[2 * (n % 2) + 1]
                            own.mark(dve.tensor_tensor(w0[:], bank[ft][:], ksb[:, conv, a, cols], ALU.mult))
                            dve.tensor_tensor(w1[:], bank[2 + ft][:], ksb[:, conv, b_, cols],
                                              ALU.mult).then_inc(cm_mul, 1)
                    if unit:
                        u = unit - 1
                        y = conv * 4 + u
                        seg, half = u // 2, u % 2
                        for c in range(4):
                            ch = half * 4 + c
                            tok = slice(seg * L, seg * L + L)
                            src = hyu[:, (16 if conv == 0 else 0) + ch, tok]
                            if c % 2 == 0:
                                dve.wait_ge(inv_mm, 2 * y + c // 2 + 1)
                            own(dve.scalar_tensor_tensor(src, src, vecs[:, V_HY_BIAS + 8 * conv + ch:V_HY_BIAS + 8 * conv + ch + 1],
                                                         bank[4 + c // 2][:, (c % 2) * L:(c % 2) * L + L], ALU.mult, ALU.add))
                            dst = hyu[:, (0 if conv == 0 else 8) + ch, tok]
                            dve.tensor_tensor(dst, dst, src, ALU.mult).then_inc(inv_out, 1)
                dve.wait_ge(inv_out, 16 * (conv + 1))
            for k in range(DT):
                pp_free(HYY.q + k)
                dve.tensor_copy(pp[(HYY.q + k) % 2][:], hyu[:, 8 + k, :]).then_inc(p_ready, 1)
            for j in range(5):
                if j < 4:
                    split_lo((HYOUT.w + j) % 2, HYOUT.w + j + 1, CW, (HYOUT.raw + j) % 2)
                if j:
                    for um in range(2):
                        m = (j - 1) * 2 + um
                        dve.wait_ge(w_used, HYOUT.w + j)
                        for w in range(2):
                            own.mark(dve.tensor_scalar(
                                tt[2 + um][:, w * L:w * L + L], bank[4 + um][:, w * L:w * L + L],
                                vecs[:, V_HY_OUT_B + m:V_HY_OUT_B + m + 1], mods[0][:, 5 * DT + m, w:w + 1],
                                ALU.add, ALU.mult))
                        own.sync()
                        dve.tensor_tensor(hT[:, m, :], hT[:, m, :], tt[2 + um][:], ALU.add).then_inc(h_done, 1)
            open_lo(ffn_in["01"])
            ffn("01", 0, 6, 10, False, ffn_in["10"])

            take_mods(1, 72, [(0, 72)], (1, 4, 7), (2, 8))
            ffn("10", 1, 0, 0, False, XB)
            norm("mb", 1, 3)

            def taps(pl, i, u, s, n):
                m = i * 4 + (u * 2 + s)
                first = pl.conv - 3
                src = bank[2 * u + s][:, 0:n].rearrange("p (a n) -> p a n", n=L)
                dst = tt[2 + s][:, 0:n].rearrange("p (a n) -> p a n", n=L)
                tap = lambda w: vecs[:, ds(m + (V_MB_CW + CONVT * w + first), 1)]
                dve.wait_ge(cv_in, m + (first + 1))
                own(dve.scalar_tensor_tensor(dst[:, :, 1:L], src[:, :, 0:L - 1], tap(0), dst[:, :, 1:L],
                                             ALU.mult, ALU.add))
                dve.scalar_tensor_tensor(dst[:, :, 0:L - 1], src[:, :, 1:L], tap(2), dst[:, :, 0:L - 1],
                                         ALU.mult, ALU.add).then_inc(conv_free, 1)

            def xb_pair(i, last):
                for u in range(2):
                    if last and u == 1:
                        open_lo(DTP, 8 * P)
                    else:
                        next_lo(XB, False, i, u, 2)
                    for s in range(2):
                        taps(XB, i, u, s, NT)
            steps(dve, 6, xb_pair, own, 4)

            open_lo(CP)
            hp = slice(64, 128)
            v, av, e, w = pp[0][hp, :], tt[0][hp, :], tt[1][hp, :], rs[hp, :]
            dve.wait_ge(s_par, 64)
            dve.wait_ge(w_used, DTP.w + 1)
            dve.wait_ge(p_lo, MBN.q)
            own(dve.tensor_scalar(v, bank[4][hp, :], par[hp, 0:1], None, ALU.add))
            dve.scalar_tensor_tensor(av, v, -1.0, v, ALU.mult, ALU.max).then_inc(dt_v, 1)
            own(dve.tensor_scalar(v, v, 0.0, None, ALU.max))
            dve.wait_ge(dt_e, 2)
            own(dve.tensor_scalar(w, e, 2.0, None, ALU.add))
            own(dve.reciprocal(w, w))
            z, z2, s_ = tt[0][hp, :], tt[1][hp, :], rs[hp, :]
            own(dve.tensor_tensor(z, e, w, ALU.mult))
            own(dve.tensor_tensor(z2, z, z, ALU.mult))
            own(dve.tensor_scalar(s_, z2, 1.0 / 15, None, ALU.mult))
            for c in (13, 11, 9, 7, 5, 3):
                own(dve.scalar_tensor_tensor(s_, s_, 1.0 / c, z2, ALU.add, ALU.mult))
            own(dve.scalar_tensor_tensor(s_, s_, 1.0, z, ALU.add, ALU.mult))
            dt = pp[1][hp, :]
            own(dve.scalar_tensor_tensor(dt, s_, 2.0, v, ALU.mult, ALU.add))
            da = pp[0][hp, :]
            own(dve.tensor_scalar(da, dt, par[hp, 2:3], -1.0, ALU.mult, ALU.mult))
            own(dve.memset(tt[0][hp, 0:L], 1.0))
            cs = rs[hp, :]
            for seg in range(2):
                own.mark(dve.tensor_tensor_scan(cs[:, seg * L:seg * L + L], tt[0][hp, 0:L],
                                                da[:, seg * L:seg * L + L], 0.0, ALU.mult, ALU.add))
            own.sync()

            def c_pair(i, last):
                for u in range(2):
                    if last and u == 1:
                        open_lo(ZP)
                    else:
                        next_lo(CP, False, i, u, 2)
                    for s in range(2):
                        taps(CP, i, u, s, L)
            steps(dve, 2, c_pair, own, 4)

            def z_pair(i, last):
                for u in range(2):
                    if not (last and u == 1):
                        next_lo(ZP, False, i, u, 2)
            steps(dve, 4, z_pair)

            dve.wait_ge(w_used, ZP.w + 8)
            f, b = slice(64, 96), slice(96, 128)
            lat, cx = slice(0, L), slice(L, NT)
            own.mark(dve.tensor_scalar(dts[f, 0, :], rs[f, lat], -1.0, None, ALU.mult))
            own.mark(dve.scalar_tensor_tensor(dts[b, 0, :], rs[b, lat], rs[b, L - 1:L], pp[0][b, lat],
                                              ALU.subtract, ALU.subtract))
            own.mark(dve.tensor_copy(dts[hp, 1, :], pp[1][hp, lat]))
            own.mark(dve.tensor_scalar(dts[f, 3, :], rs[f, cx], rs[f, NT - 1:NT], -1.0, ALU.subtract, ALU.mult))
            dve.tensor_tensor(dts[b, 3, :], rs[b, cx], pp[0][b, cx], ALU.subtract).then_inc(dt_v, 1)
            own.sync()
            dve.tensor_scalar(dts[hp, 5, :], dts[hp, 0, :], -1.0, None, ALU.mult).then_inc(dt_v, 1)
            dve.wait_ge(dt_e, 3)
            dve.tensor_tensor(dts[hp, 2, :], dts[hp, 4, :], pp[1][hp, cx], ALU.mult).then_inc(dt_v, 1)
            dve.wait_ge(tk_t, 1)
            dve.tensor_copy(tk[:].rearrange("p a n -> p (a n)"), bank[7][:, 0:384]).then_inc(tk_out, 1)
            dve.wait_ge(tk_out, 1)

            def token_major(x0, row):
                for b8 in range(8):
                    T, c = b8 // 4, b8 % 4
                    dve.wait_ge(tr_mm, x0 + b8 + 1)
                    for d in range(2):
                        ins = dve.tensor_tensor(
                            xtok[:, d, T, c * 512:c * 512 + 512].rearrange("p (h w) -> p h w", w=HD),
                            bank[(x0 + b8) % 4][:].rearrange("p (h w) -> p h w", w=HD),
                            tk[:, row + T, 32 * d + 8 * c:32 * d + 8 * c + 8].unsqueeze(2).to_broadcast([P, 8, HD]),
                            ALU.mult)
                    ins.then_inc(tr_out, 1)
            token_major(0, 4)
            dve.wait_ge(st_mm, GROUPS)
            token_major(8, 2)
            dve.wait_ge(s_mask, 16)

            def group(i, u, first, finish):
                g = i * 2 + u
                for r in range(HPG):
                    if finish and r == 2:
                        gate_y(g)
                    bf = r % 2
                    h = i * 8 + (u * HPG + r)
                    use = i * 4 + (u * 2 + r // 2 + 1)
                    dve.wait_ge(afb_in[bf], use * 16)
                    if not (first and r == 0):
                        dve.wait_ge(e_done, h)
                    for d, T, t0, a in ((0, 0, 0, 0), (0, 1, P, 256), (1, 0, 0, 384), (1, 1, 0, 512)):
                        n = 128 if a in (256, 384) else 256
                        ins = dve.scalar_tensor_tensor(dm[:, a:a + n], afb[bf][:, d, t0:t0 + n],
                                                       tk[:, T, ds(h + 32 * d, 1)], mask[:, a:a + n], ALU.add, ALU.add)
                    ins.then_inc(d_done, 1)
                    dve.wait_ge(ex_done, h + 1)
                    dve.tensor_tensor(csx[bf][:], csx[bf][:], csb[:, g, :].unsqueeze(1).to_broadcast([P, 2, L]),
                                      ALU.mult).then_inc(cs_done, 1)

            def gate_y(g):
                dve.wait_ge(yt_t, g)
                for mt in range(2):
                    m = g * 2 + (mt - 2)
                    own.mark(dve.scalar_tensor_tensor(tt[3][:, mt * L:mt * L + L], xb[:, 0, m, :], dcol[:, ds(m, 1)],
                                                      bank[2][:, mt * L:mt * L + L], ALU.mult, ALU.add))
                own.sync()
                zz = zsb[:, ds(g * 2 - 2, 2), :]
                dve.tensor_tensor(zz, zz, tt[3][:].rearrange("p (a n) -> p a n", a=2), ALU.mult).then_inc(y_done, 1)

            core_groups(dve, group, lambda: gate_y(GROUPS), own, 4)

            for g in range(GROUPS):
                dve.wait_ge(g_rms, g + 1)
                own(dve.reciprocal(rs[:, 0:L], rs[:, 0:L]))
                q = MBN.q + g
                pp_free(q)
                p = pp[q % 2][:].rearrange("p (a n) -> p a n", a=2)
                ins = dve.tensor_tensor(p, zsb[:, 2 * g:2 * g + 2, :], rs[:, 0:L].unsqueeze(1).to_broadcast([P, 2, L]),
                                        ALU.mult)
                ins.then_inc(g_read, 1)
                dve.wait_ge(g_read, g + 1)
                for mt in range(2):
                    ins = dve.tensor_scalar(p[:, mt, :], p[:, mt, :], vecs[:, V_MB_NORM + 2 * g + mt:V_MB_NORM + 2 * g + mt + 1],
                                            None, ALU.mult)
                ins.then_inc(p_ready, 1)
            open_lo(MBOUT)

            def mb_pair(i, last):
                for um in range(2):
                    if last and um == 1:
                        open_lo(ffn_in["11"])
                    else:
                        next_lo(MBOUT, False, i, um, 2)
                    residual(MBOUT, 1, 5, i, um, L, i * 2 + (MBOUT.w + um + 1))
            steps(dve, DT // 2, mb_pair)
            ffn("11", 1, 6, 0, False, None, L)

            dve.wait_ge(rms_done, norms["fin"].norm + 1)
            own(dve.reciprocal(rs[:, 0:L], rs[:, 0:L]))
            for k in range(DT):
                if k >= 2:
                    dve.wait_ge(fin_t, k - 1)
                own(dve.tensor_tensor(pp[k % 2][:, 0:L], hT[:, k, 0:L], rs[:, 0:L], ALU.mult))
                dve.tensor_scalar(pp[k % 2][:, 0:L], pp[k % 2][:, 0:L], vecs[:, V_FINAL + k:V_FINAL + k + 1], None,
                                  ALU.mult).then_inc(fin_p, 1)

        @block.gpsimd
        def _(pool):
            own = Chain(pool, pool_own)

            def lo_tile(q, uses, dst, hi):
                pool.wait_ge(p_hi, uses)
                n = dst.shape[-1]
                pool.tensor_tensor(dst, pp[q % 2][:, 0:n], hi.bitcast(F32), ALU.subtract).then_inc(p_lo, 1)

            def norm_lo(key, n=NT):
                pl = norms[key]
                for k in range(DT):
                    lo_tile(pl.q + k, pl.q + k + 1, xl[:, k, 0:n], xh[:, k, 0:n])

            def clear(key):
                pool.wait_ge(nsum, norms[key].norm + 1)
                pool.memset(acc[:], 0.0).then_inc(acc_zero, 1)

            def add_squares(pl, zeroed, n=NT):
                pool.wait_ge(acc_zero, zeroed)

                def pair(i, last):
                    for um in range(2):
                        pool.wait_ge(sq_done, i * 2 + (pl.h + um + 1))
                        pool.wait_ge(acc_done, i * 2 + (pl.h + um))
                        pool.tensor_tensor(acc[:, 0:n], acc[:, 0:n], tt[um][:, 0:n], ALU.add).then_inc(acc_done, 1)
                if pl.h == 0:
                    for i in range(DT // 2):
                        for um in range(2):
                            pool.wait_ge(sq_done, 2 * i + um + 1)
                            if i or um:
                                pool.wait_ge(acc_done, 2 * i + um)
                            pool.tensor_tensor(acc[:, 0:n], acc[:, 0:n], tt[um][:, 0:n], ALU.add).then_inc(acc_done, 1)
                else:
                    with pool.Fori(0, DT // 2) as i:
                        pair(i, False)

            def ffn(key, zeroed, n=NT):
                norm_lo(key, n)
                clear(key)
                pi = ffn_in[key]
                with pool.Fori(0, FT // 2) as i:
                    for u in range(2):
                        lo_tile(pi.q + u, i * 2 + (pi.q + u + 1), gl[:, i * 2 + u, 0:n], gh[:, i * 2 + u, 0:n])
                add_squares(ffn_out[key], zeroed, n)

            pool.memset(acc[:], 0.0).then_inc(acc_zero, 1)
            add_squares(P0, 1)
            for unit in range(4):
                for n in range(4):
                    q = unit * 4 + n
                    lo_tile(q, q + 1, fel[:, n % 2, n // 2, :], feh[:, n % 2, n // 2, :])
            ffn("00", 2)
            norm_lo("hy")
            clear("hy")
            for x in range(8):
                for n in range(5):
                    c0 = x * 4 + n
                    q = HYDFT.q + c0
                    if n < 4:
                        pool.wait_ge(cm_mul, c0 + 1)
                        if x or n > 1:
                            pool.wait_ge(p_lo, q - 1)
                        pool.tensor_tensor(pp[q % 2][:], tt[2 * (n % 2)][:], tt[2 * (n % 2) + 1][:],
                                           ALU.subtract if n < 2 else ALU.add).then_inc(p_ready, 1)
                    if n:
                        m = n - 1
                        lo_tile(q - 1, q, wl[1][:, m * 512:m * 512 + 512], wh[1][:, m * 512:m * 512 + 512])
            for k in range(DT):
                lo_tile(HYY.q + k, HYY.q + k + 1, xl[:, k, :], xh[:, k, :])
            add_squares(HYOUT, 3)
            ffn("01", 4)
            ffn("10", 5)
            norm_lo("mb")
            clear("mb")
            pool.wait_ge(s_set, 1)

            def group(i, u, first, finish):
                pool.wait_ge(cb_out, i * 2 + (u + 1))
                for r in range(HPG):
                    h = i * 8 + (u * HPG + r)
                    pool.wait_ge(e_done, h + 1)
                    if not (first and r < 2):
                        pool.wait_ge(head_mm, h - 1)
                    pool.tensor_tensor(mm_[r % 2][:], ee[r % 2][:], cbx[:], ALU.mult).then_inc(m_done, 1)

            core_groups(pool, group, lambda: None)
            for g in range(GROUPS):
                lo_tile(MBN.q + g, MBN.q + g + 1, ynl[:, 2 * g:2 * g + 2, :].rearrange("p a n -> p (a n)"),
                        ynh[:, 2 * g:2 * g + 2, :].rearrange("p a n -> p (a n)"))
            add_squares(MBOUT, 6, L)
            ffn("11", 7, L)

        @block.tensor
        def _(pe):
            def mm3(dst, wslot, lo, x_hi, x_lo, start, stop):
                h, l_ = wh[wslot][:, lo:lo + P], wl[wslot][:, lo:lo + P]
                pe.matmul(dst, h, x_hi, start=start, stop=False)
                pe.matmul(dst, h, x_lo, start=False, stop=False)
                return pe.matmul(dst, l_, x_hi, start=False, stop=stop)

            def ada_chunk(r_slot, uses, layer, col):
                pe.wait_ge(raw_in[r_slot], uses * 16)
                for s in range(2):
                    for k in range(DT):
                        ins = pe.matmul(bank[6 + layer][:, ds(col + 2 * s, 2)],
                                        raw[r_slot][:, k * 256 + s * P:k * 256 + s * P + P], sc[:, k, :],
                                        start=k == 0, stop=k == DT - 1)
                ins.then_inc(ada_used, 1)

            def norm(key, n=NT):
                pl = norms[key]
                pe.wait_ge(acc_done, pl.h)
                pe.matmul(bank[0][:, 0:n], ones[:], acc[:, 0:n], start=True, stop=True).then_inc(nsum, 1)

            def two_tiles(wslot, banks, q, n=NT):
                for k in range(DT):
                    pe.wait_ge(p_lo, q + k + 1)
                    for s in range(2):
                        ins = mm3(bank[banks + s][:, 0:n], wslot, k * 256 + s * P, xh[:, k, 0:n], xl[:, k, 0:n],
                                  k == 0, k == DT - 1)
                ins.then_inc(w_used, 1)

            def ffn(key, ada_in, ada_out_, n=NT):
                norm(key, n)
                pi, po = ffn_in[key], ffn_out[key]
                x0 = norms[key].q
                if ada_in and key == "00":
                    pe.wait_ge(ada_out, 1)

                def pair(i, last):
                    for u in range(2):
                        pe.wait_ge(w_lo, i * 2 + (pi.w + u + 1))
                        if u == 0:
                            pe.wait_ge(gate_ready, i * 2 + pi.gate)
                        else:
                            pe.wait_ge(p_ready, i * 2 + pi.q)
                        two_tiles((pi.w + u) % 2, 2 * u, x0, n)
                        if ada_in and not (last and ada_in[0] < FT // 2):
                            r = pi.raw + 2 * u + 1
                            ada_chunk(r % 2, i * 2 + (r // 2 + 1), ada_in[1], i * 8 + (4 * ada_in[2] + 4 * u))
                steps(pe, FT // 2, pair)

                def mpair(i, last):
                    for um in range(2):
                        pe.wait_ge(h_done, i * 2 + (po.h + um - 1))
                        for half in range(2):
                            u = um * 2 + half
                            n_ = po.w + u
                            pe.wait_ge(w_lo, i * 4 + (n_ + 1))
                            if u == 0:
                                pe.wait_ge(p_lo, pi.q + FT - 2)
                            for kk in range(11):
                                k = half * 11 + kk
                                if k == FT - 2 and um == 0:
                                    pe.wait_ge(p_lo, pi.q + FT)
                                ins = mm3(bank[4 + um][:, 0:n], n_ % 2, kk * P, gh[:, k, 0:n], gl[:, k, 0:n],
                                          k == 0, k == FT - 1)
                            ins.then_inc(w_used, 1)
                            if ada_out_:
                                r = po.raw + 2 * u + 1
                                ada_chunk(r % 2, i * 4 + (r // 2 + 1), ada_out_[1], i * 16 + (4 * ada_out_[2] + 4 * u))
                steps(pe, DT // 2, mpair)

            pe.wait_ge(s_cst, 16)
            pe.wait_ge(s_vec, 16 * VEC_DMAS)
            stage = tt[0][:, :].rearrange("p (a c) -> p a c", c=P)
            for a in range(4):
                n = min(P, V_ALL - a * P)
                ins = pe.transpose(bank[7][:, a * P:a * P + n], stage[0:n, a, :], small[0:n, 0:n])
            ins.then_inc(vec_t, 1)
            pe.wait_ge(s_x, 32)
            for k in range(DT):
                if k >= 4:
                    pe.wait_ge(h_done, k - 3)
                for a in range(4):
                    ins = pe.transpose(bank[k % 4][:, a * P:a * P + P], xstage[:, a, k * P:k * P + P], ident)
                ins.then_inc(x_t, 1)
            pe.wait_ge(s_fil, 16 * 8)
            pe.wait_ge(vec_out, 1)
            for layer in range(2):
                rows_, rhs = (33, hsm[0:33, 0, :]) if layer == 0 else (64, hsm[:, 3, :])
                if layer:
                    pe.wait_ge(hid_sin, 1)
                pe.matmul(bank[7][0:64, 0:L], hsm[0:rows_, 1, 64 * layer:64 * layer + 64], rhs,
                          start=True, stop=True).then_inc(hid_mm, 1)
            pe.wait_ge(sc_done, 1)
            pe.wait_ge(h_done, DT)
            done = 0

            def early_ada(n):
                nonlocal done
                for _ in range(n):
                    i = done
                    c = i if i < 12 else 22 + i
                    r = 2 + i
                    ada_chunk(r % 2, r // 2 + 1, 0, 4 * c)
                    done += 1
            pe.wait_ge(hid_sin, 2)
            for unit in range(4):
                o_, hh = unit // 2, unit % 2
                if unit:
                    pe.wait_ge(p_ready, unit * 4)
                for n in range(2):
                    for d in range(2):
                        c = (o_ * 2 + d) * D + hh * 512
                        ins = pe.matmul(bank[2 * d + n][:], hsm[:, 4, n * P:n * P + P], w3[:, c:c + 512],
                                        start=True, stop=True)
                    ins.then_inc(fil_mm, 1)
                early_ada(3 if unit else 2)
                pe.wait_ge(w_lo, 2)
                for kt in range(5):
                    x = unit * 5 + kt
                    if x >= 2:
                        pe.wait_ge(spec_out, x - 1)
                    eo = 1 if kt in (2, 3) else 0
                    for k in range(2):
                        pe.wait_ge(p_lo, unit * 4 + 2 * k + eo + 1)
                        slot, lo = (0, k * 512 + kt * P) if kt < 4 else (1, k * P)
                        ins = mm3(bank[4 + x % 2][:], slot, lo, feh[:, eo, k, :], fel[:, eo, k, :], k == 0, k == 1)
                    ins.then_inc(spec_mm, 1)
            early_ada(FIRST_ADA - done)
            pe.wait_ge(s_set, 2)
            pe.wait_ge(p_ready, 16)
            pe.wait_ge(spec_out, 20)
            pe.matmul(bank[5][:, 0:1], ones[:], ones[:, 0:1], start=True, stop=True).then_inc(w_used, 2)

            ffn("00", (FT // 2, 0, 12), (True, 1, 0))
            norm("hy")
            def hy_pair(i, last):
                for u in range(2):
                    pe.wait_ge(w_lo, i * 2 + (HYIN.w + u + 1))
                    pe.wait_ge(z_free, i * 4 + (HYIN.zf + 2 * u - 2))
                    two_tiles((HYIN.w + u) % 2, 2 * u, norms["hy"].q)
            steps(pe, 6, hy_pair)
            pe.wait_ge(w_lo, HYDFT.w + 1)
            pe.wait_ge(z_free, HYIN.zf + 24)
            pe.wait_ge(hy_ready, 2 + 24)
            for conv in range(2):
                if conv:
                    pe.wait_ge(inv_out, 16)
                for b in range(8):
                    x = conv * 8 + b
                    if b >= 2:
                        pe.wait_ge(vt_lo, x - 1)
                    for c in range(4):
                        ins = pe.transpose(bank[4 + b % 2][:, c * P:c * P + P],
                                           hyu[:, (0 if conv else 16) + (b % 2) * 4 + c, (b // 2) * P:(b // 2) * P + P], ident)
                    ins.then_inc(vt_t, 1)
                for unit in range(5):
                    if unit < 4:
                        x = conv * 4 + unit
                        seg, half = unit // 2, unit % 2
                        if x:
                            pe.wait_ge(cm_mul, 4 * x)
                        for ft in range(4):
                            for k in range(2):
                                b = (2 * seg + k) * 2 + half
                                pe.wait_ge(vt_lo, conv * 8 + b + 1)
                                ins = mm3(bank[ft][:], 0, k * 512 + ft * P, xh[:, b, :], xl[:, b, :], k == 0, k == 1)
                        ins.then_inc(fwd_mm, 1)
                    if unit:
                        y = conv * 4 + unit - 1
                        pe.wait_ge(p_lo, HYDFT.q + 4 * y + 4)
                        for c in range(4):
                            if c % 2 == 0:
                                if unit > 1:
                                    pe.wait_ge(inv_out, 4 * (y - 1) + c + 2)
                                else:
                                    pe.wait_ge(vt_lo, conv * 8 + 8)
                            dst = bank[4 + c // 2][:, (c % 2) * L:(c % 2) * L + L]
                            for ft in range(4):
                                y_h = wh[1][:, ft * 512 + c * P:ft * 512 + c * P + P]
                                y_l = wl[1][:, ft * 512 + c * P:ft * 512 + c * P + P]
                                f_h = wh[0][:, 1024 + ft * L:1024 + ft * L + L]
                                f_l = wl[0][:, 1024 + ft * L:1024 + ft * L + L]
                                pe.matmul(dst, y_h, f_h, start=ft == 0, stop=False)
                                pe.matmul(dst, y_h, f_l, start=False, stop=False)
                                ins = pe.matmul(dst, y_l, f_h, start=False, stop=ft == 3)
                            if c % 2:
                                ins.then_inc(inv_mm, 1)
            pe.wait_ge(cm_mul, 32)
            pe.matmul(bank[0][:, 0:1], ones[:], ones[:, 0:1], start=True, stop=True).then_inc(w_used, 1)
            for j in range(4):
                pe.wait_ge(w_lo, HYOUT.w + j + 1)
                pe.wait_ge(h_done, HYOUT.h + 2 * j) if j else pe.wait_ge(inv_out, 32)
                two_tiles((HYOUT.w + j) % 2, 4, HYY.q)
            ffn("01", (10, 1, 16), None)

            ffn("10", None, None)
            norm("mb")
            x0 = norms["mb"].q

            def wide(pl, chunks, free, base, n):
                def pair(i, last):
                    for u in range(2):
                        pe.wait_ge(w_lo, i * 2 + (pl.w + u + 1))
                        pe.wait_ge(free, i * 4 + (base + 2 * u - 2))
                        two_tiles((pl.w + u) % 2, 2 * u, x0, n)
                steps(pe, chunks // 2, pair)
            wide(XB, 12, conv_free, XB.conv, NT)
            pe.wait_ge(w_lo, DTP.w + 1)
            for k in range(DT):
                ins = mm3(bank[4][:], DTP.w % 2, k * P, xh[:, k, :], xl[:, k, :], k == 0, k == DT - 1)
            ins.then_inc(w_used, 1)
            wide(CP, 4, conv_free, CP.conv, L)
            pe.wait_ge(conv_free, CP.conv + 8)
            wide(ZP, 8, z_free, ZP.zf, L)

            pe.wait_ge(z_free, ZP.zf + 16)
            pe.wait_ge(cv_silu, 2 + 32)
            for b in range(4):
                if b >= 2:
                    pe.wait_ge(tb_out, b - 1)
                for c in range(4):
                    m = IT + (b % 2) * 4 + c
                    ins = pe.transpose(bank[6 + b % 2][:, c * P:c * P + P], xb[:, 1, m, (b // 2) * P:(b // 2) * P + P], ident)
                ins.then_inc(tb_mm, 1)

            def turn_x(x0_, seg):
                for b8 in range(8):
                    T, c4 = b8 // 4, b8 % 4
                    if x0_ + b8 >= 4:
                        pe.wait_ge(tr_out, x0_ + b8 - 3)
                    for c in range(4):
                        ins = pe.transpose(bank[(x0_ + b8) % 4][:, c * P:c * P + P],
                                           xb[:, seg, c4 * 4 + c, T * P:T * P + P], ident)
                    ins.then_inc(tr_mm, 1)
            pe.wait_ge(dt_v, 4)
            pe.wait_ge(tb_out, 4)
            for j in range(6):
                ins = pe.transpose(bank[7][:, 64 * j:64 * j + 64], dts[64:128, j // 2, (j % 2) * P:(j % 2) * P + P],
                                   small[64:128, 64:128])
            ins.then_inc(tk_t, 1)
            turn_x(0, 1)
            pe.wait_ge(tr_out, 8)
            for g in range(GROUPS):
                if g >= 2:
                    pe.wait_ge(st_out, g - 1)
                for d in range(2):
                    for T in range(2):
                        ins = pe.matmul(bank[4 + g % 2][:, d * L:d * L + L], btok[:, T, g * P:g * P + P],
                                        xtok[:, d, T, g * L:g * L + L], start=T == 0, stop=T == 1)
                ins.then_inc(st_mm, 1)
            turn_x(8, 0)
            pe.wait_ge(tr_out, 16)
            pe.wait_ge(st_out, GROUPS)
            pe.wait_ge(tk_out, 1)

            def group(i, u, first, finish):
                g = i * 2 + u
                pe.wait_ge(b_st, g + 1)
                if not first:
                    pe.wait_ge(cb_out, g)
                for T in range(2):
                    ins = pe.matmul(bank[6][:, T * L:T * L + L], bst[:, T * P:T * P + P], csb[:, g, :], start=True, stop=True)
                ins.then_inc(cb_mm, 1)
                for r in range(HPG):
                    if finish and r == 2:
                        turn_y(g)
                    b = r % 2
                    h = i * 8 + (u * HPG + r)
                    if r == 0 and not (isinstance(g, int) and g < 2):
                        pe.wait_ge(y_out, g - 1)
                    pe.wait_ge(cs_done, h + 1)
                    pe.wait_ge(m_done, h + 1)
                    for T in range(2):
                        dst = bank[4 + u][:, T * L + r * HD:T * L + r * HD + HD]
                        blocks = ((0, 0, 0), (1, 0, 384), (1, 1, 512)) if T == 0 else \
                            ((0, 0, 128), (0, 1, 256), (1, 1, 640))
                        for n, (d, s, a) in enumerate(blocks):
                            pe.matmul(dst, mm_[b][:, a:a + P], xtok[:, d, s, ds(h * HD, HD)], start=n == 0, stop=False)
                        for d in range(2):
                            ins = pe.matmul(dst, csx[b][:, d, T * P:T * P + P], ssb[:, d, ds(h * HD, HD)],
                                            start=False, stop=d == 1)
                    ins.then_inc(head_mm, 1)

            def turn_y(g):
                pe.wait_ge(y_out, g)
                if not isinstance(g, int) or g > 1:
                    pe.wait_ge(y_done, g - 1)
                for mt in range(2):
                    for T in range(2):
                        ins = pe.transpose(bank[2][:, mt * L + T * P:mt * L + T * P + P],
                                           tt[2][:, T * L + mt * P:T * L + mt * P + P], ident)
                ins.then_inc(yt_t, 1)
            core_groups(pe, group, lambda: turn_y(GROUPS))
            pe.wait_ge(cb_out, GROUPS)
            for g in range(GROUPS):
                pe.wait_ge(g_sq, g + 1)
                if g >= 2:
                    pe.wait_ge(g_rms, g - 1)
                for mt in range(2):
                    ins = pe.matmul(bank[6 + g % 2][:, 0:L], ones[:], tt[g % 2][:, mt * L:mt * L + L],
                                    start=mt == 0, stop=mt == 1)
                ins.then_inc(g_sum, 1)

            def mb_pair(i, last):
                for um in range(2):
                    n_ = MBOUT.w + um
                    pe.wait_ge(w_lo, i * 2 + (n_ + 1))
                    pe.wait_ge(h_done, i * 2 + (MBOUT.h + um - 1))
                    for k in range(IT):
                        if k % 2 == 0 and um == 0:
                            pe.wait_ge(p_lo, MBN.q + k // 2 + 1)
                        ins = mm3(bank[4 + um][:, 0:L], n_ % 2, k * P, ynh[:, k, :], ynl[:, k, :], k == 0, k == IT - 1)
                    ins.then_inc(w_used, 1)
            steps(pe, DT // 2, mb_pair)
            ffn("11", None, None, L)
            norm("fin", L)
            for k in range(DT):
                pe.wait_ge(fin_p, k + 1)
                if k >= 4:
                    pe.wait_ge(fin_o, k - 3)
                else:
                    pe.wait_ge(rms_done, norms["fin"].norm + 1)
                for T in range(2):
                    ins = pe.transpose(bank[k % 4][:, T * P:T * P + P], pp[k % 2][:, T * P:T * P + P], ident)
                ins.then_inc(fin_t, 1)


_INS = ['x', 'c', 'ctx', 'c_ctx', 'ada_w', 'ada_b', 'ffn_in', 'ffn_out', 'hy_in_w', 'hy_in_b', 'hy_conv_w',
        'hy_conv_b', 'hy_pos_w1', 'hy_pos_b1', 'hy_freq', 'hy_pos_w2', 'hy_pos_b2', 'hy_pos_w3', 'hy_bias',
        'hy_out_w', 'hy_out_b', 'mb_in_w', 'mb_conv_w', 'mb_conv_b', 'mb_dt_bias', 'mb_A_log', 'mb_D',
        'mb_norm_w', 'mb_out_w', 'final_norm_w']


def _constants():
    import math
    import numpy as np

    n = 2 * L
    f32 = np.float32
    tok = np.arange(L)
    ang = 2 * math.pi * ((tok[:, None] * np.arange(L)[None, :]) % n) / n
    alt = np.where(tok % 2, -1.0, 1.0)
    cos, sin = np.cos(ang), -np.sin(ang)
    im = sin.copy()
    im[:, 0] = alt
    cos2 = cos.copy()
    cos2[:, 0] = alt
    fwd = np.concatenate([cos, im], 1)
    inv_re = 2 * cos.T / n
    inv_re[0] /= 2
    inv_im = 2 * sin.T / n
    inv_im[0] = alt / n
    inv = np.concatenate([inv_re, inv_im], 0)
    dft1 = np.concatenate([fwd.reshape(2, P, 512).transpose(1, 0, 2).reshape(P, 1024),
                           inv.reshape(4, P, L).transpose(1, 0, 2).reshape(P, 1024)], 1)
    dft2 = cos2[:, 0:P].reshape(2, P, P).transpose(1, 0, 2).reshape(P, 256)
    tl = np.linspace(0.0, 1.0, L, dtype=f32)
    bands = np.linspace(1e-4, 15, 16, dtype=f32)
    a = (f32(2.0 * math.pi / L) * tok.astype(f32)[:, None] * bands[None, :]).astype(f32)
    z = np.concatenate([tl[:, None], np.cos(a), -np.sin(a)], 1)
    deltas = np.abs(np.linspace(math.log(1e-2) / 1.5, math.log(1e-2) / 0.3, D, dtype=f32))
    dec = np.exp(-tl[:, None] * deltas[None, :]).reshape(2, P, D).transpose(1, 0, 2).reshape(P, 2 * D)
    small = np.concatenate([np.eye(P), np.ones((P, 1))], 1)
    small[0, P] = 0
    s, tt_ = np.arange(P)[:, None], np.arange(P)[None, :]
    f = np.where(tt_ >= s, 0.0, -1e30)
    b = np.where(tt_ <= s, 0.0, -1e30)
    o = np.zeros((P, P))
    mask = np.concatenate([f, o, f, b, o, b], 1)
    return {k: np.ascontiguousarray(v, dtype=f32) for k, v in
            dict(c_dft1=dft1, c_dft2=dft2, c_z=z.T, c_decay=dec, c_small=small, c_mask=mask).items()}


def kernel(**inputs):
    import numpy as _np
    import concourse.bacc as _bacc
    from concourse.bass_utils import run_bass_kernel_spmd as _run

    nc = _bacc.Bacc("TRN2", target_bir_lowering=False, num_devices=1)
    arrays, args = {}, {}
    given = {name: _np.ascontiguousarray(inputs[name]) for name in _INS}
    given.update(_constants())
    for name, a in given.items():
        arrays[f"in_{name}"] = a
        args[name] = nc.dram_tensor(f"in_{name}", a.shape, mybir.dt.from_np(a.dtype), kind="ExternalInput").ap()
    out = nc.dram_tensor("out_0", (1, L, D), F32, kind="ExternalOutput").ap()
    kscr = nc.dram_tensor("filter_spectra", (P, 10 * D), F32, kind="Internal").ap()
    afscr = nc.dram_tensor("decays", (HEADS, 2, L), F32, kind="Internal").ap()
    build(nc, args, out, kscr, afscr)
    r = _run(nc, [arrays], core_ids=[0])
    return r.results[0]["out_0"]
```

```python
from contextlib import ExitStack, contextmanager

import concourse.bass as bass
from concourse import mybir

F32 = mybir.dt.float32
F32R = mybir.dt.float32r
ALU = mybir.AluOpType
ACT = mybir.ActivationFunctionType

P = 128
D = 1024
DT = D // P
L = 256
NT = 2 * L
FFN = 2816
FT = FFN // P
INNER = 2048
IT = INNER // P
GROUPS = 8
HPG = 4
HEADS = GROUPS * HPG
HD = 64
CONVT = 32
MB_IN = 6208
EPS = 1e-6
CW = 2048
MODT = 9 * DT
ADA_CHUNKS = 36
FIRST_ADA = 14
EARLY_V = FIRST_ADA // 2
HYENA_ADA = 14

V_ADA = 0
V_HY_IN_B = 144
V_HY_CW = 168
V_HY_CB = 240
V_HY_BIAS = 264
V_HY_OUT_B = 280
V_MB_CW = 288
V_MB_CB = 384
V_MB_NORM = 416
V_FINAL = 432
V_C = 440
V_CCTX = 448
V_ALL = 456
VEC_ROWS = (("ada_b", 144), ("hy_in_b", 24), ("hy_conv_w", 72), ("hy_conv_b", 24), ("hy_bias", 16),
            ("hy_out_b", 8), ("mb_conv_w", 96), ("mb_conv_b", 32), ("mb_norm_w", 16), ("final_norm_w", 8),
            ("c", 8), ("c_ctx", 8))


def vec_pieces():
    base, out = 0, []
    for name, count in VEC_ROWS:
        done = 0
        while done < count:
            k = min(count - done, P - (base + done) % P)
            out.append((name, done, k, base + done))
            done += k
        base += count
    return out


VEC_DMAS = len(vec_pieces())

TWO_PI = (6.28125, 0.0019350051879882812, 3.019916050561733e-07)
ROUND = 12582912.0
PI_DOWN = 3.1415925


class Chain:

    def __init__(self, eng, sem):
        self.eng, self.sem, self.base, self.n = eng, sem, 0, 0

    def mark(self, ins):
        ins.then_inc(self.sem, 1)
        self.n += 1

    def sync(self):
        self.eng.wait_ge(self.sem, self.base + self.n)

    def __call__(self, ins):
        self.mark(ins)
        self.sync()


@contextmanager
def rolled(eng, count, chain=None, per=0):
    start = chain.base + chain.n if chain else 0
    with eng.Fori(0, count) as i:
        if chain:
            chain.base, chain.n = i * per + start, 0
        yield i
        if chain:
            assert chain.n == per, (chain.n, per)
    if chain:
        chain.base, chain.n = start + count * per, 0


def steps(eng, count, body, chain=None, per=0):
    if count > 1:
        with rolled(eng, count - 1, chain, per) as i:
            body(i, False)
    body(count - 1, True)


def steps_both(eng, count, body):
    body(0, True, False)
    with eng.Fori(0, count - 2) as i:
        body(i + 1, False, False)
    body(count - 1, False, True)


class Place:

    def __init__(self, plan, w=0, a=0, v=0, q=0, h=0, gate=0, conv=0, zf=0, norm=0):
        self.v = plan["v"]
        self.w, self.a, self.raw, self.q, self.h = plan["w"], plan["a"], plan["raw"], plan["q"], plan["h"]
        self.gate, self.conv, self.zf, self.norm = plan["gate"], plan["conv"], plan["zf"], plan["norm"]
        for name, add in (("w", w), ("a", a), ("v", v), ("raw", w + a), ("q", q), ("h", h), ("gate", gate),
                          ("conv", conv), ("zf", zf), ("norm", norm)):
            plan[name] += add


def core_groups(eng, group, tail, chain=None, per=0):
    group(0, 0, True, False, False)
    group(0, 1, False, True, False)
    with rolled(eng, GROUPS // 2 - 2, chain, per) as i:
        group(i + 1, 0, False, True, False)
        group(i + 1, 1, False, True, False)
    group(GROUPS // 2 - 1, 0, False, True, False)
    group(GROUPS // 2 - 1, 1, False, True, True)
    tail()


def build(nc, t, out, kscr, afscr):
    plan = dict(w=0, a=0, v=0, raw=0, q=0, h=0, gate=1, conv=3, zf=3, norm=0)
    P0 = Place(plan, w=2, a=FIRST_ADA, v=EARLY_V, q=16, h=DT)
    ffn_in, ffn_out, norms = {}, {}, {}

    def plan_norm(key, k=DT):
        norms[key] = Place(plan, q=k, norm=1)

    def plan_ffn(key, a_in=0):
        plan_norm(key)
        ffn_in[key] = Place(plan, w=FT, a=a_in, v=a_in, q=FT, gate=FT)
        ffn_out[key] = Place(plan, w=2 * DT, h=DT)

    plan_ffn("00", FT)
    plan_norm("hy")
    HYIN = Place(plan, w=12, zf=24)
    HYDFT = Place(plan, w=1, a=HYENA_ADA, q=32)
    HYY = Place(plan, q=8)
    HYOUT = Place(plan, w=4, h=DT)
    plan_ffn("01", FT)
    plan_ffn("10")
    plan_norm("mb")
    XB = Place(plan, w=12, conv=24)
    DTP = Place(plan, w=1)
    CP = Place(plan, w=4, conv=8)
    ZP = Place(plan, w=8, zf=16)
    MBN = Place(plan, q=8)
    MBOUT = Place(plan, w=8, h=DT)
    plan_ffn("11")
    plan_norm("fin", 0)

    with ExitStack() as ctx:
        top = [16512]

        def at(name, shape, dt, offset):
            return nc.alloc_sbuf_tensor_at(name, shape, dt, offset=offset)

        def room(nbytes):
            o = top[0]
            top[0] = o + (nbytes + 31) // 32 * 32
            assert top[0] <= 229344, top[0]
            return o

        def sb(name, cols, dt=F32):
            n = 4
            for c in cols:
                n *= c
            return at(name, [P, *cols], dt, room(n))

        def sem(name):
            return ctx.enter_context(nc.semaphore(name))

        KB = 1024
        hT = sb("hT", [DT, NT])
        o_xh = room(16 * KB)
        o_xl = room(16 * KB)
        assert o_xl == o_xh + 16 * KB
        xh = at("xh", [P, DT, NT], F32R, o_xh)
        xl = at("xl", [P, DT, NT], F32R, o_xl)
        xtok = at("xtok", [P, 2, 2, INNER], F32, o_xh)
        xstage = at("xstage", [P, 4, D], F32, o_xl)
        big = room(88 * KB)
        gh = at("gh", [P, FT, NT], F32R, big)
        gl = at("gl", [P, FT, NT], F32R, big + 44 * KB)
        ksb = at("ksb", [P, 4, 5, 512], F32, big)
        hyu = at("hyu", [P, 24, NT], F32, big + 40 * KB)
        w3 = at("w3", [64, 4 * D], F32, big + 40 * KB)
        decay = at("decay", [P, 2, D], F32, big + 56 * KB)
        feh = at("feh", [P, 2, 2, 512], F32R, big + 64 * KB)
        fel = at("fel", [P, 2, 2, 512], F32R, big + 72 * KB)
        hsm = at("hsm", [64, 7, L], F32, big + 80 * KB)
        xb = at("xb", [P, 2, 24, L], F32, big)
        csb = at("csb", [P, 8, L], F32, big + 48 * KB)
        zsb = at("zsb", [P, IT, L], F32, big + 56 * KB)
        ssb = at("ssb", [P, 2, INNER], F32, big + 72 * KB)
        ynh = at("ynh", [P, IT, L], F32R, big + 24 * KB)
        ynl = at("ynl", [P, IT, L], F32R, big + 56 * KB)
        ost = at("ost", [P, 2, D], F32, big)
        raw = [sb(f"raw{i}", [CW]) for i in range(2)]
        o_w = room(32 * KB)
        wh = [at(f"wh{i}", [P, CW], F32R, o_w + i * 8 * KB) for i in range(2)]
        wl = [at(f"wl{i}", [P, CW], F32R, o_w + (2 + i) * 8 * KB) for i in range(2)]
        o = [o_w]

        def core(name, cols, parts=P):
            n = 4
            for c in cols:
                n *= c
            o[0] += n
            assert o[0] <= o_w + 32 * KB
            return at(name, [parts, *cols], F32, o[0] - n)

        ee = [core(f"ee{i}", [2 * L]) for i in range(HPG)]
        mm_ = [core(f"mm{i}", [3 * L]) for i in range(2)]
        afb = [core(f"afb{i}", [2, L]) for i in range(HPG)]
        dm = [core(f"dm{i}", [2 * P]) for i in range(2)]
        cbx = [core(f"cbx{i}", [3 * L]) for i in range(2)]
        mask = core("mask", [3, P])
        btok = at("btok", [P, 2, D], F32, o_w)
        dts = at("dts", [P, 8, L], F32, o_w + 12 * KB)
        tt = [sb(f"tt{i}", [NT]) for i in range(4)]
        early_av = [at(f"early_av{i}", [P, NT], F32, o_xh + i * 2 * KB) for i in range(2)]
        pp = [sb(f"pp{i}", [NT]) for i in range(2)]
        csx = tt[0:2] + pp
        acc = sb("acc", [NT])
        rs = sb("rs", [NT])
        vecs = sb("vecs", [V_ALL])
        mods = [sb(f"mods{i}", [MODT, 2]) for i in range(2)]
        sc = sb("sc", [DT, 2])
        small = sb("small", [129])
        ones = sb("ones", [P])
        eps = sb("eps", [1])
        par = sb("par", [4])
        dcol = sb("dcol", [IT])
        tk = sb("tk", [6, 64])
        ident = small[:, 0:P]
        mask0 = small[:, P:P + 1]

        bank = [ctx.enter_context(nc.psum_tensor(f"bank{i}", [P, 512], F32)) for i in range(8)]

        raw_in = [sem(f"raw_in{i}") for i in range(2)]
        w_hi = sem("w_hi")
        w_lo = sem("w_lo")
        w_used = sem("w_used")
        ada_dve = sem("ada_dve")
        ada_used = sem("ada_used")
        ada_out = sem("ada_out")
        p_ready = sem("p_ready")
        p_hi = sem("p_hi")
        p_lo = sem("p_lo")
        h_done = sem("h_done")
        sq_done = sem("sq_done")
        acc_done = sem("acc_done")
        acc_zero = sem("acc_zero")
        nsum = sem("nsum")
        rms_done = sem("rms_done")
        gate_ready = sem("gate_ready")
        conv_free = sem("conv_free")
        z_free = sem("z_free")
        act_own = sem("act_own")
        dve_own = sem("dve_own")
        pool_own = sem("pool_own")
        s_vec = sem("s_vec")
        s_x = sem("s_x")
        s_cst = sem("s_cst")
        s_fil = sem("s_fil")
        s_par = sem("s_par")
        s_set = sem("s_set")
        vec_t = sem("vec_t")
        vec_out = sem("vec_out")
        sc_done = sem("sc_done")
        x_t = sem("x_t")
        hid_mm = sem("hid_mm")
        hid_arg = sem("hid_arg")
        hid_sin = sem("hid_sin")
        fil_mm = sem("fil_mm")
        fil_read = sem("fil_read")
        spec_mm = sem("spec_mm")
        spec_out = sem("spec_out")
        spec_st = sem("spec_st")
        spec_ld = sem("spec_ld")
        hy_ready = sem("hy_ready")
        vt_t = sem("vt_t")
        vt_hi = sem("vt_hi")
        vt_lo = sem("vt_lo")
        fwd_mm = sem("fwd_mm")
        fwd_read = sem("fwd_read")
        cm_mul = sem("cm_mul")
        cm_add = sem("cm_add")
        inv_mm = sem("inv_mm")
        inv_out = sem("inv_out")
        cv_in = sem("cv_in")
        cv_out = sem("cv_out")
        cv_silu = sem("cv_silu")
        dt_v = sem("dt_v")
        dt_e = sem("dt_e")
        af_st = sem("af_st")
        tk_t = sem("tk_t")
        tk_out = sem("tk_out")
        tr_mm = sem("tr_mm")
        tr_out = sem("tr_out")
        tb_mm = sem("tb_mm")
        tb_out = sem("tb_out")
        st_mm = sem("st_mm")
        st_out = sem("st_out")
        s_mask = sem("s_mask")
        afb_in = [sem(f"afb_in{i}") for i in range(HPG)]
        cb_mm = sem("cb_mm")
        cb_out = sem("cb_out")
        d_done = sem("d_done")
        e_done = sem("e_done")
        ex_done = sem("ex_done")
        cs_done = sem("cs_done")
        m_done = sem("m_done")
        head_mm = sem("head_mm")
        y_done = sem("y_done")
        g_sq = sem("g_sq")
        g_sum = sem("g_sum")
        g_rms = sem("g_rms")
        g_read = sem("g_read")
        fin_p = sem("fin_p")
        fin_t = sem("fin_t")
        fin_o = sem("fin_o")
        s_out = sem("s_out")

        rows = lambda a: a.rearrange("(k p) n -> p k n", p=P)
        ada_v = [rows(t["ada_w"][i]) for i in range(2)]
        ffi_v = [[rows(t["ffn_in"][i, j]) for j in range(2)] for i in range(2)]
        ffo_v = [[rows(t["ffn_out"][i, j]) for j in range(2)] for i in range(2)]
        hyi_v = rows(t["hy_in_w"][0])
        hyo_v = rows(t["hy_out_w"][0])
        mbi_v = rows(t["mb_in_w"][0])
        mbo_v = rows(t["mb_out_w"][0])
        ds = bass.ds

        OUT_COLS = 11 * P

        def ada_multiply(dve, own, slot_free, r_slot, uses, av):
            dve.wait_ge(raw_in[r_slot], uses * 16)
            if slot_free is not None:
                dve.wait_ge(ada_used, slot_free)
            for k in range(DT):
                x = raw[r_slot][:, k * 256:k * 256 + 256]
                for c in range(2):
                    dst, w = av[:, c * L:c * L + L], sc[:, k, c:c + 1]
                    ins = dve.tensor_scalar(dst, x, w, None, ALU.mult) if k == 0 else \
                        dve.scalar_tensor_tensor(dst, x, w, dst, ALU.mult, ALU.add)
                    if k < DT - 1:
                        own.mark(ins)
                if k < DT - 1:
                    own.sync()
            ins.then_inc(ada_dve, 1)

        block = ctx.enter_context(nc.Block())

        @block.sync
        def _(sp):
            def load(r, src, k, n):
                slot = r % 2
                dst = raw[slot][:, 0:k * n].rearrange("p (k n) -> p k n", n=n)
                sp.dma_start(dst, src).then_inc(raw_in[slot], 16)

            def ada_free(count):
                sp.wait_ge(ada_dve, count)

            def begin(pl):
                if pl.w:
                    sp.wait_ge(w_lo, pl.w)
                if pl.v:
                    ada_free(pl.v)

            def stream(pl, count, src, k, n, ada=None):
                begin(pl)
                if ada is not None:
                    load(pl.raw, src(0, 0), k, n)

                def pair(i, last):
                    for u in range(2):
                        j = i * 2 + u
                        if ada is None:
                            sp.wait_ge(w_lo, pl.w - 1 + j)
                            load(pl.raw + u, src(i, u), k, n)
                        else:
                            if not (last and u == 1):
                                sp.wait_ge(w_lo, pl.w + j + 1)
                                load(pl.raw, src(i, 1) if u == 0 else src(i + 1, 0), k, n)
                            ada_free(pl.v + j)
                            load(pl.raw + 1, ada(j), 8, 256)
                if ada is None:
                    with sp.Fori(0, count // 2) as i:
                        pair(i, False)
                else:
                    steps(sp, count // 2, pair)

            def wide(view, col0=0):
                return lambda i, u: view[:, :, ds(i * 512 + (col0 + u * 256), 256)]

            def ffn_in_src(view):
                return lambda i, u: view[:, :, ds(i * 256 + u * FFN, 256)]

            def ffn_out_stream(pl, view):
                stream(pl, 2 * DT, lambda m, half: view[:, half * 11:half * 11 + 11, ds(m * P, P)], 11, P)

            def ada_src(layer, first):
                return lambda j: ada_v[layer][:, :, ds(j * 256 + first * 256, 256)]

            sp.dma_start(small[:], t["c_small"]).then_inc(s_cst, 16)
            load(0, t["c_dft1"].rearrange("p (k n) -> p k n", n=256), 8, 256)
            load(1, t["c_dft2"].rearrange("p (k n) -> p k n", n=256), 1, 256)
            sp.dma_start(xstage[:, 0:2, :], t["x"][0].rearrange("(a p) d -> p a d", p=P)).then_inc(s_x, 16)
            sp.dma_start(xstage[:, 2:4, :], t["ctx"][0].rearrange("(a p) d -> p a d", p=P)).then_inc(s_x, 16)
            for i in range(FIRST_ADA):
                if i < 2:
                    sp.wait_ge(w_lo, i + 1)
                else:
                    sp.wait_ge(ada_used, i - 1) if i % 2 else sp.wait_ge(ada_dve, i // 2)
                c = i if i < 12 else 22 + i
                load(2 + i, ada_v[0][:, :, c * 256:c * 256 + 256], 8, 256)

            stream(ffn_in["00"], FT, ffn_in_src(ffi_v[0][0]), 8, 256, ada_src(0, 12))
            ffn_out_stream(ffn_out["00"], ffo_v[0][0])

            stream(HYIN, 12, wide(hyi_v), 8, 256)
            begin(HYDFT)
            load(HYDFT.raw, t["c_dft1"].rearrange("p (k n) -> p k n", n=256), 8, 256)
            ada = ada_src(1, 0)
            load(HYDFT.raw + 1, ada(0), 8, 256)
            sp.wait_ge(w_lo, HYDFT.w + 1)
            load(HYDFT.raw + 2, ada(1), 8, 256)
            with sp.Fori(0, HYENA_ADA // 2 - 1) as i:
                for u in range(2):
                    sp.wait_ge(ada_used, i * 2 + (HYDFT.a + u + 1))
                    load(HYDFT.raw + 1 + u, ada(i * 2 + (u + 2)), 8, 256)
            begin(HYOUT)
            sp.wait_ge(ada_used, HYDFT.a + HYENA_ADA)
            for j in range(4):
                if j >= 2:
                    sp.wait_ge(w_lo, HYOUT.w - 1 + j)
                load(HYOUT.raw + j, hyo_v[:, :, j * 256:j * 256 + 256], 8, 256)

            stream(ffn_in["01"], FT, ffn_in_src(ffi_v[0][1]), 8, 256, ada_src(1, HYENA_ADA))
            ffn_out_stream(ffn_out["01"], ffo_v[0][1])

            stream(ffn_in["10"], FT, ffn_in_src(ffi_v[1][0]), 8, 256)
            ffn_out_stream(ffn_out["10"], ffo_v[1][0])

            stream(XB, 12, wide(mbi_v, INNER), 8, 256)
            begin(DTP)
            load(DTP.raw, mbi_v[:, :, MB_IN - P:MB_IN], 8, P)
            stream(CP, 4, wide(mbi_v, INNER + 3072), 8, 256)
            stream(ZP, 8, wide(mbi_v, 0), 8, 256)

            sp.wait_ge(af_st, 32)
            sp.wait_ge(st_out, GROUPS)
            for r in range(HPG):
                sp.dma_start(afb[r][:], afscr[r].partition_broadcast(P)).then_inc(afb_in[r], 16)
            with sp.Fori(0, GROUPS - 1) as g:
                for r in range(HPG):
                    sp.wait_ge(d_done, g * HPG + r + 1)
                    sp.wait_ge(e_done, g * HPG + r + 1)
                    sp.dma_start(afb[r][:], afscr[g * HPG + HPG + r].partition_broadcast(P)).then_inc(afb_in[r], 16)

            begin(MBOUT)
            with sp.Fori(0, DT // 2) as i:
                for u in range(2):
                    sp.wait_ge(w_lo, MBOUT.w - 1 + i * 2 + u)
                    load(MBOUT.raw + u, mbo_v[:, :, ds(i * 256 + u * P, P)], 16, P)

            stream(ffn_in["11"], FT, ffn_in_src(ffi_v[1][1]), 8, 256)
            ffn_out_stream(ffn_out["11"], ffo_v[1][1])

            sp.wait_ge(fin_o, DT)
            sp.dma_start(out[0].rearrange("(a p) d -> p a d", p=P), ost[:]).then_inc(s_out, 16)
            sp.wait_ge(s_out, 16)
            sp.wait_ge(spec_st, 64)
            sp.wait_ge(af_st, 32)

        @block.scalar
        def _(act):
            own = Chain(act, act_own)

            def split_hi(n, cols, r_slot, r_uses, w_free):
                act.wait_ge(raw_in[r_slot], r_uses * 16)
                if w_free is not None:
                    act.wait_ge(w_used, w_free)
                return act.activation(wh[n % 2][:, 0:cols], raw[r_slot][:, 0:cols], ACT.Copy).then_inc(w_hi, 1)

            def next_hi(pl, ada, i, u, per, cols=CW, ahead=1):
                j = i * per + (u + ahead)
                r = pl.raw + (2 * (u + ahead) if ada else u + ahead)
                rr = per * (2 if ada else 1) // 2
                split_hi((pl.w + u + ahead) % 2, cols, r % 2, i * rr + (r // 2 + 1), pl.w - 1 + j)

            def hi_tile(q, uses, dst, src=None):
                act.wait_ge(p_ready, uses)
                act.activation(dst, src if src is not None else pp[q % 2][:, :], ACT.Copy).then_inc(p_hi, 1)

            def norm(key, n=NT):
                pl = norms[key]
                act.wait_ge(nsum, pl.norm + 1)
                act.activation(rs[:, 0:n], bank[0][:, 0:n], ACT.Sqrt, bias=eps[:, 0:1],
                               scale=1.0 / D).then_inc(rms_done, 1)

            def norm_hi(key, n=NT):
                pl = norms[key]
                for k in range(DT):
                    hi_tile(pl.q + k, pl.q + k + 1, xh[:, k, 0:n], pp[(pl.q + k) % 2][:, 0:n])

            def ffn(key, ada, after, n=NT):
                norm(key, n)
                norm_hi(key, n)
                if key == "00":
                    act.wait_ge(spec_st, 64)
                pi, po = ffn_in[key], ffn_out[key]
                next_hi(pi, ada, 0, 0, 2)

                def pair(i, last):
                    act.wait_ge(w_used, i * 2 + (pi.w + 1))
                    act.wait_ge(p_ready, i * 2 + pi.q)
                    for u in range(2):
                        act.activation(tt[u][:, 0:n], bank[u][:, 0:n], ACT.Silu).then_inc(gate_ready, 1)
                    if last:
                        split_hi(po.w, OUT_COLS, po.raw % 2, po.raw // 2 + 1, po.w - 1)
                    else:
                        next_hi(pi, ada, i, 0, 2, ahead=2)
                        next_hi(pi, ada, i, 0, 2, ahead=3)
                    for u in range(2):
                        hi_tile(pi.q + u, i * 2 + (pi.q + u + 1), gh[:, i * 2 + u, 0:n], pp[(pi.q + u) % 2][:, 0:n])

                steps(act, FT // 2, pair)
                act.wait_ge(p_ready, pi.q + FT)

                def mpair(i, last):
                    for um in range(2):
                        for half in range(2):
                            u = um * 2 + half
                            if last and u == 3:
                                if after is not None:
                                    split_hi(after.w, CW, after.raw % 2, after.raw // 2 + 1, after.w - 1)
                            else:
                                next_hi(po, False, i, u, 4, OUT_COLS)
                        square(po, i, um, n)

                steps(act, DT // 2, mpair)

            def square(pl, i, um, n):
                act.wait_ge(h_done, i * 2 + (pl.h + um + 1))
                act.wait_ge(acc_done, i * 2 + (pl.h + um - 1))
                act.activation(tt[um][:, 0:n], hT[:, i * 2 + um, 0:n], ACT.Square).then_inc(sq_done, 1)

            stage = tt[0][:, :].rearrange("p (a c) -> p a c", c=P)
            for name, row, k, r in vec_pieces():
                v = t[name]
                if len(v.shape) > 1:
                    v = v.rearrange({2: "a b -> (a b)", 3: "a b c -> (a b c)"}[len(v.shape)])
                v = v.rearrange("(r c) -> r c", c=P)
                act.dma_start(stage[r % P:r % P + k, r // P, :], v[row:row + k, :]).then_inc(s_vec, 16)
            act.dma_start(hsm[0:33, 0, :], t["c_z"]).then_inc(s_fil, 16)
            act.dma_start(hsm[0:33, 1, 0:64], t["hy_pos_w1"][0]).then_inc(s_fil, 16)
            act.dma_start(hsm[:, 1, 64:128], t["hy_pos_w2"][0]).then_inc(s_fil, 16)
            for n, name in enumerate(("hy_pos_b1", "hy_freq", "hy_pos_b2")):
                act.dma_start(hsm[:, 1, 128 + n:129 + n], t[name][0].rearrange("(p o) -> p o", o=1)).then_inc(s_fil, 16)
            act.dma_start(w3[:], t["hy_pos_w3"][0]).then_inc(s_fil, 16)
            act.dma_start(decay[:], t["c_decay"].rearrange("p (a n) -> p a n", a=2)).then_inc(s_fil, 16)
            act.dma_start(par[64:128, 0:1], t["mb_dt_bias"][0].rearrange("d (h o) -> (d h) o", o=1)).then_inc(s_par, 16)
            act.dma_start(par[64:128, 1:2], t["mb_A_log"][0].rearrange("d (h o) -> (d h) o", o=1)).then_inc(s_par, 16)
            dv = t["mb_D"][0].rearrange("(m a) -> a m", a=2)
            with nc.allow_non_contiguous_dma(reason="32 scalars spread over partitions"):
                for a in range(2):
                    act.dma_start(dcol[64 * a:64 * a + 64, :], dv[a].partition_broadcast(64)).then_inc(s_par, 16)

            split_hi(0, CW, 0, 1, None)
            split_hi(1, 256, 1, 1, None)
            act.wait_ge(vec_out, 1)
            own.mark(act.activation(sc[:, :, 0], vecs[:, V_C:V_C + DT], ACT.Silu))
            act.activation(sc[:, :, 1], vecs[:, V_CCTX:V_CCTX + DT], ACT.Silu).then_inc(sc_done, 1)
            own.sync()
            act.activation(tt[3][:, 0:1], small[:, 0:1], ACT.Silu).then_inc(gate_ready, 1)
            act.activation(tt[3][:, 1:2], small[:, 0:1], ACT.Copy).then_inc(z_free, 3)
            act.activation(tt[3][:, 10:11], small[:, 0:1], ACT.Copy).then_inc(cv_silu, 2)
            for layer in range(2):
                act.wait_ge(hid_arg, layer + 1)
                act.activation(hsm[:, 3 + layer, :], hsm[:, 2, :], ACT.Sin).then_inc(hid_sin, 1)
            for m in range(DT):
                act.wait_ge(h_done, m + 1)
                if m >= 2:
                    act.wait_ge(acc_done, m - 1)
                act.activation(tt[m % 2][:], hT[:, m, :], ACT.Square).then_inc(sq_done, 1)
            for unit in range(4):
                o_, hh = unit // 2, unit % 2
                if unit:
                    act.wait_ge(spec_mm, 5 * unit)
                for n in range(4):
                    q = unit * 4 + n
                    hi_tile(q, q + 1, feh[:, n % 2, n // 2, :])
                for kt in range(5):
                    x = unit * 5 + kt
                    act.wait_ge(spec_mm, x + 1)
                    act.activation(ksb[:, unit, kt, :], bank[4 + x % 2][:], ACT.Identity,
                                   scale=mask0 if kt == 2 else 1.0).then_inc(spec_out, 1)
                act.wait_ge(spec_out, 5 * unit + 5)
                act.dma_start(kscr[:, unit], ksb[:, unit]).then_inc(spec_st, 16)
            pl = ffn_in["00"]
            split_hi(pl.w, CW, pl.raw % 2, pl.raw // 2 + 1, pl.w - 1)

            ffn("00", True, HYIN)
            norm("hy")
            norm_hi("hy")
            act.dma_start(ksb[:], kscr).then_inc(spec_ld, 16)

            def hy_in_pair(i, last):
                for u in range(2):
                    if last and u == 1:
                        split_hi(HYDFT.w, CW, HYDFT.raw % 2, HYDFT.raw // 2 + 1, HYDFT.w - 1)
                    else:
                        next_hi(HYIN, False, i, u, 2)
                    act.wait_ge(w_used, i * 2 + (HYIN.w + u + 1))
                    for s in range(2):
                        m = i * 4 + (u * 2 + s)
                        act.wait_ge(hy_ready, m + 1)
                        act.activation(tt[s][:], bank[2 * u + s][:], ACT.Identity,
                                       bias=vecs[:, ds(m + V_HY_IN_B, 1)]).then_inc(z_free, 1)
            steps(act, 6, hy_in_pair)

            for conv in range(2):
                for b in range(8):
                    act.wait_ge(vt_t, conv * 8 + b + 1)
                    act.activation(xh[:, b, :], bank[4 + b % 2][:], ACT.Copy).then_inc(vt_hi, 1)
                for unit in range(4):
                    x = conv * 4 + unit
                    if x:
                        act.wait_ge(inv_mm, 2 * x)
                    for n in range(4):
                        q = HYDFT.q + x * 4 + n
                        hi_tile(q, q + 1, wh[1][:, n * 512:n * 512 + 512])
            for k in range(DT):
                hi_tile(HYY.q + k, HYY.q + k + 1, xh[:, k, :])
            for j in range(4):
                r = HYOUT.raw + j
                split_hi(HYOUT.w + j, CW, r % 2, r // 2 + 1, HYOUT.w if j == 0 else HYOUT.w + j - 1)
                if j:
                    for um in range(2):
                        square(HYOUT, j - 1, um, NT)
            for um in range(2):
                square(HYOUT, 3, um, NT)
            pl = ffn_in["01"]
            split_hi(pl.w, CW, pl.raw % 2, pl.raw // 2 + 1, pl.w - 1)
            ffn("01", True, ffn_in["10"])

            ffn("10", False, XB)
            norm("mb")
            norm_hi("mb")

            def conv_chunk(pl, i, u, count, split, dst, n):
                split()
                act.wait_ge(w_used, i * 2 + (pl.w + u + 1))
                first = pl.conv - 3
                for s in range(2):
                    m = i * 4 + (u * 2 + s)
                    act.wait_ge(cv_silu, m + (first + 1))
                    act.activation(tt[2 + s][:, 0:n], bank[2 * u + s][:, 0:n], ACT.Identity,
                                   bias=vecs[:, ds(m + (V_MB_CB + first), 1)],
                                   scale=vecs[:, ds(m + (V_MB_CW + CONVT + first), 1)]).then_inc(cv_in, 1)
                for s in range(2):
                    m = i * 4 + (u * 2 + s)
                    act.wait_ge(conv_free, m + (pl.conv + 1))
                    act.activation(dst(m), tt[2 + s][:, 0:n] if n == L else
                                   tt[2 + s][:].rearrange("p (a n) -> p a n", a=2), ACT.Silu).then_inc(cv_silu, 1)

            def xb_pair(i, last):
                for u in range(2):
                    split = lambda: (split_hi(DTP.w, 8 * P, DTP.raw % 2, DTP.raw // 2 + 1, DTP.w - 1)
                                     if last and u == 1 else next_hi(XB, False, i, u, 2))
                    conv_chunk(XB, i, u, 12, split, lambda m: xb[:, :, m, :], NT)
            steps(act, 6, xb_pair)

            split_hi(CP.w, CW, CP.raw % 2, CP.raw // 2 + 1, CP.w - 1)
            act.wait_ge(s_par, 64)
            act.wait_ge(dt_v, 1)
            act.activation(tt[1][64:128, :], tt[0][64:128, :], ACT.Exp, scale=-1.0).then_inc(dt_e, 1)
            act.activation(par[64:128, 2:3], par[64:128, 1:2], ACT.Exp).then_inc(dt_e, 1)

            def c_pair(i, last):
                for u in range(2):
                    split = lambda: (split_hi(ZP.w, CW, ZP.raw % 2, ZP.raw // 2 + 1, ZP.w - 1)
                                     if last and u == 1 else next_hi(CP, False, i, u, 2))
                    conv_chunk(CP, i, u, 4, split, lambda m: csb[:, m, :], L)
            steps(act, 2, c_pair)

            def z_pair(i, last):
                for u in range(2):
                    if not (last and u == 1):
                        next_hi(ZP, False, i, u, 2)
                    act.wait_ge(w_used, i * 2 + (ZP.w + u + 1))
                    for s in range(2):
                        act.activation(zsb[:, i * 4 + (u * 2 + s), :], bank[2 * u + s][:, 0:L],
                                       ACT.Silu).then_inc(z_free, 1)
            steps(act, 4, z_pair)

            act.wait_ge(dt_v, 2)
            act.activation(dts[64:128, 4, :], dts[64:128, 3, :], ACT.Exp).then_inc(dt_e, 1)
            act.wait_ge(dt_v, 3)
            for d in range(2):
                act.dma_start(afscr[:, d, :], dts[64 + 32 * d:96 + 32 * d, 5, :]).then_inc(af_st, 16)
            for b in range(4):
                act.wait_ge(tb_mm, b + 1)
                act.activation(btok[:, b // 2, (b % 2) * 512:(b % 2) * 512 + 512], bank[6 + b % 2][:],
                               ACT.Copy).then_inc(tb_out, 1)
            for g in range(GROUPS):
                act.wait_ge(st_mm, g + 1)
                act.activation(ssb[:, :, g * 256:g * 256 + 256], bank[4 + g % 2][:].rearrange("p (a n) -> p a n", a=2),
                               ACT.Copy).then_inc(st_out, 1)
            act.wait_ge(st_mm, GROUPS)
            act.dma_start(mask[:].rearrange("p a n -> p (a n)"), t["c_mask"]).then_inc(s_mask, 16)

            def group(i, u, first, finish, last):
                for r in range(HPG):
                    b = r % 2
                    h1 = i * 8 + (u * HPG + r + 1)
                    act.wait_ge(afb_in[r], i * 32 + (u * 16 + 16))
                    if not first:
                        act.wait_ge(head_mm, h1 - 4)
                    act.activation(csx[r][:], afb[r][:].rearrange("p a n -> p (a n)"), ACT.Exp).then_inc(ex_done, 1)
                    if not first:
                        act.wait_ge(m_done, h1 - 4)
                    act.activation(ee[r][:, P:2 * P], afb[r][:, 0, P:L], ACT.Exp, bias=tk[:, 0, ds(h1 - 1, 1)])
                    act.activation(ee[r][:, 2 * P:3 * P], afb[r][:, 1, 0:P], ACT.Exp,
                                   bias=tk[:, 1, ds(h1 + (HEADS - 1), 1)])
                    act.wait_ge(d_done, h1)
                    act.activation(ee[r][:].rearrange("p (a n) -> p a n", n=P)[:, 0:4:3, :],
                                   dm[b][:].rearrange("p (a n) -> p a n", n=P), ACT.Exp).then_inc(e_done, 1)

            core_groups(act, group, lambda: None)

            for g in range(GROUPS + 1):
                if g < GROUPS:
                    act.wait_ge(y_done, GROUPS)
                    if g >= 2:
                        act.wait_ge(g_sum, g - 1)
                    act.activation(tt[g % 2][:], zsb[:, 2 * g:2 * g + 2, :].rearrange("p a n -> p (a n)"),
                                   ACT.Square).then_inc(g_sq, 1)
                if g:
                    act.wait_ge(g_sum, g)
                    if g >= 2:
                        act.wait_ge(g_read, g - 1)
                    act.activation(rs[:, 0:L], bank[6 + (g - 1) % 2][:, 0:L], ACT.Sqrt, bias=eps[:, 0:1],
                                   scale=1.0 / 256).then_inc(g_rms, 1)
                    hi_tile(MBN.q + g - 1, MBN.q + g, ynh[:, 2 * g - 2:2 * g, :].rearrange("p a n -> p (a n)"))

            split_hi(MBOUT.w, CW, MBOUT.raw % 2, MBOUT.raw // 2 + 1, MBOUT.w)

            def mb_pair(i, last):
                for um in range(2):
                    if last and um == 1:
                        pl = ffn_in["11"]
                        split_hi(pl.w, CW, pl.raw % 2, pl.raw // 2 + 1, pl.w - 1)
                    else:
                        next_hi(MBOUT, False, i, um, 2)
                    square(MBOUT, i, um, L)
            steps(act, DT // 2, mb_pair)
            ffn("11", False, None, L)
            norm("fin", L)
            for k in range(DT):
                act.wait_ge(fin_t, k + 1)
                act.activation(ost[:, :, k * P:k * P + P], bank[k % 4][:, 0:L].rearrange("p (a n) -> p a n", a=2),
                               ACT.Copy).then_inc(fin_o, 1)

        @block.vector
        def _(dve):
            own = Chain(dve, dve_own)

            def split_lo(n_slot, count, cols, r_slot):
                dve.wait_ge(w_hi, count)
                dve.tensor_tensor(wl[n_slot][:, 0:cols], raw[r_slot][:, 0:cols],
                                  wh[n_slot][:, 0:cols].bitcast(F32), ALU.subtract).then_inc(w_lo, 1)

            def next_lo(pl, ada, i, u, per, cols=CW):
                r = pl.raw + (2 * (u + 1) if ada else u + 1)
                split_lo((pl.w + u + 1) % 2, i * per + (pl.w + u + 2), cols, r % 2)

            def open_lo(pl, cols=CW):
                split_lo(pl.w % 2, pl.w + 1, cols, pl.raw % 2)

            def pp_free(q):
                if not isinstance(q, int) or q >= 2:
                    dve.wait_ge(p_lo, q - 1)

            def norm(key, layer, k0, n=NT):
                pl = norms[key]
                m = mods[layer]
                dve.wait_ge(rms_done, pl.norm + 1)
                own(dve.reciprocal(rs[:, 0:n], rs[:, 0:n]))
                for k in range(DT):
                    q = pl.q + k
                    p = pp[q % 2]
                    pp_free(q)
                    own(dve.tensor_tensor(p[:, 0:n], hT[:, k, 0:n], rs[:, 0:n], ALU.mult))
                    sh, s1 = DT * k0 + k, DT * (k0 + 1) + k
                    for w in range(n // L):
                        ins = dve.tensor_scalar(p[:, w * L:w * L + L], p[:, w * L:w * L + L], m[:, s1, w:w + 1],
                                                m[:, sh, w:w + 1], ALU.mult, ALU.add)
                    ins.then_inc(p_ready, 1)

            def residual(pl, layer, k5, i, um, n, chunk_done):
                dve.wait_ge(w_used, chunk_done)
                for w in range(n // L):
                    x = hT[:, i * 2 + um, w * L:w * L + L]
                    ins = dve.scalar_tensor_tensor(x, bank[4 + um][:, w * L:w * L + L],
                                                   mods[layer][:, i * 2 + (DT * k5 + um), w:w + 1], x,
                                                   ALU.mult, ALU.add)
                ins.then_inc(h_done, 1)

            def ffn(key, layer, k0, ada, after, n=NT):
                norm(key, layer, k0, n)
                pi, po = ffn_in[key], ffn_out[key]

                def weigh(i, u):
                    if ada:
                        ada_multiply(dve, own, i * 2 + (pi.a + u - 1), (pi.raw + 1) % 2,
                                     i * 2 + ((pi.raw + 2 * u + 1) // 2 + 1), tt[2 + u])

                def pair(i, last):
                    next_lo(pi, ada, i, 0, 2)
                    weigh(i, 0)
                    if last:
                        weigh(i, 1)
                        open_lo(po, OUT_COLS)
                    else:
                        next_lo(pi, ada, i, 1, 2)
                        weigh(i, 1)
                    dve.wait_ge(w_used, i * 2 + (pi.w + 2))
                    for u in range(2):
                        dve.wait_ge(gate_ready, i * 2 + (pi.gate + u + 1))
                        pp_free(i * 2 + (pi.q + u))
                        dve.tensor_tensor(pp[(pi.q + u) % 2][:, 0:n], tt[u][:, 0:n], bank[2 + u][:, 0:n],
                                          ALU.mult).then_inc(p_ready, 1)
                steps(dve, FT // 2, pair, own, 4 * (DT - 1) if ada else 0)

                def mpair(i, last):
                    for um in range(2):
                        for half in range(2):
                            u = um * 2 + half
                            if last and u == 3:
                                if after is not None:
                                    open_lo(after)
                            else:
                                next_lo(po, False, i, u, 4, OUT_COLS)
                        residual(po, layer, k0 + 2, i, um, n, i * 4 + (po.w + 2 * um + 2))
                steps(dve, DT // 2, mpair)

            def take_mods(layer, used, spans, plus, halve, outs):
                dve.wait_ge(ada_used, used)
                m = mods[layer]
                for a, b in spans:
                    n = b - a
                    own.mark(dve.tensor_tensor(
                        m[:, a:b, :], bank[6 + layer][:, 2 * a:2 * b].rearrange("p (m c) -> p m c", c=2),
                        vecs[:, V_ADA + MODT * layer + a:V_ADA + MODT * layer + b].unsqueeze(2).to_broadcast([P, n, 2]),
                        ALU.add))
                own.sync()
                for idx in plus:
                    x = m[:, DT * idx:DT * idx + DT, :]
                    own.mark(dve.tensor_scalar(x, x, 1.0, None, ALU.add))
                for idx in halve:
                    x = m[:, DT * idx:DT * idx + DT, :]
                    dve.tensor_scalar(x, x, 0.5, None, ALU.mult).then_inc(ada_out, 1)
                own.sync()
                dve.wait_ge(ada_out, outs)

            own.mark(dve.memset(tt[3][:, 2:8], 0.0))
            dve.memset(ones[:], 1.0).then_inc(s_set, 1)
            dve.memset(eps[:], EPS).then_inc(s_set, 1)
            dve.memset(tt[3][:, 8:9], 0.0).then_inc(conv_free, 3)
            dve.memset(tt[3][:, 9:10], 0.0).then_inc(hy_ready, 2)
            own.sync()
            split_lo(0, 1, CW, 0)
            split_lo(1, 2, 256, 1)
            dve.wait_ge(vec_t, 1)
            dve.tensor_copy(vecs[:], bank[7][:, 0:V_ALL]).then_inc(vec_out, 1)
            for m in range(DT):
                dve.wait_ge(x_t, m + 1)
                dve.tensor_copy(hT[:, m, :], bank[m % 4][:]).then_inc(h_done, 1)
            dve.wait_ge(s_fil, 16 * 8)

            def early_ada(a):
                ada_multiply(dve, own, a - 3 if a >= 4 else None, 0, a // 2 + 2, early_av[a // 2 % 2])
            for layer in range(2):
                arg, cyc, red = hsm[:, 5, :], hsm[:, 6, :], hsm[:, 2, :]
                dve.wait_ge(hid_mm, layer + 1)
                b = hsm[:, 1, 128 + 2 * layer:129 + 2 * layer]
                if layer:
                    dve.wait_ge(hid_sin, 1)
                own(dve.tensor_scalar(arg, bank[7][0:64, 0:L], b, hsm[:, 1, 129:130], ALU.add, ALU.mult))
                own(dve.tensor_scalar(cyc, arg, 0.15915494309189535, ROUND, ALU.mult, ALU.add))
                own(dve.tensor_scalar(cyc, cyc, ROUND, None, ALU.subtract))
                for part in TWO_PI:
                    own(dve.scalar_tensor_tensor(arg, cyc, -part, arg, ALU.mult, ALU.add))
                dve.tensor_scalar(red, arg, PI_DOWN, -PI_DOWN, ALU.min, ALU.max).then_inc(hid_arg, 1)
                if layer == 0:
                    dve.wait_ge(sc_done, 1)
                early_ada(2 * layer)
            for unit in range(4):
                o_, hh = unit // 2, unit % 2
                cols = slice(hh * 512, hh * 512 + 512)
                for n in range(2):
                    dve.wait_ge(fil_mm, unit * 2 + n + 1)
                    if unit or n:
                        dve.wait_ge(p_ready, unit * 4 + n * 2)
                    own.mark(dve.tensor_tensor(tt[2][:], bank[n][:], decay[:, n, cols], ALU.mult))
                    own.mark(dve.scalar_tensor_tensor(tt[3][:], bank[2 + n][:], mask0 if n == 0 else 1.0,
                                                      decay[:, n, cols], ALU.mult, ALU.mult))
                    own.sync()
                    for w in range(2):
                        q = unit * 4 + n * 2 + w
                        pp_free(q)
                        ins = dve.tensor_tensor(pp[q % 2][:], tt[2][:], tt[3][:], ALU.subtract if w else ALU.add)
                        ins.then_inc(p_ready, 1)
                early_ada(4 + unit * 2)
            early_ada(12)
            take_mods(0, FIRST_ADA, [(0, 24), (68, 72)], (1,), (2,), 1)
            open_lo(ffn_in["00"])

            ffn("00", 0, 0, True, HYIN)
            take_mods(0, FIRST_ADA + 22, [(24, 68)], (4, 7), (8,), 2)
            norm("hy", 0, 3)

            def hy_in_pair(i, last):
                for u in range(2):
                    if last and u == 1:
                        open_lo(HYDFT)
                    else:
                        next_lo(HYIN, False, i, u, 2)
                    for s in range(2):
                        m = i * 4 + (u * 2 + s)
                        src = tt[s][:].rearrange("p (a n) -> p a n", a=2)
                        dst = hyu[:, m, :].rearrange("p (a n) -> p a n", a=2)
                        tap = lambda w: vecs[:, ds(m + (V_HY_CW + 24 * w), 1)]
                        dve.wait_ge(z_free, m + (HYIN.zf + 1))
                        own(dve.tensor_scalar(hyu[:, m, :], tt[s][:], tap(1), vecs[:, ds(m + V_HY_CB, 1)],
                                              ALU.mult, ALU.add))
                        own(dve.scalar_tensor_tensor(dst[:, :, 1:L], src[:, :, 0:L - 1], tap(0), dst[:, :, 1:L],
                                                     ALU.mult, ALU.add))
                        dve.scalar_tensor_tensor(dst[:, :, 0:L - 1], src[:, :, 1:L], tap(2), dst[:, :, 0:L - 1],
                                                 ALU.mult, ALU.add).then_inc(hy_ready, 1)
            dve.wait_ge(w_used, HYIN.w)
            steps(dve, 6, hy_in_pair, own, 8)

            dve.wait_ge(spec_ld, 16)
            for conv in range(2):
                for b in range(8):
                    dve.wait_ge(vt_hi, conv * 8 + b + 1)
                    dve.tensor_tensor(xl[:, b, :], bank[4 + b % 2][:], xh[:, b, :].bitcast(F32),
                                      ALU.subtract).then_inc(vt_lo, 1)
                for unit in range(5):
                    x = conv * 4 + unit
                    if unit < 4:
                        for n in range(4):
                            ft = n % 2
                            a, b_ = (ft, 2 + ft) if n < 2 else (2 + ft, 4 if ft == 0 else ft)
                            dve.wait_ge(fwd_mm, x + 1)
                            c0 = x * 4 + n
                            if c0 >= 2:
                                dve.wait_ge(p_ready, HYDFT.q + c0 - 1)
                            w0, w1 = tt[2 * (n % 2)], tt[2 * (n % 2) + 1]
                            own.mark(dve.tensor_tensor(w0[:], bank[ft][:], ksb[:, 2 * conv + unit % 2, a, :], ALU.mult))
                            dve.tensor_tensor(w1[:], bank[2 + ft][:], ksb[:, 2 * conv + unit % 2, b_, :],
                                              ALU.mult).then_inc(cm_mul, 1)
                    if unit:
                        u = unit - 1
                        y = conv * 4 + u
                        seg, half = u // 2, u % 2
                        for c in range(4):
                            ch = half * 4 + c
                            tok = slice(seg * L, seg * L + L)
                            src = hyu[:, (16 if conv == 0 else 0) + ch, tok]
                            if c % 2 == 0:
                                dve.wait_ge(inv_mm, 2 * y + c // 2 + 1)
                            own(dve.scalar_tensor_tensor(src, src, vecs[:, V_HY_BIAS + 8 * conv + ch:V_HY_BIAS + 8 * conv + ch + 1],
                                                         bank[4 + c // 2][:, (c % 2) * L:(c % 2) * L + L], ALU.mult, ALU.add))
                            dst = hyu[:, (0 if conv == 0 else 8) + ch, tok]
                            dve.tensor_tensor(dst, dst, src, ALU.mult).then_inc(inv_out, 1)
                dve.wait_ge(inv_out, 16 * (conv + 1))
            for k in range(DT):
                pp_free(HYY.q + k)
                dve.tensor_copy(pp[(HYY.q + k) % 2][:], hyu[:, 8 + k, :]).then_inc(p_ready, 1)
            for j in range(5):
                if j < 4:
                    split_lo((HYOUT.w + j) % 2, HYOUT.w + j + 1, CW, (HYOUT.raw + j) % 2)
                if j:
                    for um in range(2):
                        m = (j - 1) * 2 + um
                        dve.wait_ge(w_used, HYOUT.w + j)
                        for w in range(2):
                            own.mark(dve.tensor_scalar(
                                tt[2 + um][:, w * L:w * L + L], bank[4 + um][:, w * L:w * L + L],
                                vecs[:, V_HY_OUT_B + m:V_HY_OUT_B + m + 1], mods[0][:, 5 * DT + m, w:w + 1],
                                ALU.add, ALU.mult))
                        own.sync()
                        dve.tensor_tensor(hT[:, m, :], hT[:, m, :], tt[2 + um][:], ALU.add).then_inc(h_done, 1)
            open_lo(ffn_in["01"])
            ffn("01", 0, 6, True, ffn_in["10"])

            take_mods(1, 72, [(0, 72)], (1, 4, 7), (2, 8), 4)
            ffn("10", 1, 0, False, XB)
            norm("mb", 1, 3)

            def taps(pl, i, u, s, n):
                m = i * 4 + (u * 2 + s)
                first = pl.conv - 3
                src = bank[2 * u + s][:, 0:n].rearrange("p (a n) -> p a n", n=L)
                dst = tt[2 + s][:, 0:n].rearrange("p (a n) -> p a n", n=L)
                tap = lambda w: vecs[:, ds(m + (V_MB_CW + CONVT * w + first), 1)]
                dve.wait_ge(cv_in, m + (first + 1))
                own(dve.scalar_tensor_tensor(dst[:, :, 1:L], src[:, :, 0:L - 1], tap(0), dst[:, :, 1:L],
                                             ALU.mult, ALU.add))
                dve.scalar_tensor_tensor(dst[:, :, 0:L - 1], src[:, :, 1:L], tap(2), dst[:, :, 0:L - 1],
                                         ALU.mult, ALU.add).then_inc(conv_free, 1)

            def xb_pair(i, last):
                for u in range(2):
                    if last and u == 1:
                        open_lo(DTP, 8 * P)
                    else:
                        next_lo(XB, False, i, u, 2)
                    for s in range(2):
                        taps(XB, i, u, s, NT)
            steps(dve, 6, xb_pair, own, 4)

            open_lo(CP)
            hp = slice(64, 128)
            v, av, e, w = pp[0][hp, :], tt[0][hp, :], tt[1][hp, :], rs[hp, :]
            dve.wait_ge(s_par, 64)
            dve.wait_ge(w_used, DTP.w + 1)
            dve.wait_ge(p_lo, MBN.q)
            own(dve.tensor_scalar(v, bank[4][hp, :], par[hp, 0:1], None, ALU.add))
            dve.scalar_tensor_tensor(av, v, -1.0, v, ALU.mult, ALU.max).then_inc(dt_v, 1)
            own(dve.tensor_scalar(v, v, 0.0, None, ALU.max))
            dve.wait_ge(dt_e, 2)
            own(dve.tensor_scalar(w, e, 2.0, None, ALU.add))
            own(dve.reciprocal(w, w))
            z, z2, s_ = tt[0][hp, :], tt[1][hp, :], rs[hp, :]
            own(dve.tensor_tensor(z, e, w, ALU.mult))
            own(dve.tensor_tensor(z2, z, z, ALU.mult))
            own(dve.tensor_scalar(s_, z2, 1.0 / 15, None, ALU.mult))
            for c in (13, 11, 9, 7, 5, 3):
                own(dve.scalar_tensor_tensor(s_, s_, 1.0 / c, z2, ALU.add, ALU.mult))
            own(dve.scalar_tensor_tensor(s_, s_, 1.0, z, ALU.add, ALU.mult))
            dt = pp[1][hp, :]
            own(dve.scalar_tensor_tensor(dt, s_, 2.0, v, ALU.mult, ALU.add))
            da = pp[0][hp, :]
            own(dve.tensor_scalar(da, dt, par[hp, 2:3], -1.0, ALU.mult, ALU.mult))
            own(dve.memset(tt[0][hp, 0:L], 1.0))
            cs = rs[hp, :]
            for seg in range(2):
                own.mark(dve.tensor_tensor_scan(cs[:, seg * L:seg * L + L], tt[0][hp, 0:L],
                                                da[:, seg * L:seg * L + L], 0.0, ALU.mult, ALU.add))
            own.sync()

            def c_pair(i, last):
                for u in range(2):
                    if last and u == 1:
                        open_lo(ZP)
                    else:
                        next_lo(CP, False, i, u, 2)
                    for s in range(2):
                        taps(CP, i, u, s, L)
            steps(dve, 2, c_pair, own, 4)

            def z_pair(i, last):
                for u in range(2):
                    if not (last and u == 1):
                        next_lo(ZP, False, i, u, 2)
            steps(dve, 4, z_pair)

            dve.wait_ge(w_used, ZP.w + 8)
            f, b = slice(64, 96), slice(96, 128)
            lat, cx = slice(0, L), slice(L, NT)
            own.mark(dve.tensor_scalar(dts[f, 0, :], rs[f, lat], -1.0, None, ALU.mult))
            own.mark(dve.scalar_tensor_tensor(dts[b, 0, :], rs[b, lat], rs[b, L - 1:L], pp[0][b, lat],
                                              ALU.subtract, ALU.subtract))
            own.mark(dve.tensor_copy(dts[hp, 1, :], pp[1][hp, lat]))
            own.mark(dve.tensor_scalar(dts[f, 3, :], rs[f, cx], rs[f, NT - 1:NT], -1.0, ALU.subtract, ALU.mult))
            dve.tensor_tensor(dts[b, 3, :], rs[b, cx], pp[0][b, cx], ALU.subtract).then_inc(dt_v, 1)
            own.sync()
            dve.tensor_scalar(dts[hp, 5, :], dts[hp, 0, :], -1.0, None, ALU.mult).then_inc(dt_v, 1)
            dve.wait_ge(dt_e, 3)
            dve.tensor_tensor(dts[hp, 2, :], dts[hp, 4, :], pp[1][hp, cx], ALU.mult).then_inc(dt_v, 1)
            dve.wait_ge(tk_t, 1)
            dve.tensor_copy(tk[:].rearrange("p a n -> p (a n)"), bank[7][:, 0:384]).then_inc(tk_out, 1)
            dve.wait_ge(tk_out, 1)

            def token_major(x0, row):
                for b8 in range(8):
                    T, c = b8 // 4, b8 % 4
                    dve.wait_ge(tr_mm, x0 + b8 + 1)
                    for d in range(2):
                        ins = dve.tensor_tensor(
                            xtok[:, d, T, c * 512:c * 512 + 512].rearrange("p (h w) -> p h w", w=HD),
                            bank[(x0 + b8) % 4][:].rearrange("p (h w) -> p h w", w=HD),
                            tk[:, row + T, 32 * d + 8 * c:32 * d + 8 * c + 8].unsqueeze(2).to_broadcast([P, 8, HD]),
                            ALU.mult)
                    ins.then_inc(tr_out, 1)
            token_major(0, 4)
            dve.wait_ge(st_mm, GROUPS)
            token_major(8, 2)
            dve.wait_ge(s_mask, 16)

            def b_dot_c(g, cb):
                dve.wait_ge(cb_mm, g + 1)
                if not isinstance(g, int) or g > 1:
                    dve.wait_ge(m_done, g * HPG - HPG)
                edges = bank[6][:].rearrange("p (a n) -> p a n", n=P)[:, 0:4:3, :]
                dve.tensor_tensor(cb[:, 0:512].rearrange("p (a n) -> p a n", n=P)[:, 0:4:3, :], edges,
                                  mask[:, 0:2, :], ALU.mult)
                dve.tensor_tensor(cb[:, 512:768].rearrange("p (a n) -> p a n", n=P), edges, mask[:, 1:3, :], ALU.mult)
                dve.tensor_copy(cb[:, P:3 * P], bank[6][:, P:3 * P]).then_inc(cb_out, 1)

            def group(i, u, first, finish, last):
                g = i * 2 + u
                if first:
                    b_dot_c(0, cbx[0])
                for r in range(HPG):
                    if finish and r == 1:
                        gate_y(g, 1 - u)
                    if r == 2 and not last:
                        b_dot_c(g + 1, cbx[1 - u])
                    bf = r % 2
                    h = i * 8 + (u * HPG + r)
                    dve.wait_ge(afb_in[r], i * 32 + (u * 16 + 16))
                    if not (first and r < 2):
                        dve.wait_ge(e_done, h - 1)
                    af, tks, d_ = afb[r], [[tk[:, T, ds(h + 32 * d, 1)] for T in range(2)] for d in range(2)], dm[bf]
                    own.mark(dve.tensor_scalar(d_[:, 0:P], af[:, 0, 0:P], tks[0][0], None, ALU.add))
                    own.mark(dve.tensor_scalar(d_[:, P:2 * P], af[:, 1, P:L], tks[1][1], None, ALU.add))
                    own.sync()
                    own.mark(dve.scalar_tensor_tensor(d_[:, 0:P], af[:, 1, 0:P], tks[1][0], d_[:, 0:P], ALU.add, ALU.min))
                    dve.scalar_tensor_tensor(d_[:, P:2 * P], af[:, 0, P:L], tks[0][1], d_[:, P:2 * P],
                                             ALU.add, ALU.min).then_inc(d_done, 1)
                    dve.wait_ge(ex_done, h + 1)
                    cs = csx[r][:].rearrange("p (d n) -> p d n", d=2)
                    dve.tensor_tensor(cs, cs, csb[:, g, :].unsqueeze(1).to_broadcast([P, 2, L]), ALU.mult).then_inc(cs_done, 1)

            def gate_y(g, odd):
                dve.wait_ge(head_mm, g * HPG)
                if not isinstance(g, int) or g > 1:
                    dve.wait_ge(y_done, g - 1)
                for mt in range(2):
                    m = g * 2 + (mt - 2)
                    own.mark(dve.scalar_tensor_tensor(tt[3][:, mt * L:mt * L + L], xb[:, 0, m, :], dcol[:, ds(m, 1)],
                                                      bank[4 + odd][:, mt * L:mt * L + L], ALU.mult, ALU.add))
                own.sync()
                zz = zsb[:, ds(g * 2 - 2, 2), :]
                dve.tensor_tensor(zz, zz, tt[3][:].rearrange("p (a n) -> p a n", a=2), ALU.mult).then_inc(y_done, 1)

            core_groups(dve, group, lambda: gate_y(GROUPS, 1), own, 2 * (3 * HPG + 2))

            for g in range(GROUPS):
                dve.wait_ge(g_rms, g + 1)
                own(dve.reciprocal(rs[:, 0:L], rs[:, 0:L]))
                q = MBN.q + g
                pp_free(q)
                p = pp[q % 2][:].rearrange("p (a n) -> p a n", a=2)
                ins = dve.tensor_tensor(p, zsb[:, 2 * g:2 * g + 2, :], rs[:, 0:L].unsqueeze(1).to_broadcast([P, 2, L]),
                                        ALU.mult)
                ins.then_inc(g_read, 1)
                dve.wait_ge(g_read, g + 1)
                for mt in range(2):
                    ins = dve.tensor_scalar(p[:, mt, :], p[:, mt, :], vecs[:, V_MB_NORM + 2 * g + mt:V_MB_NORM + 2 * g + mt + 1],
                                            None, ALU.mult)
                ins.then_inc(p_ready, 1)
            open_lo(MBOUT)

            def mb_pair(i, last):
                for um in range(2):
                    if last and um == 1:
                        open_lo(ffn_in["11"])
                    else:
                        next_lo(MBOUT, False, i, um, 2)
                    residual(MBOUT, 1, 5, i, um, L, i * 2 + (MBOUT.w + um + 1))
            steps(dve, DT // 2, mb_pair)
            ffn("11", 1, 6, False, None, L)

            dve.wait_ge(rms_done, norms["fin"].norm + 1)
            own(dve.reciprocal(rs[:, 0:L], rs[:, 0:L]))
            for k in range(DT):
                if k >= 2:
                    dve.wait_ge(fin_t, k - 1)
                own(dve.tensor_tensor(pp[k % 2][:, 0:L], hT[:, k, 0:L], rs[:, 0:L], ALU.mult))
                dve.tensor_scalar(pp[k % 2][:, 0:L], pp[k % 2][:, 0:L], vecs[:, V_FINAL + k:V_FINAL + k + 1], None,
                                  ALU.mult).then_inc(fin_p, 1)

        @block.gpsimd
        def _(pool):
            own = Chain(pool, pool_own)

            def lo_tile(q, uses, dst, hi):
                pool.wait_ge(p_hi, uses)
                n = dst.shape[-1]
                pool.tensor_tensor(dst, pp[q % 2][:, 0:n], hi.bitcast(F32), ALU.subtract).then_inc(p_lo, 1)

            def norm_lo(key, n=NT):
                pl = norms[key]
                for k in range(DT):
                    lo_tile(pl.q + k, pl.q + k + 1, xl[:, k, 0:n], xh[:, k, 0:n])

            def clear(key):
                pool.wait_ge(nsum, norms[key].norm + 1)
                pool.memset(acc[:], 0.0).then_inc(acc_zero, 1)

            def add_square(pl, i, um, n):
                pool.wait_ge(sq_done, i * 2 + (pl.h + um + 1))
                pool.wait_ge(acc_done, i * 2 + (pl.h + um))
                pool.tensor_tensor(acc[:, 0:n], acc[:, 0:n], tt[um][:, 0:n], ALU.add).then_inc(acc_done, 1)

            def add_squares(pl, zeroed, n=NT):
                pool.wait_ge(acc_zero, zeroed)

                if pl.h == 0:
                    for i in range(DT // 2):
                        for um in range(2):
                            pool.wait_ge(sq_done, 2 * i + um + 1)
                            if i or um:
                                pool.wait_ge(acc_done, 2 * i + um)
                            pool.tensor_tensor(acc[:, 0:n], acc[:, 0:n], tt[um][:, 0:n], ALU.add).then_inc(acc_done, 1)
                else:
                    with pool.Fori(0, DT // 2) as i:
                        for um in range(2):
                            add_square(pl, i, um, n)

            def ffn(key, zeroed, n=NT):
                norm_lo(key, n)
                clear(key)
                pi = ffn_in[key]
                with pool.Fori(0, FT // 2) as i:
                    for u in range(2):
                        lo_tile(pi.q + u, i * 2 + (pi.q + u + 1), gl[:, i * 2 + u, 0:n], gh[:, i * 2 + u, 0:n])
                add_squares(ffn_out[key], zeroed, n)

            pool.memset(acc[:], 0.0).then_inc(acc_zero, 1)
            add_squares(P0, 1)
            for unit in range(4):
                for n in range(4):
                    q = unit * 4 + n
                    lo_tile(q, q + 1, fel[:, n % 2, n // 2, :], feh[:, n % 2, n // 2, :])
            ffn("00", 2)
            norm_lo("hy")
            clear("hy")
            for x in range(8):
                for n in range(5):
                    c0 = x * 4 + n
                    q = HYDFT.q + c0
                    if n < 4:
                        pool.wait_ge(cm_mul, c0 + 1)
                        if x or n > 1:
                            pool.wait_ge(p_lo, q - 1)
                        pool.tensor_tensor(pp[q % 2][:], tt[2 * (n % 2)][:], tt[2 * (n % 2) + 1][:],
                                           ALU.subtract if n < 2 else ALU.add).then_inc(p_ready, 1)
                    if n:
                        m = n - 1
                        lo_tile(q - 1, q, wl[1][:, m * 512:m * 512 + 512], wh[1][:, m * 512:m * 512 + 512])
            for k in range(DT):
                lo_tile(HYY.q + k, HYY.q + k + 1, xl[:, k, :], xh[:, k, :])
            add_squares(HYOUT, 3)
            ffn("01", 4)
            ffn("10", 5)
            norm_lo("mb")
            clear("mb")
            pool.wait_ge(s_set, 1)

            def group(i, u, first, finish, last):
                pool.wait_ge(cb_out, i * 2 + (u + 1))
                for r in range(HPG):
                    h = i * 8 + (u * HPG + r)
                    pool.wait_ge(e_done, h + 1)
                    if not (first and r < 2):
                        pool.wait_ge(head_mm, h - 1)
                    pool.tensor_tensor(mm_[r % 2][:, 0:512], ee[r][:], cbx[u][:, 0:512], ALU.mult)
                    pool.tensor_tensor(mm_[r % 2][:, 512:768].rearrange("p (a n) -> p a n", n=P),
                                       ee[r][:].rearrange("p (a n) -> p a n", n=P)[:, 0:4:3, :],
                                       cbx[u][:, 512:768].rearrange("p (a n) -> p a n", n=P), ALU.mult).then_inc(m_done, 1)

            core_groups(pool, group, lambda: None)
            for g in range(GROUPS):
                lo_tile(MBN.q + g, MBN.q + g + 1, ynl[:, 2 * g:2 * g + 2, :].rearrange("p a n -> p (a n)"),
                        ynh[:, 2 * g:2 * g + 2, :].rearrange("p a n -> p (a n)"))
            add_squares(MBOUT, 6, L)
            ffn("11", 7, n=L)

        @block.tensor
        def _(pe):
            def mm3(dst, wslot, lo, x_hi, x_lo, start, stop):
                h, l_ = wh[wslot][:, lo:lo + P], wl[wslot][:, lo:lo + P]
                pe.matmul(dst, h, x_hi, start=start, stop=False)
                pe.matmul(dst, h, x_lo, start=False, stop=False)
                return pe.matmul(dst, l_, x_hi, start=False, stop=stop)

            def ada_chunk(v, layer, col, av):
                pe.wait_ge(ada_dve, v + 1)
                for s in range(2):
                    for c in range(2):
                        ins = pe.matmul(bank[6 + layer][:, ds(col + (2 * s + c), 1)],
                                        av[:, c * L + s * P:c * L + s * P + P], ones[:, 0:1], start=True, stop=True)
                ins.then_inc(ada_used, 1)

            def ada_direct(r, layer, col):
                pe.wait_ge(raw_in[r % 2], (r // 2 + 1) * 16)
                for s in range(2):
                    for k in range(DT):
                        ins = pe.matmul(bank[6 + layer][:, col + 2 * s:col + 2 * s + 2],
                                        raw[r % 2][:, k * 256 + s * P:k * 256 + s * P + P], sc[:, k, :],
                                        start=k == 0, stop=k == DT - 1)
                ins.then_inc(ada_used, 1)

            def norm(key, n=NT):
                pl = norms[key]
                pe.wait_ge(acc_done, pl.h)
                pe.matmul(bank[0][:, 0:n], ones[:], acc[:, 0:n], start=True, stop=True).then_inc(nsum, 1)

            def two_tiles(wslot, banks, q, n=NT):
                for k in range(DT):
                    pe.wait_ge(p_lo, q + k + 1)
                    for s in range(2):
                        ins = mm3(bank[banks + s][:, 0:n], wslot, k * 256 + s * P, xh[:, k, 0:n], xl[:, k, 0:n],
                                  k == 0, k == DT - 1)
                ins.then_inc(w_used, 1)

            def ffn(key, ada=None, n=NT):
                norm(key, n)
                pi, po = ffn_in[key], ffn_out[key]
                x0 = norms[key].q
                if key == "00":
                    pe.wait_ge(ada_out, 1)

                def ada_sum(j, odd):
                    ada_chunk(j + pi.v, ada[0], j * 4 + 4 * ada[1], tt[2 + odd])

                def pair(i, first, last):
                    for u in range(2):
                        pe.wait_ge(w_lo, i * 2 + (pi.w + u + 1))
                        if u == 0:
                            pe.wait_ge(gate_ready, i * 2 + pi.gate)
                        else:
                            pe.wait_ge(p_ready, i * 2 + pi.q)
                        two_tiles((pi.w + u) % 2, 2 * u, x0, n)
                        if ada and not (first and u == 0):
                            ada_sum(i * 2 + (u - 1), 1 - u)
                steps_both(pe, FT // 2, pair)
                if ada:
                    ada_sum(FT - 1, 1)

                def mpair(i, last):
                    for um in range(2):
                        pe.wait_ge(h_done, i * 2 + (po.h + um - 1))
                        for half in range(2):
                            u = um * 2 + half
                            n_ = po.w + u
                            pe.wait_ge(w_lo, i * 4 + (n_ + 1))
                            if u == 0:
                                pe.wait_ge(p_lo, pi.q + FT - 2)
                            for kk in range(11):
                                k = half * 11 + kk
                                if k == FT - 2 and um == 0:
                                    pe.wait_ge(p_lo, pi.q + FT)
                                ins = mm3(bank[4 + um][:, 0:n], n_ % 2, kk * P, gh[:, k, 0:n], gl[:, k, 0:n],
                                          k == 0, k == FT - 1)
                            ins.then_inc(w_used, 1)
                steps(pe, DT // 2, mpair)

            pe.wait_ge(s_cst, 16)
            pe.wait_ge(s_vec, 16 * VEC_DMAS)
            stage = tt[0][:, :].rearrange("p (a c) -> p a c", c=P)
            for a in range(4):
                n = min(P, V_ALL - a * P)
                ins = pe.transpose(bank[7][:, a * P:a * P + n], stage[0:n, a, :], small[0:n, 0:n])
            ins.then_inc(vec_t, 1)
            pe.wait_ge(s_x, 32)
            for k in range(DT):
                if k >= 4:
                    pe.wait_ge(h_done, k - 3)
                for a in range(4):
                    ins = pe.transpose(bank[k % 4][:, a * P:a * P + P], xstage[:, a, k * P:k * P + P], ident)
                ins.then_inc(x_t, 1)
            pe.wait_ge(s_fil, 16 * 8)
            pe.wait_ge(vec_out, 1)
            for layer in range(2):
                rows_, rhs = (33, hsm[0:33, 0, :]) if layer == 0 else (64, hsm[:, 3, :])
                if layer:
                    pe.wait_ge(hid_sin, 1)
                pe.matmul(bank[7][0:64, 0:L], hsm[0:rows_, 1, 64 * layer:64 * layer + 64], rhs,
                          start=True, stop=True).then_inc(hid_mm, 1)
            pe.wait_ge(h_done, DT)
            pe.wait_ge(s_set, 1)

            def early_ada(a):
                ada_chunk(a // 2, 0, early_col(a), early_av[a // 2 % 2])
                ada_direct(a + 3, 0, early_col(a + 1))

            def early_col(a):
                return 4 * (a if a < 12 else 22 + a)
            pe.wait_ge(sc_done, 1)
            early_ada(0)
            pe.wait_ge(hid_sin, 2)

            def filters(unit):
                o_, hh = unit // 2, unit % 2
                if unit:
                    pe.wait_ge(p_ready, unit * 4)
                for n in range(2):
                    for d in range(2):
                        c = (o_ * 2 + d) * D + hh * 512
                        ins = pe.matmul(bank[2 * d + n][:], hsm[:, 4, n * P:n * P + P], w3[:, c:c + 512],
                                        start=True, stop=True)
                    ins.then_inc(fil_mm, 1)
            filters(0)
            early_ada(2)
            pe.wait_ge(w_lo, 2)
            for unit in range(4):
                if unit < 3:
                    filters(unit + 1)
                for kt in range(5):
                    x = unit * 5 + kt
                    if x >= 2:
                        pe.wait_ge(spec_out, x - 1)
                    eo = 1 if kt in (2, 3) else 0
                    for k in range(2):
                        pe.wait_ge(p_lo, unit * 4 + 2 * k + eo + 1)
                        slot, lo = (0, k * 512 + kt * P) if kt < 4 else (1, k * P)
                        ins = mm3(bank[4 + x % 2][:], slot, lo, feh[:, eo, k, :], fel[:, eo, k, :], k == 0, k == 1)
                    ins.then_inc(spec_mm, 1)
                early_ada(4 + 2 * unit)
            early_ada(12)
            pe.wait_ge(s_set, 2)
            pe.wait_ge(p_ready, 16)
            pe.wait_ge(spec_out, 20)
            pe.matmul(bank[5][:, 0:1], ones[:], ones[:, 0:1], start=True, stop=True).then_inc(w_used, 2)

            ffn("00", (0, 12))
            norm("hy")
            def hy_pair(i, last):
                for u in range(2):
                    pe.wait_ge(w_lo, i * 2 + (HYIN.w + u + 1))
                    pe.wait_ge(z_free, i * 4 + (HYIN.zf + 2 * u - 2))
                    two_tiles((HYIN.w + u) % 2, 2 * u, norms["hy"].q)
            steps(pe, 6, hy_pair)
            pe.wait_ge(w_lo, HYDFT.w + 1)
            pe.wait_ge(z_free, HYIN.zf + 24)
            pe.wait_ge(hy_ready, 2 + 24)
            for conv in range(2):
                if conv:
                    pe.wait_ge(inv_out, 16)
                for b in range(8):
                    x = conv * 8 + b
                    if b >= 2:
                        pe.wait_ge(vt_lo, x - 1)
                    for c in range(4):
                        ins = pe.transpose(bank[4 + b % 2][:, c * P:c * P + P],
                                           hyu[:, (0 if conv else 16) + (b % 2) * 4 + c, (b // 2) * P:(b // 2) * P + P], ident)
                    ins.then_inc(vt_t, 1)
                for unit in range(5):
                    if unit < 4:
                        x = conv * 4 + unit
                        seg, half = unit // 2, unit % 2
                        if x:
                            pe.wait_ge(cm_mul, 4 * x)
                        for ft in range(4):
                            for k in range(2):
                                b = (2 * seg + k) * 2 + half
                                pe.wait_ge(vt_lo, conv * 8 + b + 1)
                                ins = mm3(bank[ft][:], 0, k * 512 + ft * P, xh[:, b, :], xl[:, b, :], k == 0, k == 1)
                        ins.then_inc(fwd_mm, 1)
                        for j in (2 * x, 2 * x + 1):
                            if j < HYENA_ADA:
                                ada_direct(HYDFT.raw + 1 + j, 1, 4 * j)
                    if unit:
                        y = conv * 4 + unit - 1
                        pe.wait_ge(p_lo, HYDFT.q + 4 * y + 4)
                        for c in range(4):
                            if c % 2 == 0:
                                if unit > 1:
                                    pe.wait_ge(inv_out, 4 * (y - 1) + c + 2)
                                else:
                                    pe.wait_ge(vt_lo, conv * 8 + 8)
                            dst = bank[4 + c // 2][:, (c % 2) * L:(c % 2) * L + L]
                            for ft in range(4):
                                y_h = wh[1][:, ft * 512 + c * P:ft * 512 + c * P + P]
                                y_l = wl[1][:, ft * 512 + c * P:ft * 512 + c * P + P]
                                f_h = wh[0][:, 1024 + ft * L:1024 + ft * L + L]
                                f_l = wl[0][:, 1024 + ft * L:1024 + ft * L + L]
                                pe.matmul(dst, y_h, f_h, start=ft == 0, stop=False)
                                pe.matmul(dst, y_h, f_l, start=False, stop=False)
                                ins = pe.matmul(dst, y_l, f_h, start=False, stop=ft == 3)
                            if c % 2:
                                ins.then_inc(inv_mm, 1)
            pe.wait_ge(cm_mul, 32)
            pe.matmul(bank[0][:, 0:1], ones[:], ones[:, 0:1], start=True, stop=True).then_inc(w_used, 1)
            for j in range(4):
                pe.wait_ge(w_lo, HYOUT.w + j + 1)
                pe.wait_ge(h_done, HYOUT.h + 2 * j) if j else pe.wait_ge(inv_out, 32)
                two_tiles((HYOUT.w + j) % 2, 4, HYY.q)
            ffn("01", (1, HYENA_ADA))

            ffn("10")
            norm("mb")
            x0 = norms["mb"].q

            def wide(pl, chunks, free, base, n):
                def pair(i, last):
                    for u in range(2):
                        pe.wait_ge(w_lo, i * 2 + (pl.w + u + 1))
                        pe.wait_ge(free, i * 4 + (base + 2 * u - 2))
                        two_tiles((pl.w + u) % 2, 2 * u, x0, n)
                steps(pe, chunks // 2, pair)
            wide(XB, 12, conv_free, XB.conv, NT)
            pe.wait_ge(w_lo, DTP.w + 1)
            for k in range(DT):
                ins = mm3(bank[4][:], DTP.w % 2, k * P, xh[:, k, :], xl[:, k, :], k == 0, k == DT - 1)
            ins.then_inc(w_used, 1)
            wide(CP, 4, conv_free, CP.conv, L)
            pe.wait_ge(conv_free, CP.conv + 8)
            wide(ZP, 8, z_free, ZP.zf, L)

            pe.wait_ge(z_free, ZP.zf + 16)
            pe.wait_ge(cv_silu, 2 + 32)
            for b in range(4):
                if b >= 2:
                    pe.wait_ge(tb_out, b - 1)
                for c in range(4):
                    m = IT + (b % 2) * 4 + c
                    ins = pe.transpose(bank[6 + b % 2][:, c * P:c * P + P], xb[:, 1, m, (b // 2) * P:(b // 2) * P + P], ident)
                ins.then_inc(tb_mm, 1)

            def turn_x(x0_, seg):
                for b8 in range(8):
                    T, c4 = b8 // 4, b8 % 4
                    if x0_ + b8 >= 4:
                        pe.wait_ge(tr_out, x0_ + b8 - 3)
                    for c in range(4):
                        ins = pe.transpose(bank[(x0_ + b8) % 4][:, c * P:c * P + P],
                                           xb[:, seg, c4 * 4 + c, T * P:T * P + P], ident)
                    ins.then_inc(tr_mm, 1)
            pe.wait_ge(dt_v, 4)
            pe.wait_ge(tb_out, 4)
            for j in range(6):
                ins = pe.transpose(bank[7][:, 64 * j:64 * j + 64], dts[64:128, j // 2, (j % 2) * P:(j % 2) * P + P],
                                   small[64:128, 64:128])
            ins.then_inc(tk_t, 1)
            turn_x(0, 1)
            pe.wait_ge(tr_out, 8)
            for g in range(GROUPS):
                if g >= 2:
                    pe.wait_ge(st_out, g - 1)
                for d in range(2):
                    for T in range(2):
                        ins = pe.matmul(bank[4 + g % 2][:, d * L:d * L + L], btok[:, T, g * P:g * P + P],
                                        xtok[:, d, T, g * L:g * L + L], start=T == 0, stop=T == 1)
                ins.then_inc(st_mm, 1)
            turn_x(8, 0)
            pe.wait_ge(tr_out, 16)
            pe.wait_ge(st_out, GROUPS)
            pe.wait_ge(tk_out, 1)

            def b_dot_c(g):
                if g:
                    pe.wait_ge(cb_out, g)
                for T in range(2):
                    ins = pe.matmul(bank[6][:, T * L:T * L + L], xb[:, 0, IT + g, T * P:T * P + P], csb[:, g, :],
                                    start=True, stop=True)
                ins.then_inc(cb_mm, 1)

            b_dot_c(0)
            for g in range(GROUPS):
                if g >= 2:
                    pe.wait_ge(y_done, g - 1)
                for r in range(HPG):
                    if r == 1 and g + 1 < GROUPS:
                        b_dot_c(g + 1)
                    h = g * HPG + r
                    b = r % 2
                    hc = slice(h * HD, h * HD + HD)
                    dst = bank[4 + g % 2][b * HD:b * HD + HD, r // 2 * L:r // 2 * L + L]
                    pe.wait_ge(cs_done, h + 1)
                    for d in range(2):
                        pe.matmul(dst, ssb[:, d, hc], csx[r][:, d * L:d * L + L], start=d == 0, stop=False)
                    pe.wait_ge(m_done, h + 1)
                    m = mm_[b]
                    pe.matmul(dst, xtok[:, 0, 0, hc], m[:, 0:256], start=False, stop=False)
                    pe.matmul(dst[:, 0:P], xtok[:, 1, 0, hc], m[:, 512:640], start=False, stop=False)
                    pe.matmul(dst[:, P:L], xtok[:, 0, 1, hc], m[:, 640:768], start=False, stop=False)
                    pe.matmul(dst, xtok[:, 1, 1, hc], m[:, 256:512], start=False, stop=True).then_inc(head_mm, 1)
            pe.wait_ge(cb_out, GROUPS)
            for g in range(GROUPS):
                pe.wait_ge(g_sq, g + 1)
                if g >= 2:
                    pe.wait_ge(g_rms, g - 1)
                for mt in range(2):
                    ins = pe.matmul(bank[6 + g % 2][:, 0:L], ones[:], tt[g % 2][:, mt * L:mt * L + L],
                                    start=mt == 0, stop=mt == 1)
                ins.then_inc(g_sum, 1)

            def mb_pair(i, last):
                for um in range(2):
                    n_ = MBOUT.w + um
                    pe.wait_ge(w_lo, i * 2 + (n_ + 1))
                    pe.wait_ge(h_done, i * 2 + (MBOUT.h + um - 1))
                    for k in range(IT):
                        if k % 2 == 0 and um == 0:
                            pe.wait_ge(p_lo, MBN.q + k // 2 + 1)
                        ins = mm3(bank[4 + um][:, 0:L], n_ % 2, k * P, ynh[:, k, :], ynl[:, k, :], k == 0, k == IT - 1)
                    ins.then_inc(w_used, 1)
            steps(pe, DT // 2, mb_pair)
            ffn("11", n=L)
            norm("fin", L)
            for k in range(DT):
                pe.wait_ge(fin_p, k + 1)
                if k >= 4:
                    pe.wait_ge(fin_o, k - 3)
                else:
                    pe.wait_ge(rms_done, norms["fin"].norm + 1)
                for T in range(2):
                    ins = pe.transpose(bank[k % 4][:, T * P:T * P + P], pp[k % 2][:, T * P:T * P + P], ident)
                ins.then_inc(fin_t, 1)


_INS = ['x', 'c', 'ctx', 'c_ctx', 'ada_w', 'ada_b', 'ffn_in', 'ffn_out', 'hy_in_w', 'hy_in_b', 'hy_conv_w',
        'hy_conv_b', 'hy_pos_w1', 'hy_pos_b1', 'hy_freq', 'hy_pos_w2', 'hy_pos_b2', 'hy_pos_w3', 'hy_bias',
        'hy_out_w', 'hy_out_b', 'mb_in_w', 'mb_conv_w', 'mb_conv_b', 'mb_dt_bias', 'mb_A_log', 'mb_D',
        'mb_norm_w', 'mb_out_w', 'final_norm_w']


def _constants():
    import math
    import numpy as np

    n = 2 * L
    f32 = np.float32
    tok = np.arange(L)
    ang = 2 * math.pi * ((tok[:, None] * np.arange(L)[None, :]) % n) / n
    alt = np.where(tok % 2, -1.0, 1.0)
    cos, sin = np.cos(ang), -np.sin(ang)
    im = sin.copy()
    im[:, 0] = alt
    cos2 = cos.copy()
    cos2[:, 0] = alt
    fwd = np.concatenate([cos, im], 1)
    inv_re = 2 * cos.T / n
    inv_re[0] /= 2
    inv_im = 2 * sin.T / n
    inv_im[0] = alt / n
    inv = np.concatenate([inv_re, inv_im], 0)
    dft1 = np.concatenate([fwd.reshape(2, P, 512).transpose(1, 0, 2).reshape(P, 1024),
                           inv.reshape(4, P, L).transpose(1, 0, 2).reshape(P, 1024)], 1)
    dft2 = cos2[:, 0:P].reshape(2, P, P).transpose(1, 0, 2).reshape(P, 256)
    tl = np.linspace(0.0, 1.0, L, dtype=f32)
    bands = np.linspace(1e-4, 15, 16, dtype=f32)
    a = (f32(2.0 * math.pi / L) * tok.astype(f32)[:, None] * bands[None, :]).astype(f32)
    z = np.concatenate([tl[:, None], np.cos(a), -np.sin(a)], 1)
    deltas = np.abs(np.linspace(math.log(1e-2) / 1.5, math.log(1e-2) / 0.3, D, dtype=f32))
    dec = np.exp(-tl[:, None] * deltas[None, :]).reshape(2, P, D).transpose(1, 0, 2).reshape(P, 2 * D)
    small = np.concatenate([np.eye(P), np.ones((P, 1))], 1)
    small[0, P] = 0
    s, tt_ = np.arange(P)[:, None], np.arange(P)[None, :]
    f = np.where(tt_ >= s, 1.0, 0.0)
    b = np.where(tt_ <= s, 1.0, 0.0)
    mask = np.concatenate([f, b, f], 1)
    return {k: np.ascontiguousarray(v, dtype=f32) for k, v in
            dict(c_dft1=dft1, c_dft2=dft2, c_z=z.T, c_decay=dec, c_small=small, c_mask=mask).items()}


def kernel(**inputs):
    import numpy as _np
    import concourse.bacc as _bacc
    from concourse.bass_utils import run_bass_kernel_spmd as _run

    nc = _bacc.Bacc("TRN2", target_bir_lowering=False, num_devices=1)
    arrays, args = {}, {}
    given = {name: _np.ascontiguousarray(inputs[name]) for name in _INS}
    given.update(_constants())
    for name, a in given.items():
        arrays[f"in_{name}"] = a
        args[name] = nc.dram_tensor(f"in_{name}", a.shape, mybir.dt.from_np(a.dtype), kind="ExternalInput").ap()
    out = nc.dram_tensor("out_0", (1, L, D), F32, kind="ExternalOutput").ap()
    kscr = nc.dram_tensor("filter_spectra", (P, 4, 5, 512), F32, kind="Internal").ap()
    afscr = nc.dram_tensor("decays", (HEADS, 2, L), F32, kind="Internal").ap()
    build(nc, args, out, kscr, afscr)
    r = _run(nc, [arrays], core_ids=[0])
    return r.results[0]["out_0"]
```

```python
from contextlib import ExitStack, contextmanager

import concourse.bass as bass
from concourse import mybir

F32 = mybir.dt.float32
F32R = mybir.dt.float32r
ALU = mybir.AluOpType
ACT = mybir.ActivationFunctionType

P = 128
D = 1024
DT = D // P
L = 256
NT = 2 * L
FFN = 2816
FT = FFN // P
INNER = 2048
IT = INNER // P
GROUPS = 8
HPG = 4
HEADS = GROUPS * HPG
HD = 64
CONVT = 32
MB_IN = 6208
EPS = 1e-6
CW = 2048
MODT = 9 * DT
ADA_CHUNKS = 36
FIRST_ADA = 12
EARLY_V = FIRST_ADA // 2
FFN_ADA = 20
ADA_FIRST = [FIRST_ADA + i * FFN_ADA for i in range(3)]
assert ADA_FIRST[2] + FFN_ADA == 2 * ADA_CHUNKS

V_ADA = 0
V_HY_IN_B = 144
V_HY_CW = 168
V_HY_CB = 240
V_HY_BIAS = 264
V_HY_OUT_B = 280
V_MB_CW = 288
V_MB_CB = 384
V_MB_NORM = 416
V_FINAL = 432
V_C = 440
V_CCTX = 448
V_ALL = 456
VEC_ROWS = (("ada_b", 144), ("hy_in_b", 24), ("hy_conv_w", 72), ("hy_conv_b", 24), ("hy_bias", 16),
            ("hy_out_b", 8), ("mb_conv_w", 96), ("mb_conv_b", 32), ("mb_norm_w", 16), ("final_norm_w", 8),
            ("c", 8), ("c_ctx", 8))


def vec_pieces():
    base, out = 0, []
    for name, count in VEC_ROWS:
        done = 0
        while done < count:
            k = min(count - done, P - (base + done) % P)
            out.append((name, done, k, base + done))
            done += k
        base += count
    return out


VEC_DMAS = len(vec_pieces())

TWO_PI = (6.28125, 0.0019350051879882812, 3.019916050561733e-07)
ROUND = 12582912.0
PI_DOWN = 3.1415925


class Chain:

    def __init__(self, eng, sem):
        self.eng, self.sem, self.base, self.n = eng, sem, 0, 0

    def mark(self, ins):
        ins.then_inc(self.sem, 1)
        self.n += 1

    def sync(self):
        self.eng.wait_ge(self.sem, self.base + self.n)

    def __call__(self, ins):
        self.mark(ins)
        self.sync()


@contextmanager
def rolled(eng, count, chain=None, per=0):
    start = chain.base + chain.n if chain else 0
    with eng.Fori(0, count) as i:
        if chain:
            chain.base, chain.n = i * per + start, 0
        yield i
        if chain:
            assert chain.n == per, (chain.n, per)
    if chain:
        chain.base, chain.n = start + count * per, 0


def steps(eng, count, body, chain=None, per=0):
    if count > 1:
        with rolled(eng, count - 1, chain, per) as i:
            body(i, False)
    body(count - 1, True)


def steps_both(eng, count, body):
    body(0, True, False)
    with eng.Fori(0, count - 2) as i:
        body(i + 1, False, False)
    body(count - 1, False, True)


class Place:

    def __init__(self, plan, w=0, a=0, v=0, q=0, h=0, gate=0, conv=0, zf=0, norm=0):
        self.v = plan["v"]
        self.w, self.a, self.raw, self.q, self.h = plan["w"], plan["a"], plan["raw"], plan["q"], plan["h"]
        self.gate, self.conv, self.zf, self.norm = plan["gate"], plan["conv"], plan["zf"], plan["norm"]
        for name, add in (("w", w), ("a", a), ("v", v), ("raw", w + a), ("q", q), ("h", h), ("gate", gate),
                          ("conv", conv), ("zf", zf), ("norm", norm)):
            plan[name] += add


def core_groups(eng, group, tail, chain=None, per=0):
    group(0, 0, True, False, False)
    group(0, 1, False, True, False)
    with rolled(eng, GROUPS // 2 - 2, chain, per) as i:
        group(i + 1, 0, False, True, False)
        group(i + 1, 1, False, True, False)
    group(GROUPS // 2 - 1, 0, False, True, False)
    group(GROUPS // 2 - 1, 1, False, True, True)
    tail()


def build(nc, t, out, kscr, afscr):
    plan = dict(w=0, a=0, v=0, raw=0, q=0, h=0, gate=1, conv=3, zf=3, norm=0)
    P0 = Place(plan, w=2, a=FIRST_ADA, v=EARLY_V, q=16, h=DT)
    ffn_in, ffn_out, norms = {}, {}, {}

    def plan_norm(key, k=DT):
        norms[key] = Place(plan, q=k, norm=1)

    def plan_ffn(key, a_in=0):
        plan_norm(key)
        ffn_in[key] = Place(plan, w=FT, a=a_in, v=a_in, q=FT, gate=FT)
        ffn_out[key] = Place(plan, w=2 * DT, h=DT)

    plan_ffn("00", FFN_ADA)
    plan_norm("hy")
    HYIN = Place(plan, w=12, zf=24)
    HYDFT = Place(plan, w=1)
    HYOUT = Place(plan, w=4, h=DT)
    plan_ffn("01", FFN_ADA)
    plan_ffn("10", FFN_ADA)
    plan_norm("mb")
    XB = Place(plan, w=12, conv=24)
    DTP = Place(plan, w=1)
    CP = Place(plan, w=4, conv=8)
    ZP = Place(plan, w=8, zf=16)
    MBN = Place(plan, q=8)
    MBOUT = Place(plan, w=8, h=DT)
    plan_ffn("11")
    plan_norm("fin", 0)

    with ExitStack() as ctx:
        top = [16512]

        def at(name, shape, dt, offset):
            return nc.alloc_sbuf_tensor_at(name, shape, dt, offset=offset)

        def room(nbytes):
            o = top[0]
            top[0] = o + (nbytes + 31) // 32 * 32
            assert top[0] <= 229344, top[0]
            return o

        def sb(name, cols, dt=F32):
            n = 4
            for c in cols:
                n *= c
            return at(name, [P, *cols], dt, room(n))

        def sem(name):
            return ctx.enter_context(nc.semaphore(name))

        KB = 1024
        hT = sb("hT", [DT, NT])
        o_xh = room(16 * KB)
        o_xl = room(16 * KB)
        assert o_xl == o_xh + 16 * KB
        xh = at("xh", [P, DT, NT], F32R, o_xh)
        xl = at("xl", [P, DT, NT], F32R, o_xl)
        xtok = at("xtok", [P, 2, 2, INNER], F32, o_xh)
        xstage = at("xstage", [P, 4, D], F32, o_xl)
        big = room(88 * KB)
        gh = at("gh", [P, FT, NT], F32R, big)
        gl = at("gl", [P, FT, NT], F32R, big + 44 * KB)
        ksb = at("ksb", [P, 4, 5, 512], F32, big)
        hyu = at("hyu", [P, 24, NT], F32, big + 40 * KB)
        w3 = at("w3", [64, 4 * D], F32, big + 40 * KB)
        decay = at("decay", [P, 2, D], F32, big + 56 * KB)
        feh = [at(f"feh{i}", [P, 2, 2, 512], F32R, o) for i, o in enumerate((big + 64 * KB, o_xl))]
        fel = [at(f"fel{i}", [P, 2, 2, 512], F32R, o) for i, o in enumerate((big + 72 * KB, o_xl + 8 * KB))]
        hsm = at("hsm", [64, 7, L], F32, big + 80 * KB)
        xb = at("xb", [P, 2, 24, L], F32, big)
        csb = at("csb", [P, 8, L], F32, big + 48 * KB)
        zsb = at("zsb", [P, IT, L], F32, big + 56 * KB)
        ssb = at("ssb", [P, 2, INNER], F32, big + 72 * KB)
        ynh = at("ynh", [P, IT, L], F32R, big + 24 * KB)
        ynl = at("ynl", [P, IT, L], F32R, big + 56 * KB)
        ost = at("ost", [P, 2, D], F32, big)
        raw = [sb(f"raw{i}", [CW]) for i in range(2)]
        o_w = room(32 * KB)
        wh = [at(f"wh{i}", [P, CW], F32R, o_w + i * 8 * KB) for i in range(2)]
        wl = [at(f"wl{i}", [P, CW], F32R, o_w + (2 + i) * 8 * KB) for i in range(2)]
        prod = [at(f"prod{i}", [P, 4, 512], F32, o_w + (8 + 16 * i) * KB) for i in range(2)]
        assert HYDFT.w % 2 == 0
        o = [o_w]

        def core(name, cols, parts=P):
            n = 4
            for c in cols:
                n *= c
            o[0] += n
            assert o[0] <= o_w + 32 * KB
            return at(name, [parts, *cols], F32, o[0] - n)

        ee = [core(f"ee{i}", [2 * L]) for i in range(HPG)]
        mm_ = [core(f"mm{i}", [3 * L]) for i in range(2)]
        afb = [core(f"afb{i}", [2, L]) for i in range(HPG)]
        dm = [core(f"dm{i}", [2 * P]) for i in range(2)]
        cbx = [core(f"cbx{i}", [3 * L]) for i in range(2)]
        mask = core("mask", [3, P])
        btok = at("btok", [P, 2, D], F32, o_w)
        dts = at("dts", [P, 8, L], F32, o_w + 12 * KB)
        tt = [sb(f"tt{i}", [NT]) for i in range(4)]
        early_av = [at(f"early_av{i}", [P, NT], F32, o_xh + i * 2 * KB) for i in range(2)]
        pp = [sb(f"pp{i}", [NT]) for i in range(2)]
        csx = tt[0:2] + pp
        acc = sb("acc", [NT])
        rs = sb("rs", [NT])
        sel = sb("sel", [GROUPS, GROUPS])
        vecs = sb("vecs", [V_ALL])
        mods = [sb(f"mods{i}", [MODT, 2]) for i in range(2)]
        sc = sb("sc", [DT, 2])
        small = sb("small", [129])
        ones = sb("ones", [P])
        eps = sb("eps", [1])
        par = sb("par", [4])
        dcol = sb("dcol", [IT])
        tk = sb("tk", [6, 64])
        ident = small[:, 0:P]
        mask0 = small[:, P:P + 1]

        bank = [ctx.enter_context(nc.psum_tensor(f"bank{i}", [P, 512], F32)) for i in range(8)]

        raw_in = [sem(f"raw_in{i}") for i in range(2)]
        w_hi = sem("w_hi")
        w_lo = sem("w_lo")
        w_used = sem("w_used")
        ada_dve = sem("ada_dve")
        ada_used = sem("ada_used")
        ada_out = sem("ada_out")
        p_ready = sem("p_ready")
        p_hi = sem("p_hi")
        p_lo = sem("p_lo")
        h_done = sem("h_done")
        sq_done = sem("sq_done")
        acc_done = sem("acc_done")
        acc_zero = sem("acc_zero")
        g_rec = sem("g_rec")
        g_bc = sem("g_bc")
        nsum = sem("nsum")
        rms_done = sem("rms_done")
        rms_inv = sem("rms_inv")
        rms_bc = sem("rms_bc")
        gate_ready = sem("gate_ready")
        conv_free = sem("conv_free")
        z_free = sem("z_free")
        dve_own = sem("dve_own")
        s_vec = sem("s_vec")
        s_x = sem("s_x")
        s_cst = sem("s_cst")
        s_fil = sem("s_fil")
        s_par = sem("s_par")
        s_set = sem("s_set")
        vec_t = sem("vec_t")
        vec_out = sem("vec_out")
        sc_done = sem("sc_done")
        x_t = sem("x_t")
        hid_mm = sem("hid_mm")
        hid_arg = sem("hid_arg")
        hid_sin = sem("hid_sin")
        fil_mm = sem("fil_mm")
        spec_mm = sem("spec_mm")
        spec_out = sem("spec_out")
        spec_st = sem("spec_st")
        spec_ld = sem("spec_ld")
        hy_ready = sem("hy_ready")
        y_hi = sem("y_hi")
        y_lo = sem("y_lo")
        vt_t = sem("vt_t")
        vt_hi = sem("vt_hi")
        vt_lo = sem("vt_lo")
        fwd_mm = sem("fwd_mm")
        cm_mul = sem("cm_mul")
        y_sum = sem("y_sum")
        inv_mm = sem("inv_mm")
        inv_out = sem("inv_out")
        cv_in = sem("cv_in")
        cv_silu = sem("cv_silu")
        dt_v = sem("dt_v")
        dt_e = sem("dt_e")
        af_st = sem("af_st")
        tk_t = sem("tk_t")
        tk_out = sem("tk_out")
        tr_mm = sem("tr_mm")
        tr_out = sem("tr_out")
        tb_mm = sem("tb_mm")
        tb_out = sem("tb_out")
        st_mm = sem("st_mm")
        st_out = sem("st_out")
        s_mask = sem("s_mask")
        afb_in = [sem(f"afb_in{i}") for i in range(HPG)]
        cb_mm = sem("cb_mm")
        cb_out = sem("cb_out")
        d_done = sem("d_done")
        e_done = sem("e_done")
        ex_done = sem("ex_done")
        cs_done = sem("cs_done")
        m_done = sem("m_done")
        head_mm = sem("head_mm")
        y_done = sem("y_done")
        g_sq = sem("g_sq")
        g_sum = sem("g_sum")
        g_rms = sem("g_rms")
        fin_p = sem("fin_p")
        fin_t = sem("fin_t")
        fin_o = sem("fin_o")
        s_out = sem("s_out")

        rows = lambda a: a.rearrange("(k p) n -> p k n", p=P)
        ada_v = [rows(t["ada_w"][i]) for i in range(2)]
        ffi_v = [[rows(t["ffn_in"][i, j]) for j in range(2)] for i in range(2)]
        ffo_v = [[rows(t["ffn_out"][i, j]) for j in range(2)] for i in range(2)]
        hyi_v = rows(t["hy_in_w"][0])
        hyo_v = rows(t["hy_out_w"][0])
        mbi_v = rows(t["mb_in_w"][0])
        mbo_v = rows(t["mb_out_w"][0])
        ds = bass.ds

        OUT_COLS = 11 * P

        def ada_multiply(dve, own, slot_free, r_slot, uses, av):
            dve.wait_ge(raw_in[r_slot], uses * 16)
            if slot_free is not None:
                dve.wait_ge(ada_used, slot_free)
            for k in range(DT):
                x = raw[r_slot][:, k * 256:k * 256 + 256]
                for c in range(2):
                    dst, w = av[:, c * L:c * L + L], sc[:, k, c:c + 1]
                    ins = dve.tensor_scalar(dst, x, w, None, ALU.mult) if k == 0 else \
                        dve.scalar_tensor_tensor(dst, x, w, dst, ALU.mult, ALU.add)
                    if k < DT - 1:
                        own.mark(ins)
                if k < DT - 1:
                    own.sync()
            ins.then_inc(ada_dve, 1)

        TURN = (0, 2, 1, 3, 4, 6, 5, 7)

        block = ctx.enter_context(nc.Block())

        @block.sync
        def _(sp):
            def load(r, src, k, n):
                slot = r % 2
                dst = raw[slot][:, 0:k * n].rearrange("p (k n) -> p k n", n=n)
                sp.dma_start(dst, src).then_inc(raw_in[slot], 16)

            def ada_free(count):
                sp.wait_ge(ada_dve, count)

            def begin(pl):
                if pl.w:
                    sp.wait_ge(w_lo, pl.w)
                if pl.v:
                    ada_free(pl.v)

            def stream(pl, count, src, k, n):
                sp.wait_ge(w_lo, pl.w)
                with sp.Fori(0, count // 2) as i:
                    for u in range(2):
                        sp.wait_ge(w_lo, i * 2 + (pl.w - 1 + u))
                        if u:
                            ada_free(pl.v)
                        load(pl.raw + u, src(i, u), k, n)

            def mixed_stream(pl, src, first):
                begin(pl)
                load(pl.raw, src(0, 0), 8, 256)
                pairs = FFN_ADA // 2
                turn = min(pairs, max(0, (ADA_CHUNKS - first) // 2))
                for layer, a, b in ((0, 0, turn), (1, turn, pairs)):
                    if a == b:
                        continue
                    col0 = (first - layer * ADA_CHUNKS + 2 * a) * 256
                    with sp.Fori(0, b - a) as i:
                        for u in range(2):
                            sp.wait_ge(w_lo, i * 2 + (pl.w + 2 * a + u + 1))
                            load(pl.raw, src(i + a, 1) if u == 0 else src(i + (a + 1), 0), 8, 256)
                            ada_free(i * 2 + (pl.v + 2 * a + u))
                            load(pl.raw + 1, ada_v[layer][:, :, ds(i * 512 + (col0 + u * 256), 256)], 8, 256)
                sp.wait_ge(w_lo, pl.w + FT - 1)
                ada_free(pl.v + FFN_ADA)
                load(pl.raw + 2 * FFN_ADA + 1, src(FT // 2 - 1, 1), 8, 256)

            def wide(view, col0=0):
                return lambda i, u: view[:, :, ds(i * 512 + (col0 + u * 256), 256)]

            def ffn_in_src(view):
                return lambda i, u: view[:, :, ds(i * 256 + u * FFN, 256)]

            def ffn_out_stream(pl, view):
                stream(pl, 2 * DT, lambda m, half: view[:, half * 11:half * 11 + 11, ds(m * P, P)], 11, P)

            sp.dma_start(small[:], t["c_small"]).then_inc(s_cst, 16)
            load(0, t["c_dft1"].rearrange("p (k n) -> p k n", n=256), 8, 256)
            load(1, t["c_dft2"].rearrange("p (k n) -> p k n", n=256), 1, 256)
            sp.dma_start(xstage[:, 0:2, :], t["x"][0].rearrange("(a p) d -> p a d", p=P)).then_inc(s_x, 16)
            sp.dma_start(xstage[:, 2:4, :], t["ctx"][0].rearrange("(a p) d -> p a d", p=P)).then_inc(s_x, 16)
            for i in range(FIRST_ADA):
                if i < 2:
                    sp.wait_ge(w_lo, i + 1)
                else:
                    sp.wait_ge(ada_used, i - 1) if i % 2 else sp.wait_ge(ada_dve, i // 2)
                load(2 + i, ada_v[0][:, :, i * 256:i * 256 + 256], 8, 256)

            mixed_stream(ffn_in["00"], ffn_in_src(ffi_v[0][0]), ADA_FIRST[0])
            ffn_out_stream(ffn_out["00"], ffo_v[0][0])

            stream(HYIN, 12, wide(hyi_v), 8, 256)
            begin(HYDFT)
            load(HYDFT.raw, t["c_dft1"].rearrange("p (k n) -> p k n", n=256), 8, 256)
            begin(HYOUT)
            for j in range(4):
                if j == 1:
                    sp.wait_ge(inv_mm, 16)
                if j >= 2:
                    sp.wait_ge(w_lo, HYOUT.w - 1 + j)
                load(HYOUT.raw + j, hyo_v[:, :, j * 256:j * 256 + 256], 8, 256)

            mixed_stream(ffn_in["01"], ffn_in_src(ffi_v[0][1]), ADA_FIRST[1])
            ffn_out_stream(ffn_out["01"], ffo_v[0][1])

            mixed_stream(ffn_in["10"], ffn_in_src(ffi_v[1][0]), ADA_FIRST[2])
            ffn_out_stream(ffn_out["10"], ffo_v[1][0])

            stream(XB, 12, wide(mbi_v, INNER), 8, 256)
            begin(DTP)
            load(DTP.raw, mbi_v[:, :, MB_IN - P:MB_IN], 8, P)
            stream(CP, 4, wide(mbi_v, INNER + 3072), 8, 256)
            stream(ZP, 8, wide(mbi_v, 0), 8, 256)

            sp.wait_ge(af_st, 32)
            sp.wait_ge(st_out, GROUPS)
            for r in range(HPG):
                sp.dma_start(afb[r][:], afscr[r].partition_broadcast(P)).then_inc(afb_in[r], 16)
            with sp.Fori(0, GROUPS - 1) as g:
                for r in range(HPG):
                    sp.wait_ge(d_done, g * HPG + r + 1)
                    sp.wait_ge(e_done, g * HPG + r + 1)
                    sp.dma_start(afb[r][:], afscr[g * HPG + HPG + r].partition_broadcast(P)).then_inc(afb_in[r], 16)

            begin(MBOUT)
            with sp.Fori(0, DT // 2) as i:
                for u in range(2):
                    sp.wait_ge(w_lo, MBOUT.w - 1 + i * 2 + u)
                    load(MBOUT.raw + u, mbo_v[:, :, ds(i * 256 + u * P, P)], 16, P)

            stream(ffn_in["11"], FT, ffn_in_src(ffi_v[1][1]), 8, 256)
            ffn_out_stream(ffn_out["11"], ffo_v[1][1])

            sp.wait_ge(fin_o, DT)
            sp.dma_start(out[0].rearrange("(a p) d -> p a d", p=P), ost[:]).then_inc(s_out, 16)
            sp.wait_ge(s_out, 16)
            sp.wait_ge(spec_st, 64)
            sp.wait_ge(af_st, 32)

        @block.scalar
        def _(act):
            def split_hi(n, cols, r_slot, r_uses, w_free):
                act.wait_ge(raw_in[r_slot], r_uses * 16)
                if w_free is not None:
                    act.wait_ge(w_used, w_free)
                return act.activation(wh[n % 2][:, 0:cols], raw[r_slot][:, 0:cols], ACT.Copy).then_inc(w_hi, 1)

            def next_hi(pl, ada, i, u, per, cols=CW, ahead=1):
                j = i * per + (u + ahead)
                r = pl.raw + (2 * (u + ahead) if ada else u + ahead)
                rr = per * (2 if ada else 1) // 2
                split_hi((pl.w + u + ahead) % 2, cols, r % 2, i * rr + (r // 2 + 1), pl.w - 1 + j)

            def hi_tile(q, uses, dst, src=None):
                act.wait_ge(p_ready, uses)
                act.activation(dst, src if src is not None else pp[q % 2][:, :], ACT.Copy).then_inc(p_hi, 1)

            def norm(key, n=NT):
                pl = norms[key]
                act.wait_ge(nsum, pl.norm + 1)
                j = n // P
                act.activation(rs[0:j, 0:P], bank[7][0:j, 0:P], ACT.Sqrt, bias=eps[0:j, 0:1],
                               scale=1.0 / D).then_inc(rms_done, 1)

            def norm_hi(key, n=NT):
                pl = norms[key]
                for k in range(DT):
                    hi_tile(pl.q + k, pl.q + k + 1, xh[:, k, 0:n], pp[(pl.q + k) % 2][:, 0:n])

            def ffn(key, ada, after, n=NT):
                norm(key, n)
                norm_hi(key, n)
                if key == "00":
                    act.wait_ge(spec_st, 64)
                pi, po = ffn_in[key], ffn_out[key]
                next_hi(pi, ada, 0, 0, 2)

                def pair(i, before_last, last):
                    act.wait_ge(w_used, i * 2 + (pi.w + 1))
                    act.wait_ge(p_ready, i * 2 + pi.q)
                    for u in range(2):
                        act.activation(tt[u][:, 0:n], bank[u][:, 0:n], ACT.Silu).then_inc(gate_ready, 1)
                    if last:
                        split_hi(po.w, OUT_COLS, po.raw % 2, po.raw // 2 + 1, po.w - 1)
                    else:
                        next_hi(pi, ada, i, 0, 2, ahead=2)
                        if before_last and ada:
                            r = pi.raw + 2 * ada + 1
                            split_hi(pi.w + FT - 1, CW, r % 2, r // 2 + 1, pi.w + FT - 2)
                        else:
                            next_hi(pi, ada, i, 0, 2, ahead=3)
                    for u in range(2):
                        hi_tile(pi.q + u, i * 2 + (pi.q + u + 1), gh[:, i * 2 + u, 0:n], pp[(pi.q + u) % 2][:, 0:n])

                with act.Fori(0, FT // 2 - 2) as i:
                    pair(i, False, False)
                pair(FT // 2 - 2, True, False)
                pair(FT // 2 - 1, False, True)
                act.wait_ge(p_ready, pi.q + FT)

                next_hi(po, False, 0, 0, 4, OUT_COLS)

                def mpair(i, last):
                    for um in range(2):
                        for half in range(2):
                            u = um * 2 + half
                            if not (last and um):
                                next_hi(po, False, i, u, 4, OUT_COLS, ahead=2)
                            elif half == 0 and after is not None:
                                split_hi(after.w, CW, after.raw % 2, after.raw // 2 + 1, after.w - 1)
                        square(po, i, um, n)

                steps(act, DT // 2, mpair)

            def square(pl, i, um, n):
                act.wait_ge(h_done, i * 2 + (pl.h + um + 1))
                act.wait_ge(acc_done, i * 2 + (pl.h + um - 1))
                act.activation(tt[um][:, 0:n], hT[:, i * 2 + um, 0:n], ACT.Square).then_inc(sq_done, 1)

            stage = tt[0][:, :].rearrange("p (a c) -> p a c", c=P)
            for name, row, k, r in vec_pieces():
                v = t[name]
                if len(v.shape) > 1:
                    v = v.rearrange({2: "a b -> (a b)", 3: "a b c -> (a b c)"}[len(v.shape)])
                v = v.rearrange("(r c) -> r c", c=P)
                act.dma_start(stage[r % P:r % P + k, r // P, :], v[row:row + k, :]).then_inc(s_vec, 16)
            act.dma_start(hsm[0:33, 0, :], t["c_z"]).then_inc(s_fil, 16)
            act.dma_start(hsm[0:33, 1, 0:64], t["hy_pos_w1"][0]).then_inc(s_fil, 16)
            act.dma_start(hsm[:, 1, 64:128], t["hy_pos_w2"][0]).then_inc(s_fil, 16)
            for n, name in enumerate(("hy_pos_b1", "hy_freq", "hy_pos_b2")):
                act.dma_start(hsm[:, 1, 128 + n:129 + n], t[name][0].rearrange("(p o) -> p o", o=1)).then_inc(s_fil, 16)
            act.dma_start(w3[:], t["hy_pos_w3"][0]).then_inc(s_fil, 16)
            act.dma_start(decay[:], t["c_decay"].rearrange("p (a n) -> p a n", a=2)).then_inc(s_fil, 16)
            act.dma_start(par[64:128, 0:1], t["mb_dt_bias"][0].rearrange("d (h o) -> (d h) o", o=1)).then_inc(s_par, 16)
            act.dma_start(par[64:128, 1:2], t["mb_A_log"][0].rearrange("d (h o) -> (d h) o", o=1)).then_inc(s_par, 16)
            dv = t["mb_D"][0].rearrange("(m a) -> a m", a=2)
            with nc.allow_non_contiguous_dma(reason="32 scalars spread over partitions"):
                for a in range(2):
                    act.dma_start(dcol[64 * a:64 * a + 64, :], dv[a].partition_broadcast(64)).then_inc(s_par, 16)

            split_hi(0, CW, 0, 1, None)
            split_hi(1, 256, 1, 1, None)
            act.wait_ge(vec_out, 1)
            act.activation(sc[:, :, 0], vecs[:, V_C:V_C + DT], ACT.Silu)
            act.activation(sc[:, :, 1], vecs[:, V_CCTX:V_CCTX + DT], ACT.Silu).then_inc(sc_done, 1)
            act.activation(tt[3][:, 0:1], small[:, 0:1], ACT.Silu).then_inc(gate_ready, 1)
            act.activation(tt[3][:, 1:2], small[:, 0:1], ACT.Copy).then_inc(z_free, 3)
            act.activation(tt[3][:, 10:11], small[:, 0:1], ACT.Copy).then_inc(cv_silu, 2)
            for layer in range(2):
                act.wait_ge(hid_arg, layer + 1)
                act.activation(hsm[:, 3 + layer, :], hsm[:, 2, :], ACT.Sin).then_inc(hid_sin, 1)
            for m in range(DT):
                act.wait_ge(h_done, m + 1)
                if m >= 2:
                    act.wait_ge(acc_done, m - 1)
                act.activation(tt[m % 2][:], hT[:, m, :], ACT.Square).then_inc(sq_done, 1)
            for unit in range(4):
                if unit > 1:
                    act.wait_ge(spec_mm, 5 * (unit - 1))
                for n in range(4):
                    q = unit * 4 + n
                    hi_tile(q, q + 1, feh[unit % 2][:, n % 2, n // 2, :])
                for kt in range(5):
                    x = unit * 5 + kt
                    act.wait_ge(spec_mm, x + 1)
                    act.activation(ksb[:, unit, kt, :], bank[4 + x % 2][:], ACT.Identity,
                                   scale=mask0 if kt == 2 else 1.0).then_inc(spec_out, 1)
                act.wait_ge(spec_out, 5 * unit + 5)
                act.dma_start(kscr[:, unit], ksb[:, unit]).then_inc(spec_st, 16)
            pl = ffn_in["00"]
            split_hi(pl.w, CW, pl.raw % 2, pl.raw // 2 + 1, pl.w - 1)

            ffn("00", FFN_ADA, HYIN)
            norm("hy")
            norm_hi("hy")
            act.dma_start(ksb[:], kscr).then_inc(spec_ld, 16)

            def hy_in_pair(i, last):
                for u in range(2):
                    if last and u == 1:
                        split_hi(HYDFT.w, CW, HYDFT.raw % 2, HYDFT.raw // 2 + 1, HYDFT.w - 1)
                    else:
                        next_hi(HYIN, False, i, u, 2)
                    act.wait_ge(w_used, i * 2 + (HYIN.w + u + 1))
                    for s in range(2):
                        m = i * 4 + (u * 2 + s)
                        act.wait_ge(hy_ready, m + 1)
                        act.activation(tt[s][:], bank[2 * u + s][:], ACT.Identity,
                                       bias=vecs[:, ds(m + V_HY_IN_B, 1)]).then_inc(z_free, 1)
            steps(act, 6, hy_in_pair)

            for conv in range(2):
                for j, b in enumerate(TURN):
                    act.wait_ge(vt_t, conv * 8 + j + 1)
                    act.activation(xh[:, b, :], bank[4 + j % 2][:], ACT.Copy).then_inc(vt_hi, 1)
            act.wait_ge(fwd_mm, 8)
            for k in range(DT):
                act.wait_ge(inv_out, 24 + k + 1)
                act.activation(xh[:, k, :], hyu[:, 8 + k, :], ACT.Copy).then_inc(y_hi, 1)
            for j in range(4):
                r = HYOUT.raw + j
                split_hi(HYOUT.w + j, CW, r % 2, r // 2 + 1, HYOUT.w if j == 0 else HYOUT.w + j - 1)
                if j:
                    for um in range(2):
                        square(HYOUT, j - 1, um, NT)
            for um in range(2):
                square(HYOUT, 3, um, NT)
            pl = ffn_in["01"]
            split_hi(pl.w, CW, pl.raw % 2, pl.raw // 2 + 1, pl.w - 1)
            ffn("01", FFN_ADA, ffn_in["10"])

            ffn("10", FFN_ADA, XB)
            norm("mb")
            norm_hi("mb")

            def conv_chunk(pl, i, u, count, split, dst, n):
                split()
                act.wait_ge(w_used, i * 2 + (pl.w + u + 1))
                first = pl.conv - 3
                for s in range(2):
                    m = i * 4 + (u * 2 + s)
                    act.wait_ge(cv_silu, m + (first + 1))
                    act.activation(tt[2 + s][:, 0:n], bank[2 * u + s][:, 0:n], ACT.Identity,
                                   bias=vecs[:, ds(m + (V_MB_CB + first), 1)],
                                   scale=vecs[:, ds(m + (V_MB_CW + CONVT + first), 1)]).then_inc(cv_in, 1)
                for s in range(2):
                    m = i * 4 + (u * 2 + s)
                    act.wait_ge(conv_free, m + (pl.conv + 1))
                    act.activation(dst(m), tt[2 + s][:, 0:n] if n == L else
                                   tt[2 + s][:].rearrange("p (a n) -> p a n", a=2), ACT.Silu).then_inc(cv_silu, 1)

            def xb_pair(i, last):
                for u in range(2):
                    split = lambda: (split_hi(DTP.w, 8 * P, DTP.raw % 2, DTP.raw // 2 + 1, DTP.w - 1)
                                     if last and u == 1 else next_hi(XB, False, i, u, 2))
                    conv_chunk(XB, i, u, 12, split, lambda m: xb[:, :, m, :], NT)
            steps(act, 6, xb_pair)

            split_hi(CP.w, CW, CP.raw % 2, CP.raw // 2 + 1, CP.w - 1)
            act.wait_ge(s_par, 64)
            act.wait_ge(dt_v, 1)
            act.activation(tt[1][64:128, :], tt[0][64:128, :], ACT.Exp, scale=-1.0).then_inc(dt_e, 1)
            act.activation(par[64:128, 2:3], par[64:128, 1:2], ACT.Exp).then_inc(dt_e, 1)

            def c_pair(i, last):
                for u in range(2):
                    split = lambda: (split_hi(ZP.w, CW, ZP.raw % 2, ZP.raw // 2 + 1, ZP.w - 1)
                                     if last and u == 1 else next_hi(CP, False, i, u, 2))
                    conv_chunk(CP, i, u, 4, split, lambda m: csb[:, m, :], L)
            steps(act, 2, c_pair)

            def z_pair(i, last):
                for u in range(2):
                    if not (last and u == 1):
                        next_hi(ZP, False, i, u, 2)
                    act.wait_ge(w_used, i * 2 + (ZP.w + u + 1))
                    for s in range(2):
                        act.activation(zsb[:, i * 4 + (u * 2 + s), :], bank[2 * u + s][:, 0:L],
                                       ACT.Silu).then_inc(z_free, 1)
            steps(act, 4, z_pair)

            act.wait_ge(dt_v, 2)
            act.activation(dts[64:128, 4, :], dts[64:128, 3, :], ACT.Exp).then_inc(dt_e, 1)
            act.wait_ge(dt_v, 3)
            for d in range(2):
                act.dma_start(afscr[:, d, :], dts[64 + 32 * d:96 + 32 * d, 5, :]).then_inc(af_st, 16)
            for b in range(4):
                act.wait_ge(tb_mm, b + 1)
                act.activation(btok[:, b // 2, (b % 2) * 512:(b % 2) * 512 + 512], bank[6 + b % 2][:],
                               ACT.Copy).then_inc(tb_out, 1)
            for g in range(GROUPS):
                act.wait_ge(st_mm, g + 1)
                act.activation(ssb[:, :, g * 256:g * 256 + 256], bank[4 + g % 2][:].rearrange("p (a n) -> p a n", a=2),
                               ACT.Copy).then_inc(st_out, 1)
            act.wait_ge(st_mm, GROUPS)
            act.dma_start(mask[:].rearrange("p a n -> p (a n)"), t["c_mask"]).then_inc(s_mask, 16)

            def group(i, u, first, finish, last):
                g = i * 2 + u
                for r in range(HPG):
                    b = r % 2
                    h1 = i * 8 + (u * HPG + r + 1)
                    act.wait_ge(afb_in[r], i * 32 + (u * 16 + 16))
                    if not first:
                        act.wait_ge(head_mm, h1 - 4)
                    act.activation(csx[r][:], afb[r][:].rearrange("p a n -> p (a n)"), ACT.Exp).then_inc(ex_done, 1)
                    if not first:
                        act.wait_ge(m_done, h1 - 4)
                    act.activation(ee[r][:, P:2 * P], afb[r][:, 0, P:L], ACT.Exp, bias=tk[:, 0, ds(h1 - 1, 1)])
                    act.activation(ee[r][:, 2 * P:3 * P], afb[r][:, 1, 0:P], ACT.Exp,
                                   bias=tk[:, 1, ds(h1 + (HEADS - 1), 1)])
                    if finish and r == 3:
                        square_y(g)
                    act.wait_ge(d_done, h1)
                    act.activation(ee[r][:].rearrange("p (a n) -> p a n", n=P)[:, 0:4:3, :],
                                   dm[b][:].rearrange("p (a n) -> p a n", n=P), ACT.Exp).then_inc(e_done, 1)

            def square_y(g):
                act.wait_ge(y_done, g)
                if not isinstance(g, int) or g > 1:
                    act.wait_ge(g_sum, g - 1)
                act.activation(tt[2][:], zsb[:, ds(g * 2 - 2, 2), :].rearrange("p a n -> p (a n)"),
                               ACT.Square).then_inc(g_sq, 1)

            core_groups(act, group, lambda: square_y(GROUPS))
            split_hi(MBOUT.w, CW, MBOUT.raw % 2, MBOUT.raw // 2 + 1, MBOUT.w)
            act.wait_ge(g_sum, GROUPS)
            act.activation(tt[0][0:GROUPS, 0:L], bank[0][0:GROUPS, 0:L], ACT.Sqrt, bias=eps[0:GROUPS, 0:1],
                           scale=1.0 / L).then_inc(g_rms, 1)
            for g in range(GROUPS):
                hi_tile(MBN.q + g, MBN.q + g + 1, ynh[:, 2 * g:2 * g + 2, :].rearrange("p a n -> p (a n)"))


            next_hi(MBOUT, False, 0, 0, 2)

            def mb_pair(i, last):
                for um in range(2):
                    if not last:
                        next_hi(MBOUT, False, i, um, 2, ahead=2)
                    elif um == 0:
                        pl = ffn_in["11"]
                        split_hi(pl.w, CW, pl.raw % 2, pl.raw // 2 + 1, pl.w - 1)
                    square(MBOUT, i, um, L)
            steps(act, DT // 2, mb_pair)
            ffn("11", 0, None, L)
            norm("fin", L)
            for k in range(DT):
                act.wait_ge(fin_t, k + 1)
                act.activation(ost[:, :, k * P:k * P + P], bank[k % 4][:, 0:L].rearrange("p (a n) -> p a n", a=2),
                               ACT.Copy).then_inc(fin_o, 1)

        @block.vector
        def _(dve):
            own = Chain(dve, dve_own)

            def split_lo(n_slot, count, cols, r_slot):
                dve.wait_ge(w_hi, count)
                dve.tensor_tensor(wl[n_slot][:, 0:cols], raw[r_slot][:, 0:cols],
                                  wh[n_slot][:, 0:cols].bitcast(F32), ALU.subtract).then_inc(w_lo, 1)

            def next_lo(pl, ada, i, u, per, cols=CW):
                r = pl.raw + (2 * (u + 1) if ada else u + 1)
                split_lo((pl.w + u + 1) % 2, i * per + (pl.w + u + 2), cols, r % 2)

            def open_lo(pl, cols=CW):
                split_lo(pl.w % 2, pl.w + 1, cols, pl.raw % 2)

            def pp_free(q):
                if not isinstance(q, int) or q >= 2:
                    dve.wait_ge(p_lo, q - 1)

            def invert_rms(pl, n):
                dve.wait_ge(rms_done, pl.norm + 1)
                j = n // P
                dve.reciprocal(rs[0:j, 0:P], rs[0:j, 0:P]).then_inc(rms_inv, 1)
                dve.wait_ge(rms_bc, pl.norm + 1)

            def norm(key, layer, k0, n=NT):
                pl = norms[key]
                m = mods[layer]
                invert_rms(pl, n)
                for k in range(DT):
                    q = pl.q + k
                    p = pp[q % 2]
                    pp_free(q)
                    own(dve.tensor_tensor(p[:, 0:n], hT[:, k, 0:n], bank[7][:, 0:n], ALU.mult))
                    sh, s1 = DT * k0 + k, DT * (k0 + 1) + k
                    for w in range(n // L):
                        ins = dve.tensor_scalar(p[:, w * L:w * L + L], p[:, w * L:w * L + L], m[:, s1, w:w + 1],
                                                m[:, sh, w:w + 1], ALU.mult, ALU.add)
                    ins.then_inc(p_ready, 1)

            def residual(pl, layer, k5, i, um, n, chunk_done):
                dve.wait_ge(w_used, chunk_done)
                for w in range(n // L):
                    x = hT[:, i * 2 + um, w * L:w * L + L]
                    ins = dve.scalar_tensor_tensor(x, bank[4 + um][:, w * L:w * L + L],
                                                   mods[layer][:, i * 2 + (DT * k5 + um), w:w + 1], x,
                                                   ALU.mult, ALU.add)
                ins.then_inc(h_done, 1)

            def ffn(key, layer, k0, ada, after, n=NT, take=None):
                norm(key, layer, k0, n)
                pi, po = ffn_in[key], ffn_out[key]

                def weigh(i, u, last):
                    if ada and not last:
                        ada_multiply(dve, own, i * 2 + (pi.a + u - 1), (pi.raw + 1) % 2,
                                     i * 2 + ((pi.raw + 2 * u + 1) // 2 + 1), tt[2 + u])

                def pair(i, last):
                    if last and ada:
                        split_lo((pi.w + 1) % 2, pi.w + FT, CW, (pi.raw + 2 * ada + 1) % 2)
                    else:
                        next_lo(pi, ada, i, 0, 2)
                    weigh(i, 0, last)
                    if last:
                        open_lo(po, OUT_COLS)
                    else:
                        next_lo(pi, ada, i, 1, 2)
                    weigh(i, 1, last)
                    dve.wait_ge(w_used, i * 2 + (pi.w + 2))
                    for u in range(2):
                        dve.wait_ge(gate_ready, i * 2 + (pi.gate + u + 1))
                        pp_free(i * 2 + (pi.q + u))
                        dve.tensor_tensor(pp[(pi.q + u) % 2][:, 0:n], tt[u][:, 0:n], bank[2 + u][:, 0:n],
                                          ALU.mult).then_inc(p_ready, 1)
                steps(dve, FT // 2, pair, own, 4 * (DT - 1) if ada else 0)
                if take is not None:
                    take()

                def mpair(i, last):
                    for um in range(2):
                        for half in range(2):
                            u = um * 2 + half
                            if last and u == 3:
                                if after is not None:
                                    open_lo(after)
                            else:
                                next_lo(po, False, i, u, 4, OUT_COLS)
                        residual(po, layer, k0 + 2, i, um, n, i * 4 + (po.w + 2 * um + 2))
                steps(dve, DT // 2, mpair)

            def take_mods(used, pieces, outs):
                dve.wait_ge(ada_used, used)
                for layer, first, end in pieces:
                    a, b = DT * first, DT * end
                    o = MODT * layer
                    own.mark(dve.tensor_tensor(
                        mods[layer][:, a:b, :], bank[6][:, 2 * (o + a):2 * (o + b)].rearrange("p (m c) -> p m c", c=2),
                        vecs[:, V_ADA + o + a:V_ADA + o + b].unsqueeze(2).to_broadcast([P, b - a, 2]), ALU.add))
                own.sync()
                for layer, first, end in pieces:
                    for idx in range(first, end):
                        x = mods[layer][:, DT * idx:DT * idx + DT, :]
                        if idx % 3 == 1:
                            own.mark(dve.tensor_scalar(x, x, 1.0, None, ALU.add))
                        elif idx in (2, 8):
                            own.mark(dve.tensor_scalar(x, x, 0.5, None, ALU.mult))
                own.sync()
                dve.tensor_copy(tk[:, 0, outs:outs + 1], eps[:]).then_inc(ada_out, 1)

            own.mark(dve.memset(tt[3][:, 2:8], 0.0))
            own(dve.memset(sel[:], 0.0))
            own.mark(dve.memset(sel[:].rearrange("p a b -> p (a b)")[:, 0:GROUPS * GROUPS:GROUPS + 1], 1.0))
            dve.memset(ones[:], 1.0).then_inc(s_set, 1)
            dve.memset(eps[:], EPS).then_inc(s_set, 1)
            dve.memset(tt[3][:, 8:9], 0.0).then_inc(conv_free, 3)
            dve.memset(tt[3][:, 9:10], 0.0).then_inc(hy_ready, 2)
            own.sync()
            split_lo(0, 1, CW, 0)
            split_lo(1, 2, 256, 1)
            dve.wait_ge(vec_t, 1)
            dve.tensor_copy(vecs[:], bank[7][:, 0:V_ALL]).then_inc(vec_out, 1)
            for m in range(DT):
                dve.wait_ge(x_t, m + 1)
                dve.tensor_copy(hT[:, m, :], bank[m % 4][:]).then_inc(h_done, 1)
            dve.wait_ge(s_fil, 16 * 8)

            def early_ada(a):
                ada_multiply(dve, own, a - 3 if a >= 4 else None, 0, a // 2 + 2, early_av[a // 2 % 2])
            for layer in range(2):
                arg, cyc, red = hsm[:, 5, :], hsm[:, 6, :], hsm[:, 2, :]
                dve.wait_ge(hid_mm, layer + 1)
                b = hsm[:, 1, 128 + 2 * layer:129 + 2 * layer]
                if layer:
                    dve.wait_ge(hid_sin, 1)
                own(dve.tensor_scalar(arg, bank[7][0:64, 0:L], b, hsm[:, 1, 129:130], ALU.add, ALU.mult))
                own(dve.tensor_scalar(cyc, arg, 0.15915494309189535, ROUND, ALU.mult, ALU.add))
                own(dve.tensor_scalar(cyc, cyc, ROUND, None, ALU.subtract))
                for part in TWO_PI:
                    own(dve.scalar_tensor_tensor(arg, cyc, -part, arg, ALU.mult, ALU.add))
                dve.tensor_scalar(red, arg, PI_DOWN, -PI_DOWN, ALU.min, ALU.max).then_inc(hid_arg, 1)
                if layer == 0:
                    dve.wait_ge(sc_done, 1)
                early_ada(2 * layer)
            for unit in range(4):
                cols = slice(unit % 2 * 512, unit % 2 * 512 + 512)
                for n in range(2):
                    dve.wait_ge(fil_mm, unit * 2 + n + 1)
                    if unit or n:
                        dve.wait_ge(p_ready, unit * 4 + n * 2)
                    own.mark(dve.tensor_tensor(tt[2][:], bank[n][:], decay[:, n, cols], ALU.mult))
                    own.mark(dve.scalar_tensor_tensor(tt[3][:], bank[2 + n][:], mask0 if n == 0 else 1.0,
                                                      decay[:, n, cols], ALU.mult, ALU.mult))
                    own.sync()
                    for w in range(2):
                        q = unit * 4 + n * 2 + w
                        pp_free(q)
                        ins = dve.tensor_tensor(pp[q % 2][:], tt[2][:], tt[3][:], ALU.subtract if w else ALU.add)
                        ins.then_inc(p_ready, 1)
                early_ada(4 + unit * 2)
            take_mods(FIRST_ADA, [(0, 0, 3)], 0)
            open_lo(ffn_in["00"])

            ffn("00", 0, 0, FFN_ADA, HYIN, take=lambda: take_mods(ADA_FIRST[1], [(0, 3, 8)], 1))
            norm("hy", 0, 3)

            def hy_in_pair(i, last):
                for u in range(2):
                    if last and u == 1:
                        open_lo(HYDFT)
                    else:
                        next_lo(HYIN, False, i, u, 2)
                    for s in range(2):
                        m = i * 4 + (u * 2 + s)
                        src = tt[s][:].rearrange("p (a n) -> p a n", a=2)
                        dst = hyu[:, m, :].rearrange("p (a n) -> p a n", a=2)
                        tap = lambda w: vecs[:, ds(m + (V_HY_CW + 24 * w), 1)]
                        dve.wait_ge(z_free, m + (HYIN.zf + 1))
                        own(dve.tensor_scalar(hyu[:, m, :], tt[s][:], tap(1), vecs[:, ds(m + V_HY_CB, 1)],
                                              ALU.mult, ALU.add))
                        own(dve.scalar_tensor_tensor(dst[:, :, 1:L], src[:, :, 0:L - 1], tap(0), dst[:, :, 1:L],
                                                     ALU.mult, ALU.add))
                        dve.scalar_tensor_tensor(dst[:, :, 0:L - 1], src[:, :, 1:L], tap(2), dst[:, :, 0:L - 1],
                                                 ALU.mult, ALU.add).then_inc(hy_ready, 1)
            dve.wait_ge(w_used, HYIN.w)
            steps(dve, 6, hy_in_pair, own, 8)

            dve.wait_ge(spec_ld, 16)
            for conv in range(2):
                def turned_lo(j0):
                    for j in range(j0, j0 + 4):
                        b = TURN[j]
                        dve.wait_ge(vt_hi, conv * 8 + j + 1)
                        dve.tensor_tensor(xl[:, b, :], bank[4 + j % 2][:], xh[:, b, :].bitcast(F32),
                                          ALU.subtract).then_inc(vt_lo, 1)
                turned_lo(0)
                for unit in range(5):
                    if unit == 1:
                        turned_lo(4)
                    x = conv * 4 + unit
                    if unit < 4:
                        for n in range(4):
                            ft = n % 2
                            a, b_ = (ft, 2 + ft) if n < 2 else (2 + ft, 4 if ft == 0 else ft)
                            dve.wait_ge(fwd_mm, x + 1)
                            c0 = x * 4 + n
                            if c0 >= 2:
                                dve.wait_ge(y_sum, c0 - 1)
                            w0, w1 = tt[2 * (n % 2)], tt[2 * (n % 2) + 1]
                            own.mark(dve.tensor_tensor(w0[:], bank[ft][:], ksb[:, 2 * conv + unit % 2, a, :], ALU.mult))
                            dve.tensor_tensor(w1[:], bank[2 + ft][:], ksb[:, 2 * conv + unit % 2, b_, :],
                                              ALU.mult).then_inc(cm_mul, 1)
                    if unit:
                        u = unit - 1
                        y = conv * 4 + u
                        seg, half = u // 2, u % 2
                        for c in range(4):
                            ch = half * 4 + c
                            tok = slice(seg * L, seg * L + L)
                            src = hyu[:, (16 if conv == 0 else 0) + ch, tok]
                            if c % 2 == 0:
                                dve.wait_ge(inv_mm, 2 * y + c // 2 + 1)
                            own(dve.scalar_tensor_tensor(src, src, vecs[:, V_HY_BIAS + 8 * conv + ch:V_HY_BIAS + 8 * conv + ch + 1],
                                                         bank[4 + c // 2][:, (c % 2) * L:(c % 2) * L + L], ALU.mult, ALU.add))
                            dst = hyu[:, (0 if conv == 0 else 8) + ch, tok]
                            dve.tensor_tensor(dst, dst, src, ALU.mult).then_inc(inv_out, 1)
                dve.wait_ge(inv_out, 16 * (conv + 1))
            for j in range(5):
                if j < 4:
                    split_lo((HYOUT.w + j) % 2, HYOUT.w + j + 1, CW, (HYOUT.raw + j) % 2)
                if j:
                    for um in range(2):
                        m = (j - 1) * 2 + um
                        dve.wait_ge(w_used, HYOUT.w + j)
                        for w in range(2):
                            own.mark(dve.tensor_scalar(
                                tt[2 + um][:, w * L:w * L + L], bank[4 - (j - 1) % 2 * 2 + um][:, w * L:w * L + L],
                                vecs[:, V_HY_OUT_B + m:V_HY_OUT_B + m + 1], mods[0][:, 5 * DT + m, w:w + 1],
                                ALU.add, ALU.mult))
                        own.sync()
                        dve.tensor_tensor(hT[:, m, :], hT[:, m, :], tt[2 + um][:], ALU.add).then_inc(h_done, 1)
            open_lo(ffn_in["01"])
            ffn("01", 0, 6, FFN_ADA, ffn_in["10"],
                take=lambda: take_mods(ADA_FIRST[2], [(0, 8, 9), (1, 0, 4)], 2))

            ffn("10", 1, 0, FFN_ADA, XB, take=lambda: take_mods(2 * ADA_CHUNKS, [(1, 4, 9)], 3))
            norm("mb", 1, 3)

            def taps(pl, i, u, s, n):
                m = i * 4 + (u * 2 + s)
                first = pl.conv - 3
                src = bank[2 * u + s][:, 0:n].rearrange("p (a n) -> p a n", n=L)
                dst = tt[2 + s][:, 0:n].rearrange("p (a n) -> p a n", n=L)
                tap = lambda w: vecs[:, ds(m + (V_MB_CW + CONVT * w + first), 1)]
                dve.wait_ge(cv_in, m + (first + 1))
                own(dve.scalar_tensor_tensor(dst[:, :, 1:L], src[:, :, 0:L - 1], tap(0), dst[:, :, 1:L],
                                             ALU.mult, ALU.add))
                dve.scalar_tensor_tensor(dst[:, :, 0:L - 1], src[:, :, 1:L], tap(2), dst[:, :, 0:L - 1],
                                         ALU.mult, ALU.add).then_inc(conv_free, 1)

            def xb_pair(i, last):
                for u in range(2):
                    if last and u == 1:
                        open_lo(DTP, 8 * P)
                    else:
                        next_lo(XB, False, i, u, 2)
                    for s in range(2):
                        taps(XB, i, u, s, NT)
            steps(dve, 6, xb_pair, own, 4)

            open_lo(CP)
            hp = slice(64, 128)
            v, av, e, w = pp[0][hp, :], tt[0][hp, :], tt[1][hp, :], rs[hp, :]
            dve.wait_ge(s_par, 64)
            dve.wait_ge(w_used, DTP.w + 1)
            dve.wait_ge(p_lo, MBN.q)
            own(dve.tensor_scalar(v, bank[4][hp, :], par[hp, 0:1], None, ALU.add))
            dve.scalar_tensor_tensor(av, v, -1.0, v, ALU.mult, ALU.max).then_inc(dt_v, 1)
            own(dve.tensor_scalar(v, v, 0.0, None, ALU.max))
            dve.wait_ge(dt_e, 2)
            own(dve.tensor_scalar(w, e, 2.0, None, ALU.add))
            own(dve.reciprocal(w, w))

            def c_pair(i, last):
                for u in range(2):
                    if last and u == 1:
                        open_lo(ZP)
                    else:
                        next_lo(CP, False, i, u, 2)
                    for s in range(2):
                        taps(CP, i, u, s, L)
            steps(dve, 2, c_pair, own, 4)

            z, z2, s_ = tt[0][hp, :], tt[1][hp, :], rs[hp, :]
            own(dve.tensor_tensor(z, e, w, ALU.mult))
            own(dve.tensor_tensor(z2, z, z, ALU.mult))
            own(dve.tensor_scalar(s_, z2, 1.0 / 15, None, ALU.mult))
            for c in (13, 11, 9, 7, 5, 3):
                own(dve.scalar_tensor_tensor(s_, s_, 1.0 / c, z2, ALU.add, ALU.mult))
            own(dve.scalar_tensor_tensor(s_, s_, 1.0, z, ALU.add, ALU.mult))
            dt = pp[1][hp, :]
            own(dve.scalar_tensor_tensor(dt, s_, 2.0, v, ALU.mult, ALU.add))
            da = pp[0][hp, :]
            own(dve.tensor_scalar(da, dt, par[hp, 2:3], -1.0, ALU.mult, ALU.mult))
            own(dve.memset(tt[0][hp, 0:L], 1.0))
            cs = rs[hp, :]
            for seg in range(2):
                own.mark(dve.tensor_tensor_scan(cs[:, seg * L:seg * L + L], tt[0][hp, 0:L],
                                                da[:, seg * L:seg * L + L], 0.0, ALU.mult, ALU.add))
            own.sync()

            def z_pair(i, last):
                for u in range(2):
                    if not (last and u == 1):
                        next_lo(ZP, False, i, u, 2)
            steps(dve, 4, z_pair)

            dve.wait_ge(w_used, ZP.w + 8)
            f, b = slice(64, 96), slice(96, 128)
            lat, cx = slice(0, L), slice(L, NT)
            own.mark(dve.tensor_scalar(dts[f, 0, :], rs[f, lat], -1.0, None, ALU.mult))
            own.mark(dve.scalar_tensor_tensor(dts[b, 0, :], rs[b, lat], rs[b, L - 1:L], pp[0][b, lat],
                                              ALU.subtract, ALU.subtract))
            own.mark(dve.tensor_copy(dts[hp, 1, :], pp[1][hp, lat]))
            own.mark(dve.tensor_scalar(dts[f, 3, :], rs[f, cx], rs[f, NT - 1:NT], -1.0, ALU.subtract, ALU.mult))
            dve.tensor_tensor(dts[b, 3, :], rs[b, cx], pp[0][b, cx], ALU.subtract).then_inc(dt_v, 1)
            own.sync()
            dve.tensor_scalar(dts[hp, 5, :], dts[hp, 0, :], -1.0, None, ALU.mult).then_inc(dt_v, 1)
            dve.wait_ge(dt_e, 3)
            dve.tensor_tensor(dts[hp, 2, :], dts[hp, 4, :], pp[1][hp, cx], ALU.mult).then_inc(dt_v, 1)
            dve.wait_ge(tk_t, 1)
            dve.tensor_copy(tk[:].rearrange("p a n -> p (a n)"), bank[7][:, 0:384]).then_inc(tk_out, 1)
            dve.wait_ge(tk_out, 1)

            def token_major(x0, row):
                for b8 in range(8):
                    c, T = b8 // 2, b8 % 2
                    if x0:
                        dve.wait_ge(st_mm, 2 * c + 2)
                    dve.wait_ge(tr_mm, x0 + b8 + 1)
                    for d in range(2):
                        ins = dve.tensor_tensor(
                            xtok[:, d, T, c * 512:c * 512 + 512].rearrange("p (h w) -> p h w", w=HD),
                            bank[(x0 + b8) % 4][:].rearrange("p (h w) -> p h w", w=HD),
                            tk[:, row + T, 32 * d + 8 * c:32 * d + 8 * c + 8].unsqueeze(2).to_broadcast([P, 8, HD]),
                            ALU.mult)
                    ins.then_inc(tr_out, 1)
            token_major(0, 4)
            token_major(8, 2)
            dve.wait_ge(s_mask, 16)

            def b_dot_c(g, cb):
                dve.wait_ge(cb_mm, g + 1)
                if not isinstance(g, int) or g > 1:
                    dve.wait_ge(m_done, g * HPG - HPG)
                edges = bank[6][:].rearrange("p (a n) -> p a n", n=P)[:, 0:4:3, :]
                dve.tensor_tensor(cb[:, 0:512].rearrange("p (a n) -> p a n", n=P)[:, 0:4:3, :], edges,
                                  mask[:, 0:2, :], ALU.mult)
                dve.tensor_tensor(cb[:, 512:768].rearrange("p (a n) -> p a n", n=P), edges, mask[:, 1:3, :], ALU.mult)
                dve.tensor_copy(cb[:, P:3 * P], bank[6][:, P:3 * P]).then_inc(cb_out, 1)

            def group(i, u, first, finish, last):
                g = i * 2 + u
                if first:
                    b_dot_c(0, cbx[0])
                for r in range(HPG):
                    if finish and r == 1:
                        gate_y(g, 1 - u)
                    if r == 2 and not last:
                        b_dot_c(g + 1, cbx[1 - u])
                    bf = r % 2
                    h = i * 8 + (u * HPG + r)
                    dve.wait_ge(afb_in[r], i * 32 + (u * 16 + 16))
                    if not (first and r < 2):
                        dve.wait_ge(e_done, h - 1)
                    af, tks, d_ = afb[r], [[tk[:, T, ds(h + 32 * d, 1)] for T in range(2)] for d in range(2)], dm[bf]
                    own.mark(dve.tensor_scalar(d_[:, 0:P], af[:, 0, 0:P], tks[0][0], None, ALU.add))
                    own.mark(dve.tensor_scalar(d_[:, P:2 * P], af[:, 1, P:L], tks[1][1], None, ALU.add))
                    own.sync()
                    own.mark(dve.scalar_tensor_tensor(d_[:, 0:P], af[:, 1, 0:P], tks[1][0], d_[:, 0:P], ALU.add, ALU.min))
                    dve.scalar_tensor_tensor(d_[:, P:2 * P], af[:, 0, P:L], tks[0][1], d_[:, P:2 * P],
                                             ALU.add, ALU.min).then_inc(d_done, 1)
                    dve.wait_ge(ex_done, h + 1)
                    cs = csx[r][:].rearrange("p (d n) -> p d n", d=2)
                    dve.tensor_tensor(cs, cs, csb[:, g, :].unsqueeze(1).to_broadcast([P, 2, L]), ALU.mult).then_inc(cs_done, 1)

            def gate_y(g, odd):
                dve.wait_ge(head_mm, g * HPG)
                if not isinstance(g, int) or g > 1:
                    dve.wait_ge(y_done, g - 1)
                for mt in range(2):
                    m = g * 2 + (mt - 2)
                    own.mark(dve.scalar_tensor_tensor(tt[3][:, mt * L:mt * L + L], xb[:, 0, m, :], dcol[:, ds(m, 1)],
                                                      bank[4 + odd][:, mt * L:mt * L + L], ALU.mult, ALU.add))
                own.sync()
                zz = zsb[:, ds(g * 2 - 2, 2), :]
                dve.tensor_tensor(zz, zz, tt[3][:].rearrange("p (a n) -> p a n", a=2), ALU.mult).then_inc(y_done, 1)

            core_groups(dve, group, lambda: gate_y(GROUPS, 1), own, 2 * (3 * HPG + 2))

            open_lo(MBOUT)
            dve.wait_ge(g_rms, 1)
            dve.reciprocal(tt[0][0:GROUPS, 0:L], tt[0][0:GROUPS, 0:L]).then_inc(g_rec, 1)
            for g in range(GROUPS):
                q = MBN.q + g
                dve.wait_ge(g_bc, g + 1)
                pp_free(q)
                for mt in range(2):
                    m = 2 * g + mt
                    ins = dve.scalar_tensor_tensor(pp[q % 2][:, mt * L:mt * L + L], zsb[:, m, :],
                                                   vecs[:, V_MB_NORM + m:V_MB_NORM + m + 1],
                                                   bank[1 + g % 3][:, 0:L], ALU.mult, ALU.mult)
                ins.then_inc(p_ready, 1)

            def mb_pair(i, last):
                for um in range(2):
                    if last and um == 1:
                        open_lo(ffn_in["11"])
                    else:
                        next_lo(MBOUT, False, i, um, 2)
                    residual(MBOUT, 1, 5, i, um, L, i * 2 + (MBOUT.w + um + 1))
            steps(dve, DT // 2, mb_pair)
            ffn("11", 1, 6, 0, None, L)

            invert_rms(norms["fin"], L)
            for k in range(DT):
                if k >= 2:
                    dve.wait_ge(fin_t, k - 1)
                own(dve.tensor_tensor(pp[k % 2][:, 0:L], hT[:, k, 0:L], bank[7][:, 0:L], ALU.mult))
                dve.tensor_scalar(pp[k % 2][:, 0:L], pp[k % 2][:, 0:L], vecs[:, V_FINAL + k:V_FINAL + k + 1], None,
                                  ALU.mult).then_inc(fin_p, 1)

        @block.gpsimd
        def _(pool):
            def lo_tile(q, uses, dst, hi):
                pool.wait_ge(p_hi, uses)
                n = dst.shape[-1]
                pool.tensor_tensor(dst, pp[q % 2][:, 0:n], hi.bitcast(F32), ALU.subtract).then_inc(p_lo, 1)

            def norm_lo(key, n=NT):
                pl = norms[key]
                for k in range(DT):
                    lo_tile(pl.q + k, pl.q + k + 1, xl[:, k, 0:n], xh[:, k, 0:n])

            def clear(key):
                pool.wait_ge(nsum, norms[key].norm + 1)
                pool.memset(acc[:], 0.0).then_inc(acc_zero, 1)

            def add_square(pl, i, um, n):
                pool.wait_ge(sq_done, i * 2 + (pl.h + um + 1))
                pool.wait_ge(acc_done, i * 2 + (pl.h + um))
                pool.tensor_tensor(acc[:, 0:n], acc[:, 0:n], tt[um][:, 0:n], ALU.add).then_inc(acc_done, 1)

            def add_squares(pl, zeroed, n=NT):
                pool.wait_ge(acc_zero, zeroed)

                if pl.h == 0:
                    for i in range(DT // 2):
                        for um in range(2):
                            pool.wait_ge(sq_done, 2 * i + um + 1)
                            if i or um:
                                pool.wait_ge(acc_done, 2 * i + um)
                            pool.tensor_tensor(acc[:, 0:n], acc[:, 0:n], tt[um][:, 0:n], ALU.add).then_inc(acc_done, 1)
                else:
                    with pool.Fori(0, DT // 2) as i:
                        for um in range(2):
                            add_square(pl, i, um, n)

            def ffn(key, zeroed, n=NT):
                norm_lo(key, n)
                clear(key)
                pi = ffn_in[key]
                with pool.Fori(0, FT // 2) as i:
                    for u in range(2):
                        lo_tile(pi.q + u, i * 2 + (pi.q + u + 1), gl[:, i * 2 + u, 0:n], gh[:, i * 2 + u, 0:n])
                add_squares(ffn_out[key], zeroed, n)

            pool.memset(acc[:], 0.0).then_inc(acc_zero, 1)
            add_squares(P0, 1)
            for unit in range(4):
                for n in range(4):
                    q = unit * 4 + n
                    lo_tile(q, q + 1, fel[unit % 2][:, n % 2, n // 2, :], feh[unit % 2][:, n % 2, n // 2, :])
            ffn("00", 2)
            norm_lo("hy")
            clear("hy")
            for x in range(8):
                if x > 1:
                    pool.wait_ge(inv_mm, 2 * x - 2)
                for n in range(4):
                    pool.wait_ge(cm_mul, x * 4 + n + 1)
                    pool.tensor_tensor(prod[x % 2][:, n, :], tt[2 * (n % 2)][:], tt[2 * (n % 2) + 1][:],
                                       ALU.subtract if n < 2 else ALU.add).then_inc(y_sum, 1)
            for k in range(DT):
                pool.wait_ge(y_hi, k + 1)
                pool.tensor_tensor(xl[:, k, :], hyu[:, 8 + k, :], xh[:, k, :].bitcast(F32), ALU.subtract).then_inc(y_lo, 1)
            add_squares(HYOUT, 3)
            ffn("01", 4)
            ffn("10", 5)
            norm_lo("mb")
            clear("mb")
            pool.wait_ge(s_set, 1)

            def group(i, u, first, finish, last):
                pool.wait_ge(cb_out, i * 2 + (u + 1))
                for r in range(HPG):
                    h = i * 8 + (u * HPG + r)
                    pool.wait_ge(e_done, h + 1)
                    if not (first and r < 2):
                        pool.wait_ge(head_mm, h - 1)
                    pool.tensor_tensor(mm_[r % 2][:, 0:512], ee[r][:], cbx[u][:, 0:512], ALU.mult)
                    pool.tensor_tensor(mm_[r % 2][:, 512:768].rearrange("p (a n) -> p a n", n=P),
                                       ee[r][:].rearrange("p (a n) -> p a n", n=P)[:, 0:4:3, :],
                                       cbx[u][:, 512:768].rearrange("p (a n) -> p a n", n=P), ALU.mult).then_inc(m_done, 1)

            core_groups(pool, group, lambda: None)
            for g in range(GROUPS):
                lo_tile(MBN.q + g, MBN.q + g + 1, ynl[:, 2 * g:2 * g + 2, :].rearrange("p a n -> p (a n)"),
                        ynh[:, 2 * g:2 * g + 2, :].rearrange("p a n -> p (a n)"))
            add_squares(MBOUT, 6, L)
            ffn("11", 7, n=L)

        @block.tensor
        def _(pe):
            def mm3(dst, wslot, lo, x_hi, x_lo, start, stop):
                h, l_ = wh[wslot][:, lo:lo + P], wl[wslot][:, lo:lo + P]
                pe.matmul(dst, h, x_hi, start=start, stop=False)
                pe.matmul(dst, h, x_lo, start=False, stop=False)
                return pe.matmul(dst, l_, x_hi, start=False, stop=stop)

            def ada_chunk(v, col, av):
                pe.wait_ge(ada_dve, v + 1)
                for s in range(2):
                    for c in range(2):
                        ins = pe.matmul(bank[6][:, ds(col + (2 * s + c), 1)],
                                        av[:, c * L + s * P:c * L + s * P + P], ones[:, 0:1], start=True, stop=True)
                ins.then_inc(ada_used, 1)

            def ada_direct(r, col):
                pe.wait_ge(raw_in[r % 2], (r // 2 + 1) * 16)
                for s in range(2):
                    for k in range(DT):
                        ins = pe.matmul(bank[6][:, col + 2 * s:col + 2 * s + 2],
                                        raw[r % 2][:, k * 256 + s * P:k * 256 + s * P + P], sc[:, k, :],
                                        start=k == 0, stop=k == DT - 1)
                ins.then_inc(ada_used, 1)

            def norm(key, n=NT):
                pl = norms[key]
                pe.wait_ge(acc_done, pl.h)
                rows_ = n // P
                for j in range(rows_):
                    ins = pe.matmul(bank[7][0:GROUPS, 0:P], sel[:, j, :], acc[:, j * P:j * P + P],
                                    start=j == 0, stop=j == rows_ - 1)
                ins.then_inc(nsum, 1)
                pe.wait_ge(rms_inv, pl.norm + 1)
                for j in range(rows_):
                    ins = pe.matmul(bank[7][:, j * P:j * P + P], ident[0:rows_, j:j + 1].to_broadcast([rows_, P]),
                                    rs[0:rows_, 0:P], start=True, stop=True)
                ins.then_inc(rms_bc, 1)

            def two_tiles(wslot, banks, q, split=p_lo, n=NT):
                for k in range(DT):
                    pe.wait_ge(split, q + k + 1)
                    for s in range(2):
                        ins = mm3(bank[banks + s][:, 0:n], wslot, k * 256 + s * P, xh[:, k, 0:n], xl[:, k, 0:n],
                                  k == 0, k == DT - 1)
                ins.then_inc(w_used, 1)

            def ffn(key, ada=None, n=NT):
                norm(key, n)
                pi, po = ffn_in[key], ffn_out[key]
                x0 = norms[key].q
                if ada:
                    pe.wait_ge(ada_out, ada[1])

                def ada_sum(j, odd):
                    ada_chunk(j + pi.v, j * 4 + 4 * ada[0], tt[2 + odd])

                def pair(i, first, last):
                    for u in range(2):
                        pe.wait_ge(w_lo, i * 2 + (pi.w + u + 1))
                        if u == 0:
                            pe.wait_ge(gate_ready, i * 2 + pi.gate)
                        else:
                            pe.wait_ge(p_ready, i * 2 + pi.q)
                        two_tiles((pi.w + u) % 2, 2 * u, x0, n=n)
                        if ada and not (first and u == 0) and not (last and u):
                            ada_sum(i * 2 + (u - 1), 1 - u)
                steps_both(pe, FT // 2, pair)

                def mpair(i, last):
                    for um in range(2):
                        pe.wait_ge(h_done, i * 2 + (po.h + um - 1))
                        for half in range(2):
                            u = um * 2 + half
                            n_ = po.w + u
                            pe.wait_ge(w_lo, i * 4 + (n_ + 1))
                            if u == 0:
                                pe.wait_ge(p_lo, pi.q + FT - 2)
                            for kk in range(11):
                                k = half * 11 + kk
                                if k == FT - 2 and um == 0:
                                    pe.wait_ge(p_lo, pi.q + FT)
                                ins = mm3(bank[4 + um][:, 0:n], n_ % 2, kk * P, gh[:, k, 0:n], gl[:, k, 0:n],
                                          k == 0, k == FT - 1)
                            ins.then_inc(w_used, 1)
                steps(pe, DT // 2, mpair)

            pe.wait_ge(s_cst, 16)
            pe.wait_ge(s_vec, 16 * VEC_DMAS)
            stage = tt[0][:, :].rearrange("p (a c) -> p a c", c=P)
            for a in range(4):
                n = min(P, V_ALL - a * P)
                ins = pe.transpose(bank[7][:, a * P:a * P + n], stage[0:n, a, :], small[0:n, 0:n])
            ins.then_inc(vec_t, 1)
            pe.wait_ge(s_x, 32)
            for k in range(DT):
                if k >= 4:
                    pe.wait_ge(h_done, k - 3)
                for a in range(4):
                    ins = pe.transpose(bank[k % 4][:, a * P:a * P + P], xstage[:, a, k * P:k * P + P], ident)
                ins.then_inc(x_t, 1)
            pe.wait_ge(s_fil, 16 * 8)
            pe.wait_ge(vec_out, 1)
            for layer in range(2):
                rows_, rhs = (33, hsm[0:33, 0, :]) if layer == 0 else (64, hsm[:, 3, :])
                if layer:
                    pe.wait_ge(hid_sin, 1)
                pe.matmul(bank[7][0:64, 0:L], hsm[0:rows_, 1, 64 * layer:64 * layer + 64], rhs,
                          start=True, stop=True).then_inc(hid_mm, 1)
            pe.wait_ge(h_done, DT)
            pe.wait_ge(s_set, 1)

            def early_ada(a):
                ada_chunk(a // 2, 4 * a, early_av[a // 2 % 2])
                ada_direct(a + 3, 4 * a + 4)

            pe.wait_ge(sc_done, 1)
            early_ada(0)
            pe.wait_ge(hid_sin, 2)

            def filters(unit):
                o_, hh = unit // 2, unit % 2
                if unit:
                    pe.wait_ge(p_ready, unit * 4)
                for n in range(2):
                    for d in range(2):
                        c = (o_ * 2 + d) * D + hh * 512
                        ins = pe.matmul(bank[2 * d + n][:], hsm[:, 4, n * P:n * P + P], w3[:, c:c + 512],
                                        start=True, stop=True)
                    ins.then_inc(fil_mm, 1)
            filters(0)
            early_ada(2)
            pe.wait_ge(w_lo, 2)
            for unit in range(4):
                if unit < 3:
                    filters(unit + 1)
                for kt in range(5):
                    x = unit * 5 + kt
                    if x >= 2:
                        pe.wait_ge(spec_out, x - 1)
                    eo = 1 if kt in (2, 3) else 0
                    for k in range(2):
                        pe.wait_ge(p_lo, unit * 4 + 2 * k + eo + 1)
                        slot, lo = (0, k * 512 + kt * P) if kt < 4 else (1, k * P)
                        ins = mm3(bank[4 + x % 2][:], slot, lo, feh[unit % 2][:, eo, k, :], fel[unit % 2][:, eo, k, :], k == 0, k == 1)
                    ins.then_inc(spec_mm, 1)
                early_ada(4 + 2 * unit)
            pe.wait_ge(s_set, 2)
            pe.wait_ge(p_ready, 16)
            pe.wait_ge(spec_out, 20)
            pe.matmul(bank[5][:, 0:1], ones[:], ones[:, 0:1], start=True, stop=True).then_inc(w_used, 2)

            ffn("00", (ADA_FIRST[0], 1))
            norm("hy")
            def hy_pair(i, last):
                for u in range(2):
                    pe.wait_ge(w_lo, i * 2 + (HYIN.w + u + 1))
                    pe.wait_ge(z_free, i * 4 + (HYIN.zf + 2 * u - 2))
                    two_tiles((HYIN.w + u) % 2, 2 * u, norms["hy"].q)
            steps(pe, 6, hy_pair)
            pe.wait_ge(w_lo, HYDFT.w + 1)
            pe.wait_ge(z_free, HYIN.zf + 24)
            pe.wait_ge(hy_ready, 2 + 24)
            for conv in range(2):
                if conv:
                    pe.wait_ge(inv_out, 16)
                def turn(j0):
                    for j in range(j0, j0 + 4):
                        turn_block(conv * 8 + j, TURN[j], j)

                def turn_block(x, b, j):
                    if j >= 2:
                        pe.wait_ge(vt_lo, x - 1)
                    for c in range(4):
                        ins = pe.transpose(bank[4 + j % 2][:, c * P:c * P + P],
                                           hyu[:, (0 if conv else 16) + (b % 2) * 4 + c, (b // 2) * P:(b // 2) * P + P], ident)
                    ins.then_inc(vt_t, 1)
                turn(0)
                for unit in range(5):
                    if unit == 1:
                        turn(4)
                    if unit < 4:
                        x = conv * 4 + unit
                        seg, half = unit // 2, unit % 2
                        if x:
                            pe.wait_ge(cm_mul, 4 * x)
                        for ft in range(4):
                            for k in range(2):
                                b = (2 * seg + k) * 2 + half
                                pe.wait_ge(vt_lo, conv * 8 + 2 * unit + k + 1)
                                ins = mm3(bank[ft][:], 0, k * 512 + ft * P, xh[:, b, :], xl[:, b, :], k == 0, k == 1)
                        ins.then_inc(fwd_mm, 1)
                    if unit:
                        y = conv * 4 + unit - 1
                        pe.wait_ge(y_sum, 4 * y + 4)
                        for c in range(4):
                            if c % 2 == 0:
                                if unit > 1:
                                    pe.wait_ge(inv_out, 4 * (y - 1) + c + 2)
                                else:
                                    pe.wait_ge(vt_lo, conv * 8 + 8)
                            dst = bank[4 + c // 2][:, (c % 2) * L:(c % 2) * L + L]
                            for ft in range(4):
                                ins = pe.matmul(dst, prod[y % 2][:, ft, c * P:c * P + P],
                                                raw[HYDFT.raw % 2][:, 1024 + ft * L:1024 + ft * L + L],
                                                start=ft == 0, stop=ft == 3)
                            if c % 2:
                                ins.then_inc(inv_mm, 1)
            pe.wait_ge(cm_mul, 32)
            pe.matmul(bank[0][:, 0:1], ones[:], ones[:, 0:1], start=True, stop=True).then_inc(w_used, 1)
            for j in range(4):
                pe.wait_ge(w_lo, HYOUT.w + j + 1)
                if j == 0:
                    pe.wait_ge(inv_out, 32)
                elif j > 1:
                    pe.wait_ge(h_done, HYOUT.h + 2 * j - 2)
                two_tiles((HYOUT.w + j) % 2, 4 - j % 2 * 2, 0, y_lo)
            ffn("01", (ADA_FIRST[1], 2))

            ffn("10", (ADA_FIRST[2], 3))
            norm("mb")
            x0 = norms["mb"].q

            def wide(pl, chunks, free, base, n):
                def pair(i, last):
                    for u in range(2):
                        pe.wait_ge(w_lo, i * 2 + (pl.w + u + 1))
                        pe.wait_ge(free, i * 4 + (base + 2 * u - 2))
                        two_tiles((pl.w + u) % 2, 2 * u, x0, n=n)
                steps(pe, chunks // 2, pair)
            wide(XB, 12, conv_free, XB.conv, NT)
            pe.wait_ge(w_lo, DTP.w + 1)
            for k in range(DT):
                ins = mm3(bank[4][:], DTP.w % 2, k * P, xh[:, k, :], xl[:, k, :], k == 0, k == DT - 1)
            ins.then_inc(w_used, 1)
            wide(CP, 4, conv_free, CP.conv, L)
            pe.wait_ge(conv_free, CP.conv + 8)
            wide(ZP, 8, z_free, ZP.zf, L)

            pe.wait_ge(z_free, ZP.zf + 16)
            pe.wait_ge(cv_silu, 2 + 32)
            for b in range(4):
                if b >= 2:
                    pe.wait_ge(tb_out, b - 1)
                for c in range(4):
                    m = IT + (b % 2) * 4 + c
                    ins = pe.transpose(bank[6 + b % 2][:, c * P:c * P + P], xb[:, 1, m, (b // 2) * P:(b // 2) * P + P], ident)
                ins.then_inc(tb_mm, 1)

            def turn_x(x0_, seg, c4):
                for T in range(2):
                    x = x0_ + 2 * c4 + T
                    if x >= 4:
                        pe.wait_ge(tr_out, x - 3)
                    for c in range(4):
                        ins = pe.transpose(bank[x % 4][:, c * P:c * P + P],
                                           xb[:, seg, c4 * 4 + c, T * P:T * P + P], ident)
                    ins.then_inc(tr_mm, 1)

            def states(c4):
                pe.wait_ge(tr_out, 2 * c4 + 2)
                for g in (2 * c4, 2 * c4 + 1):
                    if g >= 2:
                        pe.wait_ge(st_out, g - 1)
                    for d in range(2):
                        for T in range(2):
                            ins = pe.matmul(bank[4 + g % 2][:, d * L:d * L + L], btok[:, T, g * P:g * P + P],
                                            xtok[:, d, T, g * L:g * L + L], start=T == 0, stop=T == 1)
                    ins.then_inc(st_mm, 1)
            pe.wait_ge(dt_v, 4)
            pe.wait_ge(tb_out, 4)
            for j in range(6):
                ins = pe.transpose(bank[7][:, 64 * j:64 * j + 64], dts[64:128, j // 2, (j % 2) * P:(j % 2) * P + P],
                                   small[64:128, 64:128])
            ins.then_inc(tk_t, 1)
            turn_x(0, 1, 0)
            for c4 in range(4):
                if c4 < 3:
                    turn_x(0, 1, c4 + 1)
                states(c4)
            for c4 in range(4):
                turn_x(8, 0, c4)
            pe.wait_ge(tr_out, 16)
            pe.wait_ge(st_out, GROUPS)
            pe.wait_ge(tk_out, 1)

            def b_dot_c(g):
                if g:
                    pe.wait_ge(cb_out, g)
                for T in range(2):
                    ins = pe.matmul(bank[6][:, T * L:T * L + L], xb[:, 0, IT + g, T * P:T * P + P], csb[:, g, :],
                                    start=True, stop=True)
                ins.then_inc(cb_mm, 1)

            def sum_squares(g):
                pe.wait_ge(g_sq, g + 1)
                for mt in range(2):
                    ins = pe.matmul(bank[0][0:GROUPS, 0:L], sel[:, g, :], tt[2][:, mt * L:mt * L + L],
                                    start=g == 0 and mt == 0, stop=g == GROUPS - 1 and mt == 1)
                ins.then_inc(g_sum, 1)

            b_dot_c(0)
            for g in range(GROUPS):
                if g >= 2:
                    pe.wait_ge(y_done, g - 1)
                for r in range(HPG):
                    if r == 1 and g + 1 < GROUPS:
                        b_dot_c(g + 1)
                    if r == 1 and g >= 2:
                        sum_squares(g - 2)
                    h = g * HPG + r
                    b = r % 2
                    hc = slice(h * HD, h * HD + HD)
                    dst = bank[4 + g % 2][b * HD:b * HD + HD, r // 2 * L:r // 2 * L + L]
                    pe.wait_ge(cs_done, h + 1)
                    for d in range(2):
                        pe.matmul(dst, ssb[:, d, hc], csx[r][:, d * L:d * L + L], start=d == 0, stop=False)
                    pe.wait_ge(m_done, h + 1)
                    m = mm_[b]
                    pe.matmul(dst, xtok[:, 0, 0, hc], m[:, 0:256], start=False, stop=False)
                    pe.matmul(dst[:, 0:P], xtok[:, 1, 0, hc], m[:, 512:640], start=False, stop=False)
                    pe.matmul(dst[:, P:L], xtok[:, 0, 1, hc], m[:, 640:768], start=False, stop=False)
                    pe.matmul(dst, xtok[:, 1, 1, hc], m[:, 256:512], start=False, stop=True).then_inc(head_mm, 1)
            sum_squares(GROUPS - 2)
            sum_squares(GROUPS - 1)
            pe.wait_ge(g_rec, 1)
            for g in range(GROUPS):
                if g >= 3:
                    pe.wait_ge(p_ready, MBN.q + g - 2)
                pe.matmul(bank[1 + g % 3][:, 0:L], ident[0:GROUPS, g:g + 1].to_broadcast([GROUPS, P]),
                          tt[0][0:GROUPS, 0:L], start=True, stop=True).then_inc(g_bc, 1)

            def mb_pair(i, last):
                for um in range(2):
                    n_ = MBOUT.w + um
                    pe.wait_ge(w_lo, i * 2 + (n_ + 1))
                    pe.wait_ge(h_done, i * 2 + (MBOUT.h + um - 1))
                    for k in range(IT):
                        if k % 2 == 0 and um == 0:
                            pe.wait_ge(p_lo, MBN.q + k // 2 + 1)
                        ins = mm3(bank[4 + um][:, 0:L], n_ % 2, k * P, ynh[:, k, :], ynl[:, k, :], k == 0, k == IT - 1)
                    ins.then_inc(w_used, 1)
            steps(pe, DT // 2, mb_pair)
            ffn("11", n=L)
            norm("fin", L)
            for k in range(DT):
                pe.wait_ge(fin_p, k + 1)
                if k >= 4:
                    pe.wait_ge(fin_o, k - 3)
                for T in range(2):
                    ins = pe.transpose(bank[k % 4][:, T * P:T * P + P], pp[k % 2][:, T * P:T * P + P], ident)
                ins.then_inc(fin_t, 1)


_INS = ['x', 'c', 'ctx', 'c_ctx', 'ada_w', 'ada_b', 'ffn_in', 'ffn_out', 'hy_in_w', 'hy_in_b', 'hy_conv_w',
        'hy_conv_b', 'hy_pos_w1', 'hy_pos_b1', 'hy_freq', 'hy_pos_w2', 'hy_pos_b2', 'hy_pos_w3', 'hy_bias',
        'hy_out_w', 'hy_out_b', 'mb_in_w', 'mb_conv_w', 'mb_conv_b', 'mb_dt_bias', 'mb_A_log', 'mb_D',
        'mb_norm_w', 'mb_out_w', 'final_norm_w']


def _constants():
    import math
    import numpy as np

    n = 2 * L
    f32 = np.float32
    tok = np.arange(L)
    ang = 2 * math.pi * ((tok[:, None] * np.arange(L)[None, :]) % n) / n
    alt = np.where(tok % 2, -1.0, 1.0)
    cos, sin = np.cos(ang), -np.sin(ang)
    im = sin.copy()
    im[:, 0] = alt
    cos2 = cos.copy()
    cos2[:, 0] = alt
    fwd = np.concatenate([cos, im], 1)
    inv_re = 2 * cos.T / n
    inv_re[0] /= 2
    inv_im = 2 * sin.T / n
    inv_im[0] = alt / n
    inv = np.concatenate([inv_re, inv_im], 0)
    dft1 = np.concatenate([fwd.reshape(2, P, 512).transpose(1, 0, 2).reshape(P, 1024),
                           inv.reshape(4, P, L).transpose(1, 0, 2).reshape(P, 1024)], 1)
    dft2 = cos2[:, 0:P].reshape(2, P, P).transpose(1, 0, 2).reshape(P, 256)
    tl = np.linspace(0.0, 1.0, L, dtype=f32)
    bands = np.linspace(1e-4, 15, 16, dtype=f32)
    a = (f32(2.0 * math.pi / L) * tok.astype(f32)[:, None] * bands[None, :]).astype(f32)
    z = np.concatenate([tl[:, None], np.cos(a), -np.sin(a)], 1)
    deltas = np.abs(np.linspace(math.log(1e-2) / 1.5, math.log(1e-2) / 0.3, D, dtype=f32))
    dec = np.exp(-tl[:, None] * deltas[None, :]).reshape(2, P, D).transpose(1, 0, 2).reshape(P, 2 * D)
    small = np.concatenate([np.eye(P), np.ones((P, 1))], 1)
    small[0, P] = 0
    s, tt_ = np.arange(P)[:, None], np.arange(P)[None, :]
    f = np.where(tt_ >= s, 1.0, 0.0)
    b = np.where(tt_ <= s, 1.0, 0.0)
    mask = np.concatenate([f, b, f], 1)
    return {k: np.ascontiguousarray(v, dtype=f32) for k, v in
            dict(c_dft1=dft1, c_dft2=dft2, c_z=z.T, c_decay=dec, c_small=small, c_mask=mask).items()}


def kernel(**inputs):
    import numpy as _np
    import concourse.bacc as _bacc
    from concourse.bass_utils import run_bass_kernel_spmd as _run

    nc = _bacc.Bacc("TRN2", target_bir_lowering=False, num_devices=1)
    arrays, args = {}, {}
    given = {name: _np.ascontiguousarray(inputs[name]) for name in _INS}
    given.update(_constants())
    for name, a in given.items():
        arrays[f"in_{name}"] = a
        args[name] = nc.dram_tensor(f"in_{name}", a.shape, mybir.dt.from_np(a.dtype), kind="ExternalInput").ap()
    out = nc.dram_tensor("out_0", (1, L, D), F32, kind="ExternalOutput").ap()
    kscr = nc.dram_tensor("filter_spectra", (P, 4, 5, 512), F32, kind="Internal").ap()
    afscr = nc.dram_tensor("decays", (HEADS, 2, L), F32, kind="Internal").ap()
    build(nc, args, out, kscr, afscr)
    r = _run(nc, [arrays], core_ids=[0])
    return r.results[0]["out_0"]
```
